# Optimizing a Trainium2 kernel written in Bass

```python
import math
import jax, jax.numpy as jnp
from jax import lax
import numpy as np

D_MODEL = 1024
BATCH = 1
SEQ = 512
DEPTH = 1
DEC_BATCH = 1
DEC_SEQ = 64
PAST_LEN = 128

CHUNK = 64
D_MIX = D_MODEL
D_A = D_MIX // 2
DK_A = 128
DV_A = 128
H_A = D_A // DV_A
A_CONV = 4
D_B = D_MIX // 4
B_BLOCKS = 4
B_BW = D_B // B_BLOCKS
B_CONV = 4
RG_C = 8.0
D_C = D_MIX - D_A - D_B
H_C = 4
DK_C = D_C // H_C
DV_C = D_C // H_C
N_MEM = 256
MEM_HEADS = 4
MEM_HEAD_DIM = D_MODEL // MEM_HEADS
D_FF = 2816
FFN_CONV = 3
RMS_EPS = 1e-6
IN_SIZES = (3 * D_A, D_A, H_A, H_A, D_B, D_B, H_C * DK_C, H_C * DK_C, D_C, D_C)
N_IN = sum(IN_SIZES)

kernel_name = "hybrid_gdn_rglru_hgrn2_stream_step"

def rmsnorm(x, w):
    xf = x.astype(jnp.float32)
    y = xf * lax.rsqrt(jnp.mean(xf * xf, axis=-1, keepdims=True) + RMS_EPS)
    return (y * w.astype(jnp.float32)).astype(x.dtype)

def l2norm(x):
    xf = x.astype(jnp.float32)
    return xf * lax.rsqrt(jnp.sum(xf * xf, axis=-1, keepdims=True) + 1e-6)

def causal_dwconv(x, prev, w):
    width, length = w.shape[0], x.shape[1]
    xp = jnp.concatenate([prev.astype(x.dtype), x], axis=1)
    y = xp[:, 0:length] * w[0]
    for j in range(1, width):
        y = y + xp[:, j:j + length] * w[j]
    return y, xp[:, length:]

def to_chunks(t, c):
    b, l = t.shape[:2]
    t = t.reshape((b, l // c, c) + t.shape[2:])
    return jnp.moveaxis(jnp.moveaxis(t, 1, 0), 2, 3)

def from_chunks(t):
    t = jnp.moveaxis(jnp.moveaxis(t, 3, 2), 0, 1)
    return t.reshape((t.shape[0], t.shape[1] * t.shape[2]) + t.shape[3:])

def gated_delta_rule(q, k, v, g, beta, s0):
    c = math.gcd(q.shape[1], CHUNK)
    q, k, v = to_chunks(q, c), to_chunks(k, c), to_chunks(v, c)
    g, beta = to_chunks(g, c), to_chunks(beta, c)
    incl = jnp.tril(jnp.ones((c, c), dtype=bool))
    strict = jnp.tril(jnp.ones((c, c), dtype=bool), -1)
    gcum = jnp.cumsum(g, axis=-1)
    gamma = jnp.exp(jnp.where(incl, gcum[..., :, None] - gcum[..., None, :], -jnp.inf))
    kk = jnp.einsum('nbhid,nbhjd->nbhij', k, k)
    m = jnp.eye(c, dtype=q.dtype) + jnp.where(strict, beta[..., :, None] * kk * gamma, 0.0)
    rhs = jnp.concatenate([v * beta[..., None], k * (beta * jnp.exp(gcum))[..., None]], axis=-1)
    sol = lax.linalg.triangular_solve(m, rhs, left_side=True, lower=True, unit_diagonal=True)
    dv = v.shape[-1]
    u, w = sol[..., :dv], sol[..., dv:]
    qk = jnp.einsum('nbhid,nbhjd->nbhij', q, k) * gamma
    q_dec = q * jnp.exp(gcum)[..., None]
    k_dec = k * jnp.exp(gcum[..., -1:] - gcum)[..., None]
    g_last = jnp.exp(gcum[..., -1])

    def step(s, inp):
        u_c, w_c, qk_c, qd_c, kd_c, gl_c = inp
        v_new = u_c - jnp.einsum('bhcd,bhdv->bhcv', w_c, s)
        o = jnp.einsum('bhcd,bhdv->bhcv', qd_c, s) + jnp.einsum('bhij,bhjv->bhiv', qk_c, v_new)
        s = gl_c[..., None, None] * s + jnp.einsum('bhcd,bhcv->bhdv', kd_c, v_new)
        return s, o

    s_last, o = lax.scan(step, s0, (u, w, qk, q_dec, k_dec, g_last))
    return from_chunks(o), s_last

def hgrn2_recurrence(q, k, v, log_f, s0):
    c = math.gcd(q.shape[1], CHUNK)
    q, k, v, log_f = [to_chunks(t, c) for t in (q, k, v, log_f)]
    incl = jnp.tril(jnp.ones((c, c), dtype=bool))

    def step(s, inp):
        q_c, k_c, v_c, lf_c = inp
        bc = jnp.cumsum(lf_c, axis=2)
        decay = jnp.exp(jnp.where(incl[..., None], bc[:, :, :, None, :] - bc[:, :, None, :, :], -jnp.inf))
        att = jnp.einsum('bhid,bhjd,bhijd->bhij', q_c, k_c, decay)
        o = jnp.einsum('bhij,bhjv->bhiv', att, v_c) + jnp.einsum('bhid,bhdv->bhiv', q_c * jnp.exp(bc), s)
        b_last = bc[:, :, -1:, :]
        s = jnp.exp(b_last[:, :, 0, :])[..., None] * s + jnp.einsum('bhjd,bhjv->bhdv', k_c * jnp.exp(b_last - bc), v_c)
        return s, o

    s_last, o = lax.scan(step, s0, (q, k, v, log_f))
    return from_chunks(o), s_last

def rg_lru_scan(a, u, h0):
    u = u.at[:, 0].add(a[:, 0] * h0)

    def combine(left, right):
        return left[0] * right[0], right[0] * left[1] + right[1]

    _, h = lax.associative_scan(combine, (a, u), axis=1)
    return h, h[:, -1]

def mixing_block(h, a_conv_prev, a_s, b_conv_prev, b_h, c_s,
                 w_in, a_conv_w, a_A_log, a_dt_bias, a_norm,
                 b_conv_w, b_conv_b, b_w_r, b_b_r, b_w_i, b_b_i, b_lambda,
                 c_lb, c_norm, w_out):
    bsz, length, _ = h.shape
    f32 = jnp.float32
    dt = h.dtype
    proj = h @ w_in
    splits = np.cumsum(IN_SIZES)[:-1].tolist()
    a_qkv, a_z, a_b, a_a, b_x, b_gate, c_q, c_f, c_i, c_g = jnp.split(proj, splits, axis=-1)

    qkv, a_conv_new = causal_dwconv(a_qkv, a_conv_prev, a_conv_w)
    qkv = jax.nn.silu(qkv)
    q, k, v = [t.reshape(bsz, length, H_A, -1) for t in jnp.split(qkv, 3, axis=-1)]
    q = l2norm(q) * (DK_A ** -0.5)
    k = l2norm(k)
    beta = jax.nn.sigmoid(a_b.astype(f32))
    g = -jnp.exp(a_A_log.astype(f32)) * jax.nn.softplus(a_a.astype(f32) + a_dt_bias.astype(f32))
    o_a, a_s_new = gated_delta_rule(q, k, v.astype(f32), g, beta, a_s.astype(f32))
    o_a = rmsnorm(o_a, a_norm) * jax.nn.silu(a_z.astype(f32).reshape(bsz, length, H_A, DV_A))
    o_a = o_a.reshape(bsz, length, D_A).astype(dt)

    xb, b_conv_new = causal_dwconv(b_x, b_conv_prev, b_conv_w)
    xb = (xb + b_conv_b).astype(f32)
    xblk = xb.reshape(bsz, length, B_BLOCKS, B_BW)
    r = jax.nn.sigmoid(jnp.einsum('blni,nij->blnj', xblk, b_w_r.astype(f32)).reshape(bsz, length, D_B) + b_b_r)
    i_gate = jax.nn.sigmoid(jnp.einsum('blni,nij->blnj', xblk, b_w_i.astype(f32)).reshape(bsz, length, D_B) + b_b_i)
    log_a = -RG_C * r * jax.nn.softplus(-b_lambda.astype(f32))
    mult = jnp.sqrt(jnp.maximum(-jnp.expm1(2.0 * log_a), 0.0))
    hb, b_h_new = rg_lru_scan(jnp.exp(log_a), mult * i_gate * xb, b_h.astype(f32))
    y_b = (hb * jax.nn.gelu(b_gate.astype(f32))).astype(dt)

    q_c = jax.nn.silu(c_q.astype(f32)).reshape(bsz, length, H_C, DK_C)
    lb = c_lb.reshape(H_C, DK_C)
    forget = lb + (1.0 - lb) * jax.nn.sigmoid(c_f.astype(f32).reshape(bsz, length, H_C, DK_C))
    v_c = c_i.astype(f32).reshape(bsz, length, H_C, DV_C)
    o_c, c_s_new = hgrn2_recurrence(q_c, 1.0 - forget, v_c, jnp.log(forget), c_s.astype(f32))
    o_c = rmsnorm(o_c, c_norm) * jax.nn.silu(c_g.astype(f32).reshape(bsz, length, H_C, DV_C))
    o_c = o_c.reshape(bsz, length, D_C).astype(dt)

    out = jnp.concatenate([o_a, y_b, o_c], axis=-1) @ w_out
    return out, (a_conv_new, a_s_new.astype(dt), b_conv_new, b_h_new.astype(dt), c_s_new.astype(dt))

def memory_kv(mem, norm_mem, w_k, w_v):
    bsz = mem.shape[0]
    mn = rmsnorm(mem, norm_mem)
    k = (mn @ w_k).reshape(bsz, -1, MEM_HEADS, MEM_HEAD_DIM)
    v = (mn @ w_v).reshape(bsz, -1, MEM_HEADS, MEM_HEAD_DIM)
    return k, v

def memory_cross_attention(h, mem_k, mem_v, w_q, w_o):
    bsz, length, _ = h.shape
    q = (h @ w_q).reshape(bsz, length, MEM_HEADS, MEM_HEAD_DIM)
    s = jnp.einsum('blhd,bmhd->bhlm', q, mem_k).astype(jnp.float32) * (MEM_HEAD_DIM ** -0.5)
    p = jax.nn.softmax(s, axis=-1).astype(h.dtype)
    o = jnp.einsum('bhlm,bmhd->blhd', p, mem_v).reshape(bsz, length, D_MODEL)
    return o @ w_o

def conv_ffn(h, conv_prev, w_up, conv_w, conv_b, w_down):
    u, conv_new = causal_dwconv(h @ w_up, conv_prev, conv_w)
    gate, val = jnp.split(u + conv_b, 2, axis=-1)
    return (jax.nn.silu(gate) * val) @ w_down, conv_new

def setup_inputs(seed: int = 0) -> dict:
    key = jax.random.key(seed)
    ks = jax.random.split(key, 48)
    idx = iter(range(48))

    def nrm(shape, scale=1.0):
        return scale * jax.random.normal(ks[next(idx)], shape, jnp.float32)

    def gain(shape):
        return 1.0 + nrm(shape, 0.02)

    def unif(shape, lo, hi):
        return jax.random.uniform(ks[next(idx)], shape, jnp.float32, lo, hi)

    a_A_log = jnp.log(unif((DEPTH, H_A), 1.0, 16.0))
    dt = jnp.exp(unif((DEPTH, H_A), math.log(1e-3), math.log(1e-1)))
    a_dt_bias = dt + jnp.log(-jnp.expm1(-dt))
    lru_s = unif((DEPTH, D_B), 0.9, 0.999) ** (1.0 / RG_C)
    b_lambda = jnp.log(lru_s) - jnp.log1p(-lru_s)
    return {
        'x_prompt': nrm((BATCH, SEQ, D_MODEL)),
        'x_sample': nrm((DEC_BATCH, DEC_SEQ, D_MODEL)),
        'cache_mem_k': nrm((DEPTH, DEC_BATCH, N_MEM, MEM_HEADS, MEM_HEAD_DIM)),
        'cache_mem_v': nrm((DEPTH, DEC_BATCH, N_MEM, MEM_HEADS, MEM_HEAD_DIM)),
        'state_a_conv': nrm((DEPTH, DEC_BATCH, A_CONV - 1, 3 * D_A)),
        'state_a_S': nrm((DEPTH, DEC_BATCH, H_A, DK_A, DV_A), 0.1),
        'state_b_conv': nrm((DEPTH, DEC_BATCH, B_CONV - 1, D_B)),
        'state_b_h': nrm((DEPTH, DEC_BATCH, D_B), 0.5),
        'state_c_S': nrm((DEPTH, DEC_BATCH, H_C, DK_C, DV_C), 0.5),
        'state_ffn_conv': nrm((DEPTH, DEC_BATCH, FFN_CONV - 1, 2 * D_FF)),
        'mem_prompt': nrm((BATCH, N_MEM, D_MODEL)),
        'norm_mix': gain((DEPTH, D_MODEL)),
        'w_in': nrm((DEPTH, D_MODEL, N_IN), D_MODEL ** -0.5),
        'a_conv_w': nrm((DEPTH, A_CONV, 3 * D_A), A_CONV ** -0.5),
        'a_A_log': a_A_log,
        'a_dt_bias': a_dt_bias,
        'a_norm': gain((DEPTH, DV_A)),
        'b_conv_w': nrm((DEPTH, B_CONV, D_B), B_CONV ** -0.5),
        'b_conv_b': nrm((DEPTH, D_B), 0.02),
        'b_w_r': nrm((DEPTH, B_BLOCKS, B_BW, B_BW), B_BW ** -0.5),
        'b_b_r': nrm((DEPTH, D_B), 0.02),
        'b_w_i': nrm((DEPTH, B_BLOCKS, B_BW, B_BW), B_BW ** -0.5),
        'b_b_i': nrm((DEPTH, D_B), 0.02),
        'b_lambda': b_lambda,
        'c_lb_logits': nrm((DEPTH, D_C), 0.1),
        'c_norm': gain((DEPTH, DV_C)),
        'w_out': nrm((DEPTH, D_MIX, D_MODEL), D_MIX ** -0.5),
        'norm_attn': gain((DEPTH, D_MODEL)),
        'norm_mem': gain((DEPTH, D_MODEL)),
        'w_q': nrm((DEPTH, D_MODEL, D_MODEL), D_MODEL ** -0.5),
        'w_k': nrm((DEPTH, D_MODEL, D_MODEL), D_MODEL ** -0.5),
        'w_v': nrm((DEPTH, D_MODEL, D_MODEL), D_MODEL ** -0.5),
        'w_o': nrm((DEPTH, D_MODEL, D_MODEL), D_MODEL ** -0.5),
        'norm_ffn': gain((DEPTH, D_MODEL)),
        'w_up': nrm((DEPTH, D_MODEL, 2 * D_FF), D_MODEL ** -0.5),
        'ffn_conv_w': nrm((DEPTH, FFN_CONV, 2 * D_FF), FFN_CONV ** -0.5),
        'ffn_conv_b': nrm((DEPTH, 2 * D_FF), 0.02),
        'w_down': nrm((DEPTH, D_FF, D_MODEL), D_FF ** -0.5),
        'norm_final': gain((D_MODEL,)),
    }

def reference(x_prompt, x_sample, cache_mem_k, cache_mem_v, state_a_conv, state_a_S, state_b_conv,
              state_b_h, state_c_S, state_ffn_conv, mem_prompt, norm_mix, w_in, a_conv_w, a_A_log,
              a_dt_bias, a_norm, b_conv_w, b_conv_b, b_w_r, b_b_r, b_w_i, b_b_i, b_lambda,
              c_lb_logits, c_norm, w_out, norm_attn, norm_mem, w_q, w_k, w_v, w_o, norm_ffn,
              w_up, ffn_conv_w, ffn_conv_b, w_down, norm_final):
    sm = jax.nn.softmax(c_lb_logits.astype(jnp.float32), axis=0)
    lower_bounds = jnp.cumsum(sm, axis=0) - sm[0]

    def layer(l, x, mem_k, mem_v, a_conv, a_s, b_conv, b_h, c_s, f_conv):
        mix, mix_state = mixing_block(
            rmsnorm(x, norm_mix[l]), a_conv, a_s, b_conv, b_h, c_s,
            w_in[l], a_conv_w[l], a_A_log[l], a_dt_bias[l], a_norm[l],
            b_conv_w[l], b_conv_b[l], b_w_r[l], b_b_r[l], b_w_i[l], b_b_i[l], b_lambda[l],
            lower_bounds[l], c_norm[l], w_out[l])
        x = x + mix
        x = x + memory_cross_attention(rmsnorm(x, norm_attn[l]), mem_k, mem_v, w_q[l], w_o[l])
        f, f_conv_new = conv_ffn(rmsnorm(x, norm_ffn[l]), f_conv, w_up[l], ffn_conv_w[l], ffn_conv_b[l], w_down[l])
        return x + f, mix_state + (f_conv_new,)

    x = x_prompt
    bsz, dt = x.shape[0], x.dtype

    def zeros(*shape):
        return jnp.zeros((bsz,) + shape, dt)

    prompt_kv, prompt_states = [], []
    for l in range(DEPTH):
        mk, mv = memory_kv(mem_prompt, norm_mem[l], w_k[l], w_v[l])
        x, st = layer(l, x, mk, mv, zeros(A_CONV - 1, 3 * D_A), zeros(H_A, DK_A, DV_A),
                      zeros(B_CONV - 1, D_B), zeros(D_B), zeros(H_C, DK_C, DV_C),
                      zeros(FFN_CONV - 1, 2 * D_FF))
        prompt_kv.append((mk, mv))
        prompt_states.append(st)
    y_prompt = rmsnorm(x, norm_final)
    p_mem_k, p_mem_v = [jnp.stack(t, axis=0) for t in zip(*prompt_kv)]
    pa_conv, pa_s, pb_conv, pb_h, pc_s, pf_conv = [jnp.stack(t, axis=0) for t in zip(*prompt_states)]

    x = x_sample
    sample_states = []
    for l in range(DEPTH):
        x, st = layer(l, x, cache_mem_k[l], cache_mem_v[l], state_a_conv[l], state_a_S[l],
                      state_b_conv[l], state_b_h[l], state_c_S[l], state_ffn_conv[l])
        sample_states.append(st)
    y_sample = rmsnorm(x, norm_final)
    sa_conv, sa_s, sb_conv, sb_h, sc_s, sf_conv = [jnp.stack(t, axis=0) for t in zip(*sample_states)]

    return (y_prompt, y_sample, p_mem_k, p_mem_v, pa_conv, pa_s, pb_conv, pb_h, pc_s, pf_conv,
            sa_conv, sa_s, sb_conv, sb_h, sc_s, sf_conv)


_drawn_inputs = setup_inputs


def setup_inputs(seed=0):
    import zlib

    import numpy as np

    out = dict(_drawn_inputs(seed))
    spreads = {}
    factors = {'state_c_S': 6.684,
     'a_norm': 6.5,
     'b_b_r': 8.0,
     'b_b_i': 8.0,
     'c_norm': 8.0,
     'norm_attn': 8.0,
     'norm_mem': 2.724,
     'norm_ffn': 2.691,
     'ffn_conv_b': 4.354,
     'norm_final': 2.874}
    for name, (base, spread) in spreads.items():
        noise = np.random.default_rng([zlib.crc32(name.encode()), seed]).standard_normal(out[name].shape)
        drawn = base * np.exp(spread * noise) if base else spread * noise
        out[name] = __import__('jax').numpy.asarray(drawn.astype(out[name].dtype))
    for name, factor in factors.items():
        out[name] = (out[name] * factor).astype(out[name].dtype)
    return out
```

```python
from contextlib import ExitStack

import concourse.bass as bass
from concourse import mybir

F32 = mybir.dt.float32
F32R = mybir.dt.float32r
U32 = mybir.dt.uint32
ALU = mybir.AluOpType
ACT = mybir.ActivationFunctionType
AX_X = mybir.AxisListType.X

P = 128
D = 1024
KC = D // P
PROMPT = 512
SAMPLE = 64
GAP = 4
TOK = PROMPT + GAP + SAMPLE
HALF = TOK // 2
S0 = PROMPT + GAP
PRE = 3
N_A, N_G, N_B, N_C = 512, 4, 256, 256
HEADS = 4
N_MEM = 256
D_FF = 2816
NF = D_FF // P
EPS = 1e-6
TILES = 5
LEVELS = 7


class Steps:

    def __init__(self, sem, rounds):
        self.sem, self.value, self.made = sem, {}, 0
        for r, names in rounds:
            for name in names:
                assert (r, name) not in self.value
                self.value[(r, name)] = len(self.value) + 1

    def at(self, r, name):
        return self.sem, self.value[(r, name)]

    def did(self, r, name):
        self.made += 1
        assert self.value[(r, name)] == self.made, (r, name)
        return self.sem, 1


def tile_len(c):
    return P if c < TILES - 1 else SAMPLE


def tile_at(c):
    return c * P if c < TILES - 1 else S0


def levels_of(c):
    return LEVELS if c < TILES - 1 else LEVELS - 1


COL = {"mix": 0, "attn": 8, "ffn": 16, "mem": 24, "final": 32, "a_w": 40, "b_w": 88, "b_b": 96, "b_r": 98, "b_i": 100,
       "lam": 102, "lb": 104, "b_h": 106, "a_norm": 108, "c_norm": 109,
       "a_st": 128, "b_st": 164, "f_b": 170, "f_w": 256, "f_w2": 384, "f_st0": 428, "f_st1": 512}
PAR_ROWS = [110, 86, 88, 88, 44]


def outputs_of_products():
    outs = [("gates", 0)]
    outs += [("qkv", i) for i in range(12)]
    for kind in ("c_q", "b_gate", "b_x", "c_f", "c_i"):
        outs += [(kind, i) for i in range(2)]
    outs += [("z", i) for i in range(4)] + [("c_g", i) for i in range(2)]
    outs += [("w_out", i) for i in range(8)]
    outs += [("w_k", i) for i in range(4)] + [("w_v", i) for i in range(4)]
    outs += [("w_q", i) for i in range(8)] + [("w_o", i) for i in range(8)]
    for f in range(NF):
        outs += [("up_gate", f), ("up_val", f)]
    outs += [("down", i) for i in range(8)]
    return outs


OUTS = outputs_of_products()
G_OF = {o: g for g, o in enumerate(OUTS)}
SLOT_K = {"down": [8, 8, 6], "w_k": [4, 4], "w_v": [4, 4]}
SLOTS = [(g, j) for g, (kind, i) in enumerate(OUTS) for j in range(len(SLOT_K.get(kind, [8])))]
FIRST_SLOT, LAST_SLOT = {}, {}
for _n, (_g, _j) in enumerate(SLOTS):
    FIRST_SLOT.setdefault(_g, _n)
    LAST_SLOT[_g] = _n
W_IN_COL = {"gates": 2048, "qkv": 0, "z": 1536, "b_x": 2056, "b_gate": 2312, "c_q": 2568, "c_f": 2824, "c_i": 3080,
            "c_g": 3336}
RAW, HL = 2, 2
CONV = {"qkv": 4, "b_x": 4, "up_gate": 3, "up_val": 3}


def schedule():
    out = [("start",)] + [("square", 0, k) for k in range(KC)] + [("split", 0, k) for k in range(KC)] + [("norm", 0)]
    prod = [("product", g) for g in range(len(OUTS))]

    def upto(kind, i):
        n = G_OF[(kind, i)] + 1
        part = [x for x in prod if x[1] < n]
        del prod[:len(part)]
        return part

    out += upto("qkv", 11) + [("gate_rows",)]
    out += upto("c_f", 1) + [("rg",)]
    mixers = []
    gdn = [("gdn", c, ph) for c in range(TILES) for ph in gdn_phases(c)]
    hg = [("hg", c, ph) for c in range(TILES) for ph in hg_phases(c)]
    fill = upto("c_i", 1)
    out += fill + [("hg_prep",)]
    fill = upto("c_g", 1)
    total, h, f = len(gdn), 0, 0
    for i, x in enumerate(gdn):
        mixers.append(x)
        while h < len(hg) and h * total < (i + 1) * len(hg):
            mixers.append(hg[h])
            h += 1
        while f < len(fill) and f * total < (i + 1) * len(fill):
            mixers.append(fill[f])
            f += 1
    out += mixers + [("mix_out",)]
    for i in range(8):
        out += upto("w_out", i) + [("square", 1, i)]
    out += [("mem",)]
    for i in range(8):
        out += upto(("w_k", "w_v")[i // 4], i % 4) + [("split", 1, i)]
    out += [("norm", 1), ("kt",)]
    out += upto("w_q", 7)
    out += [("att", c) for c in range(TILES)]
    out += [("pv",)]
    for i in range(8):
        out += upto("w_o", i) + [("square", 2, i)]
    out += [("split", 2, i) for i in range(8)] + [("norm", 2)]
    out += upto("up_val", NF - 1)
    for i in range(8):
        out += upto("down", i) + [("square", 3, i)]
    out += [("finish",)]
    assert not prod
    return out


def gdn_phases(c):
    return (["rows", "gb", "back", "kk", "turn"] + [f"level{l}" for l in range(1, levels_of(c))] + ["ks", "vnew", "o"])


def hg_phases(c):
    return ["v"] + [f"level{l}" for l in range(levels_of(c) + 1)] + ["kd", "o"]


def build(nc, x_prompt, x_sample, cache_mem_k, cache_mem_v, state_a_conv, state_a_S, state_b_conv, state_b_h, state_c_S,
          state_ffn_conv, mem_prompt, norm_mix, w_in, a_conv_w, a_A_log, a_dt_bias, a_norm, b_conv_w, b_conv_b, b_w_r,
          b_b_r, b_w_i, b_b_i, b_lambda, c_lb_logits, c_norm, w_out, norm_attn, norm_mem, w_q, w_k, w_v, w_o, norm_ffn,
          w_up, ffn_conv_w, ffn_conv_b, w_down, norm_final,
          y_prompt, y_sample, mem_k_out, mem_v_out, pa_conv, pa_S, pb_conv, pb_h, pc_S, pf_conv,
          sa_conv, sa_S, sb_conv, sb_h, sc_S, sf_conv):
    ctx = ExitStack()
    with ctx:
        def sb(name, shape, dt=F32, into=ctx):
            return into.enter_context(nc.sbuf_tensor("t_" + name, shape, dt))

        def sem(name):
            return ctx.enter_context(nc.semaphore(name))

        xT = sb("xT", [P, KC, TOK])
        XH = sb("XH", [P, KC, TOK], F32R)
        XL = sb("XL", [P, KC, TOK], F32R)
        raw = sb("raw", [P, RAW, KC * P])
        WH = sb("WH", [P, HL, KC * P], F32R)
        WL = sb("WL", [P, HL, KC * P], F32R)
        ident = sb("ident", [P, P])
        ones = sb("ones", [P, P])
        half_ones = sb("half_ones", [P, P])
        upto_m = sb("upto_m", [P, P])
        lower = sb("lower", [P, P])
        strict = sb("strict", [P, P])
        lev = sb("lev", [P, LEVELS, P])
        lev0n = sb("lev0n", [P, P])
        par = sb("par", [P, 556])
        NS = sb("NS", [P, TOK])
        R = sb("R", [P, TOK])
        SQ = sb("SQ", [P, 2, TOK])
        tails = sb("tails", [P, 2, 44])

        mix_ctx = ExitStack()
        qkvT = sb("qkvT", [P, 12, TOK], into=mix_ctx)
        zT = sb("zT", [P, 4, TOK], into=mix_ctx)
        xbT = sb("xbT", [P, 2, TOK], into=mix_ctx)
        gateT = sb("gateT", [P, 2, TOK], into=mix_ctx)
        cqT = sb("cqT", [P, 2, TOK], into=mix_ctx)
        ckT = sb("ckT", [P, 2, TOK], into=mix_ctx)
        cbT = sb("cbT", [P, 2, TOK], into=mix_ctx)
        cvT = sb("cvT", [P, 2, TOK], into=mix_ctx)
        cgT = sb("cgT", [P, 2, TOK], into=mix_ctx)
        pre_m = sb("pre_m", [P, 2, TOK + PRE], into=mix_ctx)
        NT = 12
        tmp = sb("tmp", [P, NT, 512], into=mix_ctx)
        Sa = sb("Sa", [P, 2, 512], into=mix_ctx)
        gT = sb("gT", [8, TOK], into=mix_ctx)
        gv = sb("gv", [P, 7, TILES * HEADS], into=mix_ctx)
        gv8 = gv[:, 5:7, :].rearrange("p a b -> p (a b)")
        hE = sb("hE", [P, 2, P], into=mix_ctx)
        hK = sb("hK", [P, 2, P], into=mix_ctx)
        kdt = sb("kdt", [P, 2, P], into=mix_ctx)
        Sc = sb("Sc", [P, 2, 2, P], into=mix_ctx)
        wr_bd = sb("wr_bd", [P, 2, 2, P], into=mix_ctx)
        small = sb("small", [P, 64], into=mix_ctx)
        row8 = sb("row8", [1, 8], into=mix_ctx)
        hQ, att = (xbT[:].rearrange("p a b -> p (a b)")[:, i * 512:(i + 1) * 512].rearrange("p (a b i) -> p a b i", a=2, b=2)
                   for i in range(2))
        vpad = wr_bd
        x_nat = qkvT[:].rearrange("p a b -> p (a b)")[:, 0:TILES * D].rearrange("p (c d) -> p c d", c=TILES)
        par_nat = cqT[:].rearrange("p a b -> p (a b)")[:, 0:640].rearrange("p (a b) -> p a b", a=5)
        st_rows = zT[:].rearrange("p a b -> p (a b)")
        mix_ctx.close()

        att_ctx = ExitStack()
        memH = sb("memH", [P, KC, N_MEM], F32R, into=att_ctx)
        memL = sb("memL", [P, KC, N_MEM], F32R, into=att_ctx)
        nat = sb("nat", [P, 2, D], into=att_ctx)
        Kn = sb("Kn", [P, 2, D], into=att_ctx)
        Vn = sb("Vn", [P, 2, D], into=att_ctx)
        sV = sb("sV", [P, 2, D], into=att_ctx)
        kT = sb("kT", [P, 2, KC, N_MEM], into=att_ctx)
        qT = sb("qT", [P, KC, TOK], into=att_ctx)
        PT = sb("PT", [P, 2, HEADS, PROMPT + SAMPLE], into=att_ctx)
        prob = sb("prob", [P, HEADS, N_MEM], into=att_ctx)
        mstat = sb("mstat", [P, 16], into=att_ctx)
        astat = sb("astat", [P, TILES, 12], into=att_ctx)
        att_ctx.close()

        ffn_ctx = ExitStack()
        FH = sb("FH", [P, NF, TOK], F32R, into=ffn_ctx)
        FL = sb("FL", [P, NF, TOK], F32R, into=ffn_ctx)
        pre_f = sb("pre_f", [P, 1, TOK + PRE], into=ffn_ctx)
        fg = sb("fg", [P, TOK], into=ffn_ctx)
        fv = sb("fv", [P, TOK], into=ffn_ctx)
        tail_f = sb("tail_f", [P, 2, 2, 44], into=ffn_ctx)
        ffn_ctx.close()
        fin_ctx = ExitStack()
        yrow = sb("yrow", [P, TILES, D], into=fin_ctx)
        fstat = sb("fstat", [P, 8], into=fin_ctx)
        frows = sb("frows", [P, 2, P], into=fin_ctx)
        fin_ctx.close()

        pg = [ctx.enter_context(nc.psum_tensor(f"pg{i}", [P, 2, 512], F32)) for i in range(2)]
        pm = ctx.enter_context(nc.psum_tensor("pm", [P, 4, 512], F32))
        A, B, C, DD = (pm[:, i, :] for i in range(4))

        def heads(ap):
            return ap.rearrange("p (h i) -> p h i", h=HEADS)

        def cols(v, n):
            return v.unsqueeze(2).to_broadcast([v.shape[0], v.shape[1], n])

        def over(m, h):
            return m.unsqueeze(1).to_broadcast([m.shape[0], h, m.shape[1]])

        def col(name, i=0, n=1):
            return par[:, COL[name] + i:COL[name] + i + n]

        const_ready = sem("const_ready")
        x_loaded = sem("x_loaded")
        par_loaded = sem("par_loaded")
        state_loaded = sem("state_loaded")
        mem_loaded = sem("mem_loaded")
        cache_loaded = sem("cache_loaded")
        cv_loaded = sem("cv_loaded")
        w_loaded = [sem(f"w_loaded{i}") for i in range(RAW)]
        stored = sem("stored")
        w_high = sem("w_high")
        w_low = sem("w_low")
        slot_done = sem("slot_done")

        SCHED = schedule()
        names = {
            "start_pe": [(0, ["par"] + [f"x{k}" for k in range(KC)] + ["row8"])],
            "start_dve": [(0, ["par"] + [f"x{k}" for k in range(KC)] + ["pad"])],
            "feed_act": [(s, [f"sq{k}" for k in range(KC)] + [f"hi{k}" for k in range(KC) if s < 3]) for s in range(4)],
            "feed_dve": [(s, [f"ns{k}" for k in range(1, KC)] + [("lo" if s < 3 else "xw") + str(k) for k in range(KC)])
                         for s in range(4)],
            "norm_pe": [(s, ["ss"]) for s in range(4)],
            "norm_act": [(s, ["ln", "exp"]) for s in range(3)],
        }
        order = {}
        for key, rounds in names.items():
            order[key] = Steps(sem(key), rounds)
        start_pe, start_dve, feed_act, feed_dve, norm_pe, norm_act = (order[k] for k in (
            "start_pe", "start_dve", "feed_act", "feed_dve", "norm_pe", "norm_act"))

        def post_dve_names(kind, i):
            taps = [f"tap{j}" for j in range(CONV.get(kind, 0))]
            return ((["zero"] if (kind, i) == ("up_gate", 0) else []) + ["evac"] + (["state", "tail"] if kind in CONV else []) + taps + (["prod"] if kind == "up_val" else []))

        post_dve = Steps(sem("post_dve"), [(g, post_dve_names(*OUTS[g])) for g in range(len(OUTS))])
        post_act = Steps(sem("post_act"), [(g, {"qkv": ["silu"], "c_q": ["silu"], "b_gate": ["gelu"], "up_gate": ["silu"],
                                                "up_val": ["hi"]}.get(OUTS[g][0], [])) for g in range(len(OUTS))])
        post_pool = Steps(sem("post_pool"), [(G_OF[("up_val", f)], ["lo"]) for f in range(NF)])
        gate_pe = Steps(sem("gate_pe"), [(0, ["turn", "gc"])])
        gate_dve = Steps(sem("gate_dve"), [(0, ["clear", "rows", "rows4", "arg", "pos", "neg", "g0", "g", "gc", "be"])])
        gate_act = Steps(sem("gate_act"), [(0, ["beta", "eA", "exp", "ln", "egc"])])
        rg_pe = Steps(sem("rg_pe"), [(i, ["gates"]) for i in range(2)])
        rg_dve = Steps(sem("rg_dve"), [(0, ["nlam", "abs", "sp", "c8", "c8n"])] + [
            (1 + i, ["a2", "m2", "gx"]) for i in range(2)] + [(3 + i, ["gap", "u", "scan", "scan_s", "ht", "y"]) for i in range(2)])
        rg_act = Steps(sem("rg_act"), [(0, ["exp", "ln"])] + [(1 + i, ["r", "i"]) for i in range(2)] + [(3, ["cf"])] + [
            (4 + i, ["a", "th"]) for i in range(2)] + [(6, ["mult"])])
        gdn_pe = Steps(sem("gdn_pe"), [(c, ["rows", "gb", "back", "kk", "qk", "turnL", "turnQ"] + [
            x for l in range(1, levels_of(c)) for x in ((f"T{l}", f"X{l}", f"U{l}") if l < levels_of(c) - 1 else (f"T{l}", f"U{l}"))] + [
            "ks", "vnew", "o", "S"]) for c in range(TILES)])
        gdn_dve = Steps(sem("gdn_dve"), [(c, ["ssq", "ssk", "qn", "kn", "vb", "gd", "klast", "L", "QK", "Xt", "X", "Ut", "U"] + [
            x for l in range(1, levels_of(c)) for x in ((f"X{l}", f"U{l}") if l < levels_of(c) - 1 else (f"U{l}",))] + [
            "r1", "r", "S"]) for c in range(TILES)])
        gdn_act = Steps(sem("gdn_act"), [(c, ["sqq", "sqk", "ln", "rq", "rk", "gl", "kds", "G", "qnT", "knT", "qdT", "LT", "QKT"] + [
            f"T{l}" for l in range(1, levels_of(c))] + ["vn", "o"]) for c in range(TILES)])
        gdn_pool = Steps(sem("gdn_pool"), [(c, ["diag", "qd", "kd", "Pm", "bP"] + [
            f"B{l}" for l in range(1, levels_of(c))] + ["Sgl"]) for c in range(TILES)])
        hgp_dve = Steps(sem("hgp_dve"), [(0, ["e0", "rec", "sm", "lb", "oml", "q", "v"]), (1, ["f", "k"] + [f"b{i}_{c}" for i in range(2) for c in range(TILES)])])
        hgp_act = Steps(sem("hgp_act"), [(0, ["e"]), (1, ["lf"])])
        hg_pe = Steps(sem("hg_pe"), [(c, ["v"] + [f"A{l}" for l in range(levels_of(c) + 1)] + ["kd", "o", "S"]) for c in range(TILES)])
        hg_dve = Steps(sem("hg_dve"), [(c, ["q0", "att0"] + [
            x for l in range(1, levels_of(c) + 1) for x in (f"dk{l}", f"dq{l}", f"qa{l}", f"qb{l}", f"att{l}")] + [
            "S00", "S10", "S01", "S11"]) for c in range(TILES)])
        hg_act = Steps(sem("hg_act"), [(c, ["v0", "v1"] + [f"E{l}" for l in range(1, levels_of(c) + 1)] + [
            "ek0", "ek1", "kdt", "eq", "eb", "o"]) for c in range(TILES)])
        hg_pool = Steps(sem("hg_pool"), [(c, ["k0"] + [f"k{l}" for l in range(1, levels_of(c) + 1)] + ["kd", "qe"]) for c in range(TILES)])
        mo_pe = Steps(sem("mo_pe"), [(i, ["ss"]) for i in range(6)] + [(6, ["st"])])
        mo_act = Steps(sem("mo_act"), [(0, ["siluz", "silug"])] + [(1 + i, ["sq", "ln", "exp"]) for i in range(6)] + [
            (7 + j, ["hi"]) for j in range(8)] + [(15, ["st"])])
        mo_dve = Steps(sem("mo_dve"), [(i, ["on", "oz"]) for i in range(6)] + [(6 + j, ["lo"]) for j in range(8)])
        mem_pe = Steps(sem("mem_pe"), [(k, ["t"]) for k in range(KC)])
        mem_act = Steps(sem("mem_act"), [(0, ["sq0", "sq1", "ln", "exp"])] + [(1 + k, ["hi"]) for k in range(KC)])
        mem_dve = Steps(sem("mem_dve"), [(k, ["lo"]) for k in range(KC)])
        kt_pe = Steps(sem("kt_pe"), [(j, ["t"]) for j in range(8)])
        kt_act = Steps(sem("kt_act"), [(j, ["t"]) for j in range(8)])
        at_pe = Steps(sem("at_pe"), [(c, ["s", "t"]) for c in range(TILES)])
        at_dve = Steps(sem("at_dve"), [(c, ["max", "nmax", "rec", "norm"]) for c in range(TILES)])
        at_act = Steps(sem("at_act"), [(c, ["exp0", "exp1", "exp2", "exp3", "pt"]) for c in range(TILES)])
        pv_pe = Steps(sem("pv_pe"), [(j, ["o"]) for j in range(8)])
        pv_act = Steps(sem("pv_act"), [(j, ["hi", "his"]) for j in range(8)])
        pv_dve = Steps(sem("pv_dve"), [(j, ["lo", "los"]) for j in range(8)])
        fin_pe = Steps(sem("fin_pe"), [(0, ["ss", "st"])] + [(1 + c, ["y"]) for c in range(TILES)])
        fin_act = Steps(sem("fin_act"), [(0, ["ln", "exp"])] + [(1 + c, ["y"]) for c in range(TILES)])
        fin_dve = Steps(sem("fin_dve"), [(0, ["st"])])

        block = ctx.enter_context(nc.Block())
        G_WOUT, G_WK, G_WQ, G_WO, G_UP, G_DOWN = (G_OF[(k, 0)] for k in ("w_out", "w_k", "w_q", "w_o", "up_gate", "down"))
        G_LAST_IN = G_WOUT - 1

        MIX_STORES, ALL_STORES = 12, 12 + 2 + 2 + TILES
        CONSTS, STATE_READY = 41, 16 * 7

        def rows_of(v):
            return v.rearrange("(k p) -> k p", p=P)

        def rows_of2(v):
            return v.rearrange("j (k p) -> (j k) p", p=P)

        PARAMS = [(0, COL["mix"], rows_of(norm_mix[0])), (0, COL["attn"], rows_of(norm_attn[0])),
                  (0, COL["ffn"], rows_of(norm_ffn[0])), (0, COL["mem"], rows_of(norm_mem[0])),
                  (0, COL["final"], rows_of(norm_final)), (0, COL["a_w"], rows_of2(a_conv_w[0])),
                  (0, COL["b_w"], rows_of2(b_conv_w[0])), (0, COL["b_b"], rows_of(b_conv_b[0])),
                  (0, COL["b_r"], rows_of(b_b_r[0])), (0, COL["b_i"], rows_of(b_b_i[0])),
                  (0, COL["lam"], rows_of(b_lambda[0])), (0, COL["lb"], rows_of(c_lb_logits[0])),
                  (0, COL["b_h"], rows_of(state_b_h[0, 0])), (0, COL["a_norm"], a_norm),
                  (1, 0, rows_of2(state_a_conv[0, 0])), (1, 36, rows_of2(state_b_conv[0, 0])), (1, 42, rows_of(ffn_conv_b[0])),
                  (2, 0, rows_of2(ffn_conv_w[0, 0:2])), (3, 0, rows_of(ffn_conv_w[0, 2])),
                  (3, 44, rows_of(state_ffn_conv[0, 0, 0])), (4, 0, rows_of(state_ffn_conv[0, 0, 1]))]
        PAR_DMAS = len(PARAMS) + 4


        @block.sync
        def _(sp):
            sp.dma_start(x_nat[:, 0:4, :], x_prompt[0].rearrange("(c p) d -> p c d", p=P)).then_inc(x_loaded, 16)
            sp.dma_start(x_nat[0:SAMPLE, 4, :], x_sample[0]).then_inc(x_loaded, 16)

            def source(n):
                g, j = SLOTS[n]
                kind, i = OUTS[g]
                if kind in W_IN_COL:
                    c0 = W_IN_COL[kind] + i * P
                    return w_in[0][:, c0:c0 + P].rearrange("(k p) n -> p k n", p=P), KC * P
                if kind in ("w_k", "w_v"):
                    w = {"w_k": w_k, "w_v": w_v}[kind][0]
                    return w[4 * j * P:4 * (j + 1) * P, i * 256:(i + 1) * 256].rearrange("(k p) n -> p k n", p=P), KC * P
                if kind in ("up_gate", "up_val"):
                    c0 = i * P + (D_FF if kind == "up_val" else 0)
                    return w_up[0][:, c0:c0 + P].rearrange("(k p) n -> p k n", p=P), KC * P
                if kind == "down":
                    nk = SLOT_K["down"][j]
                    return w_down[0][8 * j * P:(8 * j + nk) * P, i * P:(i + 1) * P].rearrange("(k p) n -> p k n", p=P), nk * P
                w = {"w_out": w_out, "w_q": w_q, "w_o": w_o}[kind][0]
                return w[:, i * P:(i + 1) * P].rearrange("(k p) n -> p k n", p=P), KC * P

            for n in range(len(SLOTS)):
                if n >= RAW:
                    sp.wait_ge(w_low, n - RAW + 1)
                src, size = source(n)
                nk = src.shape[1]
                sp.dma_start(raw[:, n % RAW, 0:size].rearrange("p (k n) -> p k n", k=nk), src).then_inc(w_loaded[n % RAW], 16)
                g = SLOTS[n][0]
                if OUTS[g] == ("w_out", 4):
                    sp.wait_ge(*mo_dve.at(13, "lo"))
                    sp.wait_ge(*mo_act.at(15, "st"))
                    sp.wait_ge(*gdn_dve.at(TILES - 1, "S"))
                    sp.wait_ge(*hg_dve.at(TILES - 1, "S11"))
                    sp.wait_ge(stored, 16 * MIX_STORES)
                    sp.dma_start(nat[:], mem_prompt[0].rearrange("(c p) d -> p c d", p=P)).then_inc(mem_loaded, 16)
                    sp.dma_start(sV[:], cache_mem_v[0, 0].rearrange("(c p) h d -> p c (h d)", p=P)).then_inc(cv_loaded, 16)
                if OUTS[g] == ("w_q", 0):
                    sp.wait_ge(*mem_pe.at(KC - 1, "t"))
                    sp.wait_ge(*mem_act.at(0, "sq1"))
                    sp.dma_start(nat[:], cache_mem_k[0, 0].rearrange("(c p) h d -> p c (h d)", p=P)).then_inc(cache_loaded, 16)
            sp.wait_ge(stored, 16 * ALL_STORES)

        @block.tensor
        def _(pe):
            def mm(out, lhsT, rhs, start=True, stop=True):
                return pe.matmul(out, lhsT, rhs, start=start, stop=stop)

            def product(g):
                kind, i = OUTS[g]
                ps = pg[g % 2]
                if g >= 2:
                    pe.wait_ge(*post_dve.at(g - 2, "evac"))
                elif g == 1 or g == 0:
                    pe.wait_ge(*start_dve.at(0, f"x{KC - 1}"))
                if g == G_WOUT:
                    pe.wait_ge(*mo_dve.at(13, "lo"))
                if g == G_WK:
                    pe.wait_ge(*mem_dve.at(KC - 1, "lo"))
                if g == G_WQ:
                    pe.wait_ge(*feed_dve.at(1, f"lo{KC - 1}"))
                if g == G_WO:
                    pe.wait_ge(*pv_dve.at(7, "los"))
                if g == G_DOWN:
                    pe.wait_ge(*post_pool.at(G_OF[("up_val", NF - 1)], "lo"))
                for n in range(FIRST_SLOT[g], LAST_SLOT[g] + 1):
                    j = n - FIRST_SLOT[g]
                    pe.wait_ge(w_low, n + 1)
                    nk = SLOT_K.get(kind, [8])[j]
                    if kind in ("w_k", "w_v"):
                        wh = WH[:, n % HL, :].rearrange("p (k n) -> p k n", k=4)
                        wl = WL[:, n % HL, :].rearrange("p (k n) -> p k n", k=4)
                        for k in range(4):
                            first, last = (j == 0 and k == 0), (j == 1 and k == 3)
                            for t in range(2):
                                o = ps[:, t, 0:N_MEM]
                                mh, ml = (m[:, 4 * j + k, t * P:(t + 1) * P] for m in (memH, memL))
                                mm(o, mh, wh[:, k, :], first, False)
                                mm(o, mh, wl[:, k, :], False, False)
                                q = mm(o, ml, wh[:, k, :], False, last)
                    else:
                        wh = WH[:, n % HL, :].rearrange("p (k n) -> p k n", k=KC)
                        wl = WL[:, n % HL, :].rearrange("p (k n) -> p k n", k=KC)
                        xh, xl = (FH, FL) if kind == "down" else (XH, XL)
                        for k in range(nk):
                            kk = 8 * j + k
                            if g in (0, G_UP):
                                pe.wait_ge(*feed_dve.at(0 if g == 0 else 2, f"lo{k}"))
                            first, last = (j == 0 and k == 0), (n == LAST_SLOT[g] and k == nk - 1)
                            for w, x, s0, s1 in ((wh, xh, first, False), (wh, xl, False, False), (wl, xh, False, last)):
                                for h in range(2):
                                    q = mm(ps[:, h, 0:HALF], w[:, k, :], x[:, kk, h * HALF:(h + 1) * HALF], s0, s1)
                    q.then_inc(slot_done, 1)

            def norm(s):
                pe.wait_ge(*feed_dve.at(s, f"ns{KC - 1}"))
                if s == 1:
                    pe.wait_ge(*mo_act.at(15, "st"))
                if s == 2:
                    pe.wait_ge(*pv_dve.at(7, "los"))
                    pe.wait_ge(*pv_act.at(7, "his"))
                if s == 0:
                    pe.wait_ge(*start_dve.at(0, "pad"))
                for h in range(2):
                    q = mm(pm[:, h, 0:HALF], ones[:], NS[:, h * HALF:(h + 1) * HALF])
                q.then_inc(*norm_pe.did(s, "ss"))

            def start():
                pe.wait_ge(const_ready, CONSTS)
                pe.wait_ge(par_loaded, 16 * PAR_DMAS)
                c0 = 0
                for t, rows in enumerate(PAR_ROWS):
                    dst = pg[0][:, 0, t * P:t * P + rows] if t < 4 else pg[0][:, 1, 0:rows]
                    q = pe.transpose(dst, par_nat[0:rows, t, :], ident[0:rows, 0:rows])
                q.then_inc(*start_pe.did(0, "par"))
                pe.wait_ge(x_loaded, 32)
                for k in range(KC):
                    ps = pg[(k + 1) % 2]
                    if k == 1:
                        pe.wait_ge(*start_dve.at(0, "par"))
                    if k >= 2:
                        pe.wait_ge(*start_dve.at(0, f"x{k - 2}"))
                    for c in range(4):
                        pe.transpose(ps[:, 0, c * P:(c + 1) * P], x_nat[:, c, k * P:(k + 1) * P], ident[:])
                    pe.transpose(ps[:, 1, 0:SAMPLE], x_nat[0:SAMPLE, 4, k * P:(k + 1) * P],
                                 ident[0:SAMPLE, 0:SAMPLE]).then_inc(*start_pe.did(0, f"x{k}"))
                mm(A[:, 0:8], ones[0:1, :], row8[0:1, :]).then_inc(*start_pe.did(0, "row8"))

            def gate_rows():
                pe.wait_ge(*post_dve.at(0, "evac"))
                pe.wait_ge(*norm_act.at(0, "exp"))
                for c in range(TILES):
                    n = tile_len(c)
                    q = pe.transpose(C[0:n, c * 8:(c + 1) * 8], gT[:, tile_at(c):tile_at(c) + n], ident[0:8, 0:8])
                q.then_inc(*gate_pe.did(0, "turn"))
                pe.wait_ge(*gate_dve.at(0, "g"))
                mm(DD[:, 0:TILES * 4], upto_m[:], gv[:, 1, 0:TILES * 4]).then_inc(*gate_pe.did(0, "gc"))

            def rg():
                for i in range(2):
                    pe.wait_ge(*post_dve.at(G_OF[("b_x", i)], "tap3"))
                    pe.wait_ge(*gate_dve.at(0, "gc"))
                    pe.wait_ge(state_loaded, STATE_READY)
                    if i:
                        pe.wait_ge(*rg_act.at(1, "i"))
                    for gate in range(2):
                        for h in range(2):
                            q = mm(pm[:, 2 * gate + h, 0:HALF], wr_bd[:, gate, i, :], xbT[:, i, h * HALF:(h + 1) * HALF])
                    q.then_inc(*rg_pe.did(i, "gates"))

            def gdn(c, ph):
                n, t0 = tile_len(c), tile_at(c)

                def T(i):
                    return heads(tmp[:, i, :])

                S = heads(Sa[:, 1 if c == TILES - 1 else 0, :])
                a, b, cc = heads(A), heads(B), heads(C)
                if ph == "rows":
                    if c == 0:
                        pe.wait_ge(*post_act.at(G_OF[("qkv", 11)], "silu"))
                        pe.wait_ge(*rg_act.at(2, "i"))
                    else:
                        pe.wait_ge(*gdn_dve.at(c - 1, "S"))
                        pe.wait_ge(*gdn_act.at(c - 1, "o"))
                    for part, bank in enumerate((a, b, cc)):
                        for h in range(HEADS):
                            q = pe.transpose(bank[0:n, h, :], qkvT[:, 4 * part + h, t0:t0 + n], ident[:])
                    q.then_inc(*gdn_pe.did(c, "rows"))
                elif ph == "gb":
                    pe.wait_ge(*gdn_pool.at(c, "diag"))
                    pe.wait_ge(*gdn_dve.at(c, "qn"))
                    for h in range(HEADS):
                        q = mm(a[:, h, 0:n], ones[0:n, :], heads(SQ[:, 1, 0:512])[0:n, h, 0:n])
                    q.then_inc(*gdn_pe.did(c, "gb"))
                elif ph == "back":
                    pe.wait_ge(*gdn_dve.at(c, "vb"))
                    for h in range(HEADS):
                        pe.transpose(b[:, h, 0:n], T(0)[0:n, h, :], ident[0:n, 0:n])
                    for h in range(HEADS):
                        pe.transpose(cc[:, h, 0:n], T(1)[0:n, h, :], ident[0:n, 0:n])
                    pe.wait_ge(*gdn_dve.at(c, "klast"))
                    pe.wait_ge(*gdn_act.at(c, "gl"))
                    pe.wait_ge(*gdn_pool.at(c, "qd"))
                    for h in range(HEADS):
                        q = pe.transpose(a[:, h, 0:n], T(2)[0:n, h, :], ident[0:n, 0:n])
                    q.then_inc(*gdn_pe.did(c, "back"))
                elif ph == "kk":
                    pe.wait_ge(*gdn_act.at(c, "knT"))
                    for h in range(HEADS):
                        q = mm(b[0:n, h, 0:n], T(8)[:, h, 0:n], T(8)[:, h, 0:n])
                    q.then_inc(*gdn_pe.did(c, "kk"))
                    for h in range(HEADS):
                        q = mm(cc[0:n, h, 0:n], T(7)[:, h, 0:n], T(8)[:, h, 0:n])
                    q.then_inc(*gdn_pe.did(c, "qk"))
                elif ph == "turn":
                    pe.wait_ge(*gdn_act.at(c, "qdT"))
                    pe.wait_ge(*gdn_dve.at(c, "L"))
                    for h in range(HEADS):
                        q = pe.transpose(a[0:n, h, 0:n], T(0)[0:n, h, 0:n], ident[0:n, 0:n])
                    q.then_inc(*gdn_pe.did(c, "turnL"))
                    pe.wait_ge(*gdn_dve.at(c, "QK"))
                    for h in range(HEADS):
                        q = pe.transpose(b[0:n, h, 0:n], T(1)[0:n, h, 0:n], ident[0:n, 0:n])
                    q.then_inc(*gdn_pe.did(c, "turnQ"))
                elif ph.startswith("level"):
                    l = int(ph[5:])
                    last = l == levels_of(c) - 1
                    pe.wait_ge(*gdn_pool.at(c, f"B{l}"))
                    pe.wait_ge(*gdn_dve.at(c, f"U{l - 1}" if l > 1 else "U"))
                    pe.wait_ge(*gdn_act.at(c, f"T{l - 1}" if l > 1 else "QKT"))
                    for h in range(HEADS):
                        q = mm(a[0:n, h, 0:n], T(1)[0:n, h, 0:n], T(2)[0:n, h, 0:n])
                    q.then_inc(*gdn_pe.did(c, f"T{l}"))
                    pe.wait_ge(*gdn_act.at(c, f"T{l}"))
                    if not last:
                        for h in range(HEADS):
                            q = mm(b[0:n, h, 0:n], T(5)[0:n, h, 0:n], T(0)[0:n, h, 0:n])
                        q.then_inc(*gdn_pe.did(c, f"X{l}"))
                    for h in range(HEADS):
                        q = mm(cc[0:n, h, 0:n], T(0)[0:n, h, 0:n], T(5)[0:n, h, 0:n])
                    q.then_inc(*gdn_pe.did(c, f"U{l}"))
                elif ph == "ks":
                    if c in (0, TILES - 1):
                        pe.wait_ge(state_loaded, STATE_READY)
                    for h in range(HEADS):
                        q = mm(a[0:n, h, :], T(8)[:, h, 0:n], S[:, h, :])
                    q.then_inc(*gdn_pe.did(c, "ks"))
                elif ph == "vnew":
                    pe.wait_ge(*gdn_dve.at(c, "r"))
                    for h in range(HEADS):
                        q = mm(b[0:n, h, :], T(5)[0:n, h, 0:n], T(6)[0:n, h, :])
                    q.then_inc(*gdn_pe.did(c, "vnew"))
                elif ph == "o":
                    pe.wait_ge(*gdn_act.at(c, "vn"))
                    for h in range(HEADS):
                        mm(cc[:, h, 0:n], S[:, h, :], T(9)[:, h, 0:n], True, False)
                        q = mm(cc[:, h, 0:n], T(7)[0:n, h, :], T(11)[0:n, h, 0:n], False, True)
                    q.then_inc(*gdn_pe.did(c, "o"))
                    for h in range(HEADS):
                        q = mm(a[:, h, :], T(3)[0:n, h, :], T(7)[0:n, h, :])
                    q.then_inc(*gdn_pe.did(c, "S"))

            def hg(c, ph):
                n, t0 = tile_len(c), tile_at(c)
                d4 = DD.rearrange("p (a b i) -> p a b i", a=2, b=2)
                d2 = DD[:, 0:256].rearrange("p (a i) -> p a i", a=2)
                if ph == "v":
                    pe.wait_ge(*post_dve.at(G_OF[("c_i", 1)], "evac"))
                    if c == 0:
                        pe.wait_ge(*rg_act.at(2, "i"))
                    else:
                        pe.wait_ge(*hg_dve.at(c - 1, "S11"))
                    for i in range(2):
                        q = pe.transpose(d2[0:n, i, :], cvT[:, i, t0:t0 + n], ident[:])
                    q.then_inc(*hg_pe.did(c, "v"))
                elif ph.startswith("level"):
                    l = int(ph[5:])
                    pe.wait_ge(*hg_pool.at(c, f"k{l}"))
                    pe.wait_ge(*hg_dve.at(c, f"qb{l}" if l else "q0"))
                    if l:
                        pe.wait_ge(*hg_dve.at(c, f"att{l - 1}"))
                    else:
                        pe.wait_ge(*hg_act.at(c, "v1"))
                    for i in range(2):
                        q = mm(d4[0:n, i, :, 0:n], hK[:, i, 0:n], hQ[:, i, :, 0:n])
                    q.then_inc(*hg_pe.did(c, f"A{l}"))
                elif ph == "kd":
                    pe.wait_ge(*hg_pool.at(c, "kd"))
                    pe.wait_ge(*hg_dve.at(c, f"att{levels_of(c)}"))
                    for i in range(2):
                        q = pe.transpose(d2[0:n, i, :], hK[:, i, 0:n], ident[:])
                    q.then_inc(*hg_pe.did(c, "kd"))
                elif ph == "o":
                    Sx = Sc[:, 1 if c == TILES - 1 else 0]
                    pe.wait_ge(*hg_pool.at(c, "qe"))
                    pe.wait_ge(*hg_act.at(c, "kdt"))
                    if c in (0, TILES - 1):
                        pe.wait_ge(state_loaded, STATE_READY)
                    for i in range(2):
                        mm(d4[:, 0, i, 0:n], Sx[:, i, :], hE[:, i, 0:n], True, False)
                        mm(d4[:, 0, i, 0:n], vpad[0:n, i, 0, :], att[0:n, i, 0, 0:n], False, False)
                        q = mm(d4[:, 0, i, 0:n], vpad[0:n, i, 1, :], att[0:n, i, 1, 0:n], False, True)
                    q.then_inc(*hg_pe.did(c, "o"))
                    for i in range(2):
                        mm(d4[:, 1, i, :], kdt[0:n, i, :], vpad[0:n, i, 0, :], True, False)
                        q = mm(d4[:, 1, i, :], kdt[0:n, i, :], vpad[0:n, i, 1, :], False, True)
                    q.then_inc(*hg_pe.did(c, "S"))

            def mix_out():
                for i in range(6):
                    pe.wait_ge(*mo_act.at(1 + i, "sq"))
                    if i == 0:
                        pe.wait_ge(*gdn_dve.at(TILES - 1, "S"))
                        pe.wait_ge(*gdn_act.at(TILES - 1, "o"))
                        pe.wait_ge(*hg_act.at(TILES - 1, "o"))
                        pe.wait_ge(*hg_dve.at(TILES - 1, "S11"))
                    if i >= 2:
                        pe.wait_ge(*mo_act.at(1 + i - 2, "ln"))
                    for h in range(2):
                        q = mm(pm[:, 2 * (i % 2) + h, 0:HALF], (ones if i < 4 else half_ones)[:], SQ[:, i % 2, h * HALF:(h + 1) * HALF])
                    q.then_inc(*mo_pe.did(i, "ss"))
                pe.wait_ge(*mo_act.at(6, "ln"))
                for r in range(2):
                    q = pe.transpose(pm[0:44, r, 0:P], tails[:, r, :], ident[:])
                q.then_inc(*mo_pe.did(6, "st"))

            def mem():
                pe.wait_ge(mem_loaded, 16)
                for k in range(KC):
                    if k >= 2:
                        pe.wait_ge(*mem_dve.at(k - 2, "lo"))
                    else:
                        pe.wait_ge(*mo_act.at(15, "st"))
                    for t in range(2):
                        q = pe.transpose(pm[:, 2 + k % 2, t * P:(t + 1) * P], nat[:, t, k * P:(k + 1) * P], ident[:])
                    q.then_inc(*mem_pe.did(k, "t"))

            def kt():
                for j in range(8):
                    src = Kn if j < 4 else nat
                    if j == 0:
                        pe.wait_ge(*post_dve.at(G_OF[("w_k", 3)], "evac"))
                        pe.wait_ge(*mem_dve.at(KC - 1, "lo"))
                        pe.wait_ge(*norm_act.at(1, "ln"))
                    if j == 4:
                        pe.wait_ge(cache_loaded, 16)
                    if j >= 4:
                        pe.wait_ge(*kt_act.at(j - 4, "t"))
                    for d in range(2):
                        for t in range(2):
                            ch = 2 * (j % 4) + d
                            q = pe.transpose(pm[:, j % 4, d * 256 + t * P:d * 256 + (t + 1) * P], src[:, t, ch * P:(ch + 1) * P], ident[:])
                    q.then_inc(*kt_pe.did(j, "t"))

            def attention(c):
                n, t0 = tile_len(c), tile_at(c)
                kx = kT[:, 1 if c == TILES - 1 else 0]
                if c == 0:
                    pe.wait_ge(*kt_act.at(7, "t"))
                    pe.wait_ge(*post_dve.at(G_OF[("w_q", 7)], "evac"))
                else:
                    pe.wait_ge(*at_act.at(c - 1, "exp3"))
                for h in range(HEADS):
                    o = pm[0:n, h // 2, (h % 2) * 256:(h % 2 + 1) * 256]
                    mm(o, qT[:, 2 * h, t0:t0 + n], kx[:, 2 * h, :], True, False)
                    q = mm(o, qT[:, 2 * h + 1, t0:t0 + n], kx[:, 2 * h + 1, :], False, True)
                q.then_inc(*at_pe.did(c, "s"))
                pe.wait_ge(*at_dve.at(c, "norm"))
                if c:
                    pe.wait_ge(*at_act.at(c - 1, "pt"))
                for t in range(2):
                    for h in range(HEADS):
                        q = pe.transpose(pm[:, 2 + t, h * P:h * P + n], prob[0:n, h, t * P:(t + 1) * P], ident[0:n, 0:n])
                q.then_inc(*at_pe.did(c, "t"))

            def pv():
                pe.wait_ge(*at_act.at(TILES - 1, "pt"))
                pe.wait_ge(cv_loaded, 16)
                pe.wait_ge(*post_dve.at(G_OF[("w_v", 3)], "evac"))
                for j in range(8):
                    h = j // 2
                    if j >= 2:
                        pe.wait_ge(*pv_dve.at(j - 2, "los"))
                    for (v, b, s0, s1) in ((Vn, 0, 0, PROMPT), (sV, 1, PROMPT, PROMPT + SAMPLE)):
                        for t in range(2):
                            q = mm(pm[:, 2 * (j % 2) + b, 0:s1 - s0], v[:, t, j * P:(j + 1) * P], PT[:, t, h, s0:s1], t == 0, t == 1)
                    q.then_inc(*pv_pe.did(j, "o"))

            def finish():
                pe.wait_ge(*feed_dve.at(3, f"ns{KC - 1}"))
                for c in range(TILES):
                    n, t0 = tile_len(c), tile_at(c)
                    q = mm(A[0:n, 2 * c:2 * c + 2], NS[:, t0:t0 + n], ones[:, 0:2])
                q.then_inc(*fin_pe.did(0, "ss"))
                for r in range(2):
                    q = pe.transpose(B[0:88, r * P:(r + 1) * P], tail_f[:, r].rearrange("p a b -> p (a b)"), ident[:])
                q.then_inc(*fin_pe.did(0, "st"))
                for c in range(TILES):
                    n, t0 = tile_len(c), tile_at(c)
                    if c >= 2:
                        pe.wait_ge(*fin_act.at(1 + c - 2, "y"))
                    else:
                        pe.wait_ge(*post_dve.at(len(OUTS) - 1, "evac"))
                        pe.wait_ge(*feed_dve.at(3, f"xw{KC - 1}"))
                    ps = pg[c % 2]
                    for k in range(KC):
                        q = pe.transpose(ps[0:n, k // 4, (k % 4) * P:(k % 4 + 1) * P], xT[:, k, t0:t0 + n], ident[:])
                    q.then_inc(*fin_pe.did(1 + c, "y"))

            for step in SCHED:
                what, *args = step
                if what == "start":
                    start()
                elif what == "product":
                    product(*args)
                elif what == "norm" and args[0] < 3:
                    norm(*args)
                elif what == "gate_rows":
                    gate_rows()
                elif what == "rg":
                    rg()
                elif what == "gdn":
                    gdn(*args)
                elif what == "hg":
                    hg(*args)
                elif what == "mix_out":
                    mix_out()
                elif what == "mem":
                    mem()
                elif what == "kt":
                    kt()
                elif what == "att":
                    attention(*args)
                elif what == "pv":
                    pv()
                elif what == "finish":
                    finish()


        @block.vector
        def _(v):
            def halves(ap):
                return ap.rearrange("p (h t) -> p h t", h=2)

            Rh = halves(R[:])
            conv_no = [0]

            def settle(steps):
                if steps.made:
                    v.wait_ge(steps.sem, steps.made)

            def start():
                v.wait_ge(*start_pe.at(0, "par"))
                for t, rows in enumerate(PAR_ROWS):
                    src = pg[0][:, 0, t * P:t * P + rows] if t < 4 else pg[0][:, 1, 0:rows]
                    q = v.tensor_copy(par[:, t * P:t * P + rows], src)
                q.then_inc(*start_dve.did(0, "par"))
                for k in range(KC):
                    v.wait_ge(*start_pe.at(0, f"x{k}"))
                    ps = pg[(k + 1) % 2]
                    v.tensor_copy(xT[:, k, 0:PROMPT], ps[:, 0, 0:PROMPT])
                    v.tensor_copy(xT[:, k, S0:TOK], ps[:, 1, 0:SAMPLE]).then_inc(*start_dve.did(0, f"x{k}"))
                v.wait_ge(*start_pe.at(0, "row8"))
                v.tensor_copy(small[:, 0:8], A[:, 0:8]).then_inc(*start_dve.did(0, "pad"))

            def square(s, k):
                if k:
                    v.wait_ge(*feed_act.at(s, f"sq{k}"))
                    settle(feed_dve)
                    v.tensor_tensor(NS[:], NS[:], SQ[:, k % 2, :], ALU.add).then_inc(*feed_dve.did(s, f"ns{k}"))
                if s == 3 and k == KC - 1:
                    for j in range(KC):
                        v.tensor_scalar(xT[:, j, :], xT[:, j, :], col("final", j), None, ALU.mult)\
                            .then_inc(*feed_dve.did(3, f"xw{j}"))

            def split(s, k):
                name = ("mix", "attn", "ffn")[s]
                v.wait_ge(*feed_act.at(s, f"hi{k}"))
                v.scalar_tensor_tensor(XL[:, k, :], xT[:, k, :], col(name, k), XH[:, k, :].bitcast(F32), ALU.mult,
                                       ALU.subtract).then_inc(*feed_dve.did(s, f"lo{k}"))

            def post(g):
                kind, i = OUTS[g]
                ps = pg[g % 2]
                if (kind, i) == ("up_gate", 0):
                    v.wait_ge(*pv_pe.at(7, "o"))
                    v.memset(pre_f[:, 0, 0:PRE], 0.0).then_inc(*post_dve.did(g, "zero"))
                v.wait_ge(slot_done, LAST_SLOT[g] + 1)
                if kind in ("w_out", "w_o", "down"):
                    if kind == "down":
                        pass
                    v.tensor_tensor(halves(xT[:, i, :]), ps[:, :, 0:HALF], halves(xT[:, i, :]), ALU.add)\
                        .then_inc(*post_dve.did(g, "evac"))
                    return
                if kind in ("w_k", "w_v"):
                    v.wait_ge(*mem_act.at(0, "exp"))
                    to = (Kn if kind == "w_k" else Vn)
                    for t in range(2):
                        q = v.tensor_scalar(to[:, t, i * 256:(i + 1) * 256], ps[:, t, 0:N_MEM], mstat[:, 4 + t:5 + t], None, ALU.mult)
                    q.then_inc(*post_dve.did(g, "evac"))
                    return
                v.wait_ge(*norm_act.at(0 if g < G_WOUT else 1 if kind == "w_q" else 2, "exp"))
                if kind == "gates":
                    v.tensor_tensor(halves(gT[:]), ps[0:8, :, 0:HALF], Rh[0:8], ALU.mult).then_inc(*post_dve.did(g, "evac"))
                    return
                if kind not in CONV:
                    to = {"z": zT, "b_gate": gateT, "c_q": cqT, "c_f": ckT, "c_i": cvT, "c_g": cgT, "w_q": qT}[kind]
                    v.tensor_tensor(halves(to[:, i, :]), ps[:, :, 0:HALF], Rh, ALU.mult).then_inc(*post_dve.did(g, "evac"))
                    return
                taps, b = CONV[kind], conv_no[0] % 2
                conv_no[0] += 1
                pre = pre_m[:, b, :] if kind in ("qkv", "b_x") else pre_f[:, 0, :]
                settle(post_dve)
                v.tensor_tensor(halves(pre[:, PRE:PRE + TOK]), ps[:, :, 0:HALF], Rh, ALU.mult).then_inc(*post_dve.did(g, "evac"))
                settle(post_dve)
                ch = i + (NF if kind == "up_val" else 0)
                past = {"qkv": par[:, COL["a_st"] + i:COL["a_st"] + i + 25:12], "b_x": par[:, COL["b_st"] + i:COL["b_st"] + i + 5:2],
                        }.get(kind, par[:, COL["f_st0"] + ch:COL["f_st0"] + ch + 85:84])
                v.tensor_copy(pre[:, PRE + S0 - taps + 1:PRE + S0], past).then_inc(*post_dve.did(g, "state"))
                for r, end in enumerate((PRE + PROMPT, PRE + TOK)):
                    if kind == "qkv":
                        to = tails[:, r, i:i + 25:12]
                    elif kind == "b_x":
                        to = tails[:, r, 36 + i:36 + i + 5:2]
                    else:
                        to = tail_f[:, r, :, ch]
                    q = v.tensor_copy(to, pre[:, end - taps + 1:end])
                q.then_inc(*post_dve.did(g, "tail"))
                acc = {"qkv": qkvT, "b_x": xbT}[kind][:, i, :] if kind in ("qkv", "b_x") else fg[:] if kind == "up_gate" else fv[:]
                wcol = {"qkv": [COL["a_w"] + 12 * j + i for j in range(4)], "b_x": [COL["b_w"] + 2 * j + i for j in range(4)]}.get(
                    kind, [COL["f_w"] + ch, COL["f_w"] + 44 + ch, COL["f_w2"] + ch])
                bias = {"b_x": col("b_b", i)}.get(kind, None if kind == "qkv" else col("f_b", ch))
                if kind == "up_val" and i:
                    v.wait_ge(*post_pool.at(g - 2, "lo"))
                off = PRE + 1 - taps
                settle(post_dve)
                w0 = par[:, wcol[0]:wcol[0] + 1]
                if bias is None:
                    v.tensor_scalar(acc, pre[:, off:off + TOK], w0, None, ALU.mult).then_inc(*post_dve.did(g, "tap0"))
                else:
                    v.tensor_scalar(acc, pre[:, off:off + TOK], w0, bias, ALU.mult, ALU.add).then_inc(*post_dve.did(g, "tap0"))
                for j in range(1, taps):
                    settle(post_dve)
                    v.scalar_tensor_tensor(acc, pre[:, off + j:off + j + TOK], par[:, wcol[j]:wcol[j] + 1], acc, ALU.mult,
                                           ALU.add).then_inc(*post_dve.did(g, f"tap{j}"))
                if kind == "up_val":
                    v.wait_ge(*post_act.at(g - 1, "silu"))
                    settle(post_dve)
                    v.tensor_tensor(fv[:], fg[:], fv[:], ALU.mult).then_inc(*post_dve.did(g, "prod"))

            def gv_(r):
                return gv[:, r, 0:TILES * HEADS]

            def gate_rows():
                g8 = gv8
                v.memset(gv8, 0.0).then_inc(*gate_dve.did(0, "clear"))
                v.wait_ge(*gate_pe.at(0, "turn"))
                settle(gate_dve)
                v.tensor_copy(g8[:, 0:32], C[:, 0:32]).then_inc(*gate_dve.did(0, "rows"))
                v.tensor_copy(g8[0:SAMPLE, 32:40], C[0:SAMPLE, 32:40]).then_inc(*gate_dve.did(0, "rows4"))
                settle(gate_dve)
                z = gv_(2).rearrange("p (c h) -> p c h", h=4)
                v.tensor_tensor(z, g8.rearrange("p (c h) -> p c h", h=8)[:, :, 4:8], over(small[:, 4:8], TILES), ALU.add)\
                    .then_inc(*gate_dve.did(0, "arg"))
                settle(gate_dve)
                v.tensor_scalar(gv_(3), gv_(2), 0.0, None, ALU.max).then_inc(*gate_dve.did(0, "pos"))
                v.scalar_tensor_tensor(gv_(4), gv_(2), -1.0, gv_(2), ALU.mult, ALU.max).then_inc(*gate_dve.did(0, "neg"))
                v.wait_ge(*gate_act.at(0, "ln"))
                settle(gate_dve)
                v.tensor_tensor(gv_(3), gv_(3), gv_(4), ALU.add).then_inc(*gate_dve.did(0, "g0"))
                settle(gate_dve)
                v.scalar_tensor_tensor(gv_(1).rearrange("p (c h) -> p c h", h=4), gv_(3).rearrange("p (c h) -> p c h", h=4), -1.0,
                                       over(small[:, 44:48], TILES), ALU.mult, ALU.mult).then_inc(*gate_dve.did(0, "g"))
                v.wait_ge(*gate_pe.at(0, "gc"))
                v.tensor_copy(gv_(2), DD[:, 0:TILES * HEADS]).then_inc(*gate_dve.did(0, "gc"))
                v.wait_ge(*gate_act.at(0, "egc"))
                v.tensor_tensor(gv_(4), gv_(0), gv_(3), ALU.mult).then_inc(*gate_dve.did(0, "be"))

            def rg_tmp(i):
                return tmp[:].rearrange("p a b -> p (a b)")[:, i * TOK:(i + 1) * TOK]

            def rg():
                v.tensor_scalar(small[:, 48:50], col("lam", 0, 2), -1.0, None, ALU.mult).then_inc(*rg_dve.did(0, "nlam"))
                v.scalar_tensor_tensor(small[:, 50:52], col("lam", 0, 2), -1.0, col("lam", 0, 2), ALU.mult, ALU.max).then_inc(*rg_dve.did(0, "abs"))
                v.wait_ge(*rg_act.at(0, "ln"))
                settle(rg_dve)
                v.scalar_tensor_tensor(small[:, 48:50], small[:, 48:50], 0.0, small[:, 50:52], ALU.max, ALU.add)\
                    .then_inc(*rg_dve.did(0, "sp"))
                settle(rg_dve)
                v.tensor_scalar(small[:, 52:54], small[:, 48:50], -8.0, None, ALU.mult).then_inc(*rg_dve.did(0, "c8"))
                v.tensor_scalar(small[:, 54:56], small[:, 48:50], 8.0, None, ALU.mult).then_inc(*rg_dve.did(0, "c8n"))
                for i in range(2):
                    v.wait_ge(*rg_act.at(4 + i, "th"))
                    settle(rg_dve)
                    v.tensor_tensor(rg_tmp(8), rg_tmp(4 + i), rg_tmp(4 + i), ALU.mult).then_inc(*rg_dve.did(1 + i, "a2"))
                    settle(rg_dve)
                    v.scalar_tensor_tensor(rg_tmp(6 + i), rg_tmp(8), 1.0, rg_tmp(6 + i), ALU.add, ALU.mult)\
                        .then_inc(*rg_dve.did(1 + i, "m2"))
                    v.tensor_tensor(rg_tmp(2 + i), rg_tmp(2 + i), xbT[:, i, :], ALU.mult).then_inc(*rg_dve.did(1 + i, "gx"))
                v.wait_ge(*rg_act.at(6, "mult"))
                for i in range(2):
                    v.memset(rg_tmp(i)[:, PROMPT:S0], 0.0).then_inc(*rg_dve.did(3 + i, "gap"))
                    settle(rg_dve)
                    v.tensor_tensor(rg_tmp(2 + i), rg_tmp(2 + i), rg_tmp(6 + i), ALU.mult).then_inc(*rg_dve.did(3 + i, "u"))
                    settle(rg_dve)
                    v.tensor_tensor_scan(rg_tmp(i)[:, 0:PROMPT], rg_tmp(4 + i)[:, 0:PROMPT], rg_tmp(2 + i)[:, 0:PROMPT], 0.0,
                                         ALU.mult, ALU.add).then_inc(*rg_dve.did(3 + i, "scan"))
                    v.tensor_tensor_scan(rg_tmp(i)[:, S0:TOK], rg_tmp(4 + i)[:, S0:TOK], rg_tmp(2 + i)[:, S0:TOK],
                                         col("b_h", i), ALU.mult, ALU.add).then_inc(*rg_dve.did(3 + i, "scan_s"))
                    settle(rg_dve)
                    v.tensor_copy(tails[:, 0, 42 + i:43 + i], rg_tmp(i)[:, PROMPT - 1:PROMPT])
                    v.tensor_copy(tails[:, 1, 42 + i:43 + i], rg_tmp(i)[:, TOK - 1:TOK]).then_inc(*rg_dve.did(3 + i, "ht"))
                    v.wait_ge(*post_act.at(G_OF[("b_gate", i)], "gelu"))
                    v.tensor_tensor(gateT[:, i, :], gateT[:, i, :], rg_tmp(i), ALU.mult).then_inc(*rg_dve.did(3 + i, "y"))

            def hg_prep():
                lb = small[:, 56:58]
                v.tensor_tensor(lb, col("lb", 0, 2), col("lb", 0, 2), ALU.subtract).then_inc(*hgp_dve.did(0, "e0"))
                v.wait_ge(*hgp_act.at(0, "e"))
                v.reciprocal(small[:, 58:60], lb).then_inc(*hgp_dve.did(0, "rec"))
                settle(hgp_dve)
                v.tensor_tensor(small[:, 58:60], small[:, 58:60], lb, ALU.mult).then_inc(*hgp_dve.did(0, "sm"))
                settle(hgp_dve)
                v.tensor_tensor(lb, small[:, 58:60], small[:, 58:60], ALU.subtract).then_inc(*hgp_dve.did(0, "lb"))
                settle(hgp_dve)
                v.tensor_scalar(small[:, 58:60], lb, -1.0, 1.0, ALU.mult, ALU.add).then_inc(*hgp_dve.did(0, "oml"))
                v.wait_ge(*rg_dve.at(2, "gx"))
                v.memset(hQ, 0.0).then_inc(*hgp_dve.did(0, "q"))
                v.memset(vpad[:], 0.0).then_inc(*hgp_dve.did(0, "v"))
                v.wait_ge(*rg_act.at(3, "cf"))
                settle(hgp_dve)
                for i in range(2):
                    q = v.tensor_scalar(ckT[:, i, :], ckT[:, i, :], small[:, 58 + i:59 + i], small[:, 56 + i:57 + i], ALU.mult, ALU.add)
                q.then_inc(*hgp_dve.did(1, "f"))
                v.wait_ge(*hgp_act.at(1, "lf"))
                v.tensor_scalar(ckT[:], ckT[:], -1.0, 1.0, ALU.mult, ALU.add).then_inc(*hgp_dve.did(1, "k"))
                for i in range(2):
                    for c in range(TILES):
                        n, t0 = tile_len(c), tile_at(c)
                        v.tensor_tensor_scan(cbT[:, i, t0:t0 + n], ones[:, 0:n], cbT[:, i, t0:t0 + n], 0.0, ALU.mult, ALU.add)\
                            .then_inc(*hgp_dve.did(1, f"b{i}_{c}"))

            def gdn(c, ph):
                n = tile_len(c)

                def T(i):
                    return heads(tmp[:, i, :])

                def D_(name):
                    return gdn_dve.did(c, name)

                g4 = slice(4 * c, 4 * c + 4)
                a, b, cc = heads(A), heads(B), heads(C)
                if ph == "rows":
                    v.wait_ge(*gdn_act.at(c, "sqk"))
                    v.reduce_sum(small[0:n, 8:12], heads(SQ[:, 0, 0:512])[0:n], AX_X).then_inc(*D_("ssq"))
                    v.reduce_sum(small[0:n, 12:16], heads(SQ[:, 1, 0:512])[0:n], AX_X).then_inc(*D_("ssk"))
                    v.wait_ge(*gdn_act.at(c, "rk"))
                    if c:
                        v.wait_ge(*gdn_pe.at(c - 1, "S"))
                    else:
                        v.wait_ge(*rg_dve.at(4, "y"))
                    v.tensor_tensor(T(0)[0:n], a[0:n], cols(small[0:n, 24:28], P), ALU.mult).then_inc(*D_("qn"))
                    v.tensor_tensor(T(1)[0:n], b[0:n], cols(small[0:n, 28:32], P), ALU.mult).then_inc(*D_("kn"))
                    v.tensor_tensor(T(4)[0:n], cc[0:n], cols(gv[0:n, 0, g4], P), ALU.mult).then_inc(*D_("vb"))
                elif ph == "gb":
                    v.wait_ge(*gdn_pe.at(c, "gb"))
                    for h in range(HEADS):
                        q = v.tensor_scalar(T(5)[0:n, h, 0:n], a[0:n, h, 0:n], gv[0:n, 2, 4 * c + h:4 * c + h + 1], 0.0,
                                            ALU.subtract, ALU.max)
                    q.then_inc(*D_("gd"))
                    v.tensor_tensor(small[0:n, 36:40], a[0:n, :, n - 1], gv[0:n, 2, g4], ALU.subtract).then_inc(*D_("klast"))
                elif ph == "kk":
                    v.wait_ge(*gdn_pe.at(c, "kk"))
                    v.wait_ge(*gdn_pool.at(c, "bP"))
                    v.tensor_tensor(T(0)[0:n, :, 0:n], b[0:n, :, 0:n], T(6)[0:n, :, 0:n], ALU.mult).then_inc(*D_("L"))
                    v.wait_ge(*gdn_pe.at(c, "qk"))
                    v.wait_ge(*gdn_pool.at(c, "kd"))
                    v.tensor_tensor(T(1)[0:n, :, 0:n], cc[0:n, :, 0:n], T(5)[0:n, :, 0:n], ALU.mult).then_inc(*D_("QK"))
                elif ph == "turn":
                    settle(gdn_dve)
                    v.tensor_tensor(T(2)[0:n, :, 0:n], T(0)[0:n, :, 0:n], over(lev0n[0:n, 0:n], HEADS), ALU.mult).then_inc(*D_("Xt"))
                    settle(gdn_dve)
                    v.tensor_tensor(T(2)[0:n, :, 0:n], over(ident[0:n, 0:n], HEADS), T(2)[0:n, :, 0:n], ALU.subtract)\
                        .then_inc(*D_("X"))
                    v.wait_ge(*gdn_act.at(c, "LT"))
                    v.tensor_tensor(T(5)[0:n, :, 0:n], T(10)[0:n, :, 0:n], over(lev[0:n, 0, 0:n], HEADS), ALU.mult).then_inc(*D_("Ut"))
                    settle(gdn_dve)
                    v.tensor_tensor(T(5)[0:n, :, 0:n], over(ident[0:n, 0:n], HEADS), T(5)[0:n, :, 0:n], ALU.subtract)\
                        .then_inc(*D_("U"))
                elif ph.startswith("level"):
                    l = int(ph[5:])
                    if l < levels_of(c) - 1:
                        v.wait_ge(*gdn_pe.at(c, f"X{l}"))
                        settle(gdn_dve)
                        v.wait_ge(*gdn_pe.at(c, f"U{l}"))
                        v.scalar_tensor_tensor(T(2)[0:n, :, 0:n], b[0:n, :, 0:n], -1.0, T(2)[0:n, :, 0:n], ALU.mult, ALU.add)\
                            .then_inc(*D_(f"X{l}"))
                    v.wait_ge(*gdn_pe.at(c, f"U{l}"))
                    v.scalar_tensor_tensor(T(5)[0:n, :, 0:n], cc[0:n, :, 0:n], -1.0, T(5)[0:n, :, 0:n], ALU.mult, ALU.add)\
                        .then_inc(*D_(f"U{l}"))
                elif ph == "ks":
                    v.wait_ge(*gdn_pe.at(c, "ks"))
                    settle(gdn_dve)
                    v.tensor_tensor(T(6)[0:n], a[0:n], cols(gv[0:n, 4, g4], P), ALU.mult).then_inc(*D_("r1"))
                    settle(gdn_dve)
                    v.tensor_tensor(T(6)[0:n], T(4)[0:n], T(6)[0:n], ALU.subtract).then_inc(*D_("r"))
                elif ph == "o":
                    S = Sa[:, 1 if c == TILES - 1 else 0, :]
                    v.wait_ge(*gdn_pool.at(c, "Sgl"))
                    v.wait_ge(*gdn_pe.at(c, "S"))
                    v.tensor_tensor(S, S, A, ALU.add).then_inc(*D_("S"))

            def hg(c, ph):
                n, t0 = tile_len(c), tile_at(c)
                d4 = DD.rearrange("p (a b i) -> p a b i", a=2, b=2)
                aq = att.rearrange("p a b i -> p (a b) i")[0:n, :, 0:n]
                dq = heads(DD)[0:n, :, 0:n]
                D_ = lambda name: hg_dve.did(c, name)
                if ph == "level0":
                    if c:
                        v.wait_ge(*hg_pe.at(c - 1, "S"))
                    else:
                        v.wait_ge(*hgp_dve.at(1, f"b1_{TILES - 1}"))
                        v.wait_ge(const_ready, CONSTS)
                        v.wait_ge(*post_act.at(G_OF[("c_q", 1)], "silu"))
                    for par_ in range(2):
                        r = slice(64 * par_, 64 * par_ + 64)
                        q = v.tensor_copy(hQ[r, :, par_, 0:n], cqT[r, :, t0:t0 + n])
                    q.then_inc(*D_("q0"))
                    v.wait_ge(*hg_pe.at(c, "A0"))
                    v.tensor_tensor(aq, dq, over(ident[0:n, 0:n], HEADS), ALU.mult).then_inc(*D_("att0"))
                elif ph.startswith("level"):
                    l = int(ph[5:])
                    s = 1 << (l - 1)

                    def parts(ap):
                        return ap.rearrange("p i (b h r) -> p i b h r", h=2, r=s)

                    bb = parts(cbT[:, :, t0:t0 + n])
                    ref = bb[:, :, :, 0, s - 1:s]
                    ref = ref.to_broadcast([P, 2, n // (2 * s), s])
                    E = parts(hE[:, :, 0:n])
                    if l > 1:
                        v.wait_ge(*hg_pool.at(c, f"k{l - 1}"))
                    elif c:
                        v.wait_ge(*hg_pe.at(c - 1, "S"))
                    settle(hg_dve)
                    v.tensor_tensor(E[:, :, :, 0, :], ref, bb[:, :, :, 0, :], ALU.subtract).then_inc(*D_(f"dk{l}"))
                    v.tensor_tensor(E[:, :, :, 1, :], bb[:, :, :, 1, :], ref, ALU.subtract).then_inc(*D_(f"dq{l}"))
                    v.wait_ge(*hg_act.at(c, f"E{l}"))
                    v.wait_ge(*hg_pe.at(c, f"A{l - 1}"))
                    for par_, nm in enumerate(("qa", "qb")):
                        r = slice(64 * par_, 64 * par_ + 64)
                        dst = hQ[r, :, par_, 0:n].rearrange("p i (b h r) -> p i b h r", h=2, r=s)[:, :, :, 1, :]
                        src = cqT[r, :, t0:t0 + n].rearrange("p i (b h r) -> p i b h r", h=2, r=s)[:, :, :, 1, :]
                        v.tensor_tensor(dst, src, E[r, :, :, 1, :], ALU.mult).then_inc(*D_(f"{nm}{l}"))
                    v.wait_ge(*hg_pe.at(c, f"A{l}"))
                    v.copy_predicated(aq, over(lev[0:n, l - 1, 0:n].bitcast(U32), HEADS), dq).then_inc(*D_(f"att{l}"))
                elif ph == "o":
                    v.wait_ge(*hg_act.at(c, "o"))
                    Sx = Sc[:, 1 if c == TILES - 1 else 0]
                    for i in range(2):
                        for par_ in range(2):
                            r = slice(64 * par_, 64 * par_ + 64)
                            v.scalar_tensor_tensor(Sx[r, i, r], Sx[r, i, r], small[r, 60 + i:61 + i], d4[r, 1, i, r], ALU.mult,
                                                   ALU.add).then_inc(*D_(f"S{par_}{i}"))

            def mixed(j):
                return qkvT[:, j, :] if j < 4 else gateT[:, j - 4, :] if j < 6 else cqT[:, j - 6, :]

            def mix_out():
                for i in range(6):
                    o = mixed(i if i < 4 else i + 2)
                    zz = zT[:, i, :] if i < 4 else cgT[:, i - 4, :]
                    v.wait_ge(*mo_act.at(1 + i, "exp"))
                    v.scalar_tensor_tensor(o, o, col("a_norm" if i < 4 else "c_norm"), rg_tmp(i), ALU.mult, ALU.mult)\
                        .then_inc(*mo_dve.did(i, "on"))
                    settle(mo_dve)
                    v.tensor_tensor(o, o, zz, ALU.mult).then_inc(*mo_dve.did(i, "oz"))
                for j in range(8):
                    v.wait_ge(*mo_act.at(7 + j, "hi"))
                    v.tensor_tensor(XL[:, j, :], mixed(j), XH[:, j, :].bitcast(F32), ALU.subtract).then_inc(*mo_dve.did(6 + j, "lo"))

            def mem():
                for k in range(KC):
                    v.wait_ge(*mem_act.at(1 + k, "hi"))
                    v.scalar_tensor_tensor(memL[:, k, :], pm[:, 2 + k % 2, 0:N_MEM], col("mem", k), memH[:, k, :].bitcast(F32),
                                           ALU.mult, ALU.subtract).then_inc(*mem_dve.did(k, "lo"))

            def attention(c):
                n = tile_len(c)
                s = pm[0:n, 0:2, :].rearrange("p b (h m) -> p (b h) m", m=N_MEM)
                v.wait_ge(*at_pe.at(c, "s"))
                st = astat[0:n, c, :]
                v.reduce_max(st[:, 0:4], s, AX_X).then_inc(*at_dve.did(c, "max"))
                settle(at_dve)
                v.tensor_scalar(st[:, 4:8], st[:, 0:4], -1.0 / 16, None, ALU.mult).then_inc(*at_dve.did(c, "nmax"))
                v.wait_ge(*at_act.at(c, "exp3"))
                v.reciprocal(st[:, 0:4], st[:, 8:12]).then_inc(*at_dve.did(c, "rec"))
                settle(at_dve)
                v.tensor_tensor(prob[0:n], prob[0:n], cols(st[:, 0:4], N_MEM), ALU.mult).then_inc(*at_dve.did(c, "norm"))

            def pv():
                for j in range(8):
                    b = 2 * (j % 2)
                    v.wait_ge(*pv_act.at(j, "hi"))
                    v.tensor_tensor(XL[:, j, 0:PROMPT], pm[:, b, 0:PROMPT], XH[:, j, 0:PROMPT].bitcast(F32), ALU.subtract)\
                        .then_inc(*pv_dve.did(j, "lo"))
                    v.wait_ge(*pv_act.at(j, "his"))
                    v.tensor_tensor(XL[:, j, S0:TOK], pm[:, b + 1, 0:SAMPLE], XH[:, j, S0:TOK].bitcast(F32), ALU.subtract)\
                        .then_inc(*pv_dve.did(j, "los"))

            def finish():
                v.wait_ge(*fin_pe.at(0, "st"))
                v.wait_ge(slot_done, len(SLOTS))
                v.tensor_copy(frows[0:88], B[0:88, 0:256].rearrange("p (r n) -> p r n", r=2)).then_inc(*fin_dve.did(0, "st"))

            for what, *args in SCHED:
                if what == "finish":
                    finish()
                elif what == "start":
                    start()
                elif what == "product":
                    post(*args)
                elif what == "square":
                    square(*args)
                elif what == "split":
                    split(*args)
                elif what == "gate_rows":
                    gate_rows()
                elif what == "rg":
                    rg()
                elif what == "hg_prep":
                    hg_prep()
                elif what == "gdn":
                    gdn(*args)
                elif what == "hg":
                    hg(*args)
                elif what == "mix_out":
                    mix_out()
                elif what == "mem":
                    mem()
                elif what == "att":
                    attention(*args)
                elif what == "pv":
                    pv()

        @block.scalar
        def _(act):
            def f(out, in_, fn, **kw):
                return act.activation(out, in_, fn, **kw)

            done_slots = [0]

            def split_weights(last):
                while done_slots[0] <= min(last, len(SLOTS) - 1):
                    n = done_slots[0]
                    size = P * SLOT_K["down"][SLOTS[n][1]] if OUTS[SLOTS[n][0]][0] == "down" else KC * P
                    act.wait_ge(w_loaded[n % RAW], 16 * (n // RAW + 1))
                    if n >= HL:
                        act.wait_ge(slot_done, n - HL + 1)
                    f(WH[:, n % HL, 0:size], raw[:, n % RAW, 0:size], ACT.Copy).then_inc(w_high, 1)
                    done_slots[0] += 1

            def start():
                for t, r0, src in PARAMS:
                    act.dma_start(par_nat[r0:r0 + src.shape[0], t, :], src).then_inc(par_loaded, 16)
                for h in range(2):
                    act.dma_start(par_nat[109:110, 0, 64 * h:64 * h + 64], c_norm).then_inc(par_loaded, 16)
                act.dma_start(row8[:, 0:4], a_A_log).then_inc(par_loaded, 16)
                act.dma_start(row8[:, 4:8], a_dt_bias).then_inc(par_loaded, 16)
                split_weights(1)

            def square(s, k):
                if s == 0:
                    act.wait_ge(*start_dve.at(0, f"x{k}"))
                    act.wait_ge(const_ready, CONSTS)
                else:
                    act.wait_ge(*post_dve.at((G_WOUT, G_WO, G_DOWN)[s - 1] + k, "evac"))
                if k == 0:
                    if s:
                        act.wait_ge(*norm_pe.at(s - 1, "ss"))
                    f(NS[:], xT[:, k, :], ACT.Square).then_inc(*feed_act.did(s, f"sq{k}"))
                else:
                    if k >= 2:
                        act.wait_ge(*feed_dve.at(s, f"ns{k - 1}" if k == 2 else f"ns{k - 2}"))
                    f(SQ[:, k % 2, :], xT[:, k, :], ACT.Square).then_inc(*feed_act.did(s, f"sq{k}"))

            def split(s, k):
                if k == 0:
                    if s == 1:
                        act.wait_ge(slot_done, LAST_SLOT[G_WK - 1] + 1)
                    if s == 2:
                        act.wait_ge(slot_done, LAST_SLOT[G_UP - 1] + 1)
                        act.wait_ge(stored, 16 * (MIX_STORES + 2))
                f(XH[:, k, :], xT[:, k, :], ACT.Identity, scale=col(("mix", "attn", "ffn")[s], k)).then_inc(*feed_act.did(s, f"hi{k}"))

            def norm(s):
                act.wait_ge(*norm_pe.at(s, "ss"))
                if s:
                    act.wait_ge(*post_dve.at((0, G_WOUT, G_WO)[s] - 1, "evac"))
                f(R[:].rearrange("p (h t) -> p h t", h=2), pm[:, 0:2, 0:HALF], ACT.Ln, bias=EPS, scale=1.0 / D).then_inc(*norm_act.did(s, "ln"))
                act.wait_ge(*norm_act.at(s, "ln"))
                f(R[:], R[:], ACT.Exp, scale=-0.5).then_inc(*norm_act.did(s, "exp"))

            def post(g):
                kind, i = OUTS[g]
                split_weights(LAST_SLOT[g] + HL)
                if kind == "qkv":
                    act.wait_ge(*post_dve.at(g, "tap3"))
                    f(qkvT[:, i, :], qkvT[:, i, :], ACT.Silu).then_inc(*post_act.did(g, "silu"))
                if kind == "c_q":
                    act.wait_ge(*post_dve.at(g, "evac"))
                    f(cqT[:, i, :], cqT[:, i, :], ACT.Silu).then_inc(*post_act.did(g, "silu"))
                if kind == "b_gate":
                    act.wait_ge(*post_dve.at(g, "evac"))
                    f(gateT[:, i, :], gateT[:, i, :], ACT.Gelu_apprx_tanh).then_inc(*post_act.did(g, "gelu"))
                if kind == "up_gate":
                    act.wait_ge(*post_dve.at(g, "tap2"))
                    f(fg[:], fg[:], ACT.Silu).then_inc(*post_act.did(g, "silu"))
                if kind == "up_val":
                    act.wait_ge(*post_dve.at(g, "prod"))
                    f(FH[:, i, :], fv[:], ACT.Copy).then_inc(*post_act.did(g, "hi"))

            def gv_(r):
                return gv[:, r, 0:TILES * HEADS]

            def gate_rows():
                act.wait_ge(*gate_dve.at(0, "rows4"))
                f(gv_(0).rearrange("p (c h) -> p c h", h=4), gv8.rearrange("p (c h) -> p c h", h=8)[:, :, 0:4], ACT.Sigmoid)\
                    .then_inc(*gate_act.did(0, "beta"))
                act.wait_ge(*start_dve.at(0, "pad"))
                f(small[:, 44:48], small[:, 0:4], ACT.Exp).then_inc(*gate_act.did(0, "eA"))
                act.wait_ge(*gate_dve.at(0, "neg"))
                f(gv_(4), gv_(4), ACT.Exp, scale=-1.0).then_inc(*gate_act.did(0, "exp"))
                act.wait_ge(*gate_act.at(0, "exp"))
                f(gv_(4), gv_(4), ACT.Ln, bias=1.0).then_inc(*gate_act.did(0, "ln"))
                act.wait_ge(*gate_dve.at(0, "gc"))
                f(gv_(3), gv_(2), ACT.Exp).then_inc(*gate_act.did(0, "egc"))

            def rg_tmp(i, n=1):
                return tmp[:].rearrange("p a b -> p (a b)")[:, i * TOK:(i + n) * TOK]

            def rg():
                act.wait_ge(*rg_dve.at(0, "abs"))
                f(small[:, 50:52], small[:, 50:52], ACT.Exp, scale=-1.0).then_inc(*rg_act.did(0, "exp"))
                act.wait_ge(*rg_act.at(0, "exp"))
                f(small[:, 50:52], small[:, 50:52], ACT.Ln, bias=1.0).then_inc(*rg_act.did(0, "ln"))
                for i in range(2):
                    act.wait_ge(*rg_pe.at(i, "gates"))
                    f(rg_tmp(i).rearrange("p (h t) -> p h t", h=2), pm[:, 0:2, 0:HALF], ACT.Sigmoid, bias=col("b_r", i)).then_inc(*rg_act.did(1 + i, "r"))
                    f(rg_tmp(2 + i).rearrange("p (h t) -> p h t", h=2), pm[:, 2:4, 0:HALF], ACT.Sigmoid, bias=col("b_i", i)).then_inc(*rg_act.did(1 + i, "i"))
                act.wait_ge(*post_dve.at(G_OF[("c_f", 1)], "evac"))
                f(ckT[:], ckT[:], ACT.Sigmoid).then_inc(*rg_act.did(3, "cf"))
                act.wait_ge(*rg_dve.at(0, "c8n"))
                act.wait_ge(*rg_act.at(2, "i"))
                for i in range(2):
                    f(rg_tmp(4 + i), rg_tmp(i), ACT.Exp, scale=small[:, 52 + i:53 + i]).then_inc(*rg_act.did(4 + i, "a"))
                    f(rg_tmp(6 + i), rg_tmp(i), ACT.Tanh, scale=small[:, 54 + i:55 + i]).then_inc(*rg_act.did(4 + i, "th"))
                act.wait_ge(*rg_dve.at(2, "m2"))
                f(rg_tmp(6, 2), rg_tmp(6, 2), ACT.Sqrt).then_inc(*rg_act.did(6, "mult"))

            def hg_prep():
                act.wait_ge(*hgp_dve.at(0, "e0"))
                f(small[:, 56:58], small[:, 56:58], ACT.Exp).then_inc(*hgp_act.did(0, "e"))
                act.wait_ge(*hgp_dve.at(1, "f"))
                f(cbT[:], ckT[:], ACT.Ln).then_inc(*hgp_act.did(1, "lf"))

            def gdn(c, ph):
                n, t0 = tile_len(c), tile_at(c)

                def T(i):
                    return heads(tmp[:, i, :])

                def D_(name):
                    return gdn_act.did(c, name)

                a, b, cc = heads(A), heads(B), heads(C)
                if ph == "rows":
                    act.wait_ge(*gdn_pe.at(c, "rows"))
                    if c:
                        act.wait_ge(*gdn_pe.at(c - 1, "gb"))
                        act.wait_ge(*gdn_dve.at(c - 1, "S"))
                    f(heads(SQ[:, 0, 0:512])[0:n], a[0:n], ACT.Square).then_inc(*D_("sqq"))
                    f(heads(SQ[:, 1, 0:512])[0:n], b[0:n], ACT.Square).then_inc(*D_("sqk"))
                    act.wait_ge(*gdn_dve.at(c, "ssk"))
                    f(small[0:n, 16:24], small[0:n, 8:16], ACT.Ln, bias=EPS).then_inc(*D_("ln"))
                    act.wait_ge(*gdn_act.at(c, "ln"))
                    f(small[0:n, 24:28], small[0:n, 16:20], ACT.Exp, scale=-0.5, bias=LN_SCALE).then_inc(*D_("rq"))
                    f(small[0:n, 28:32], small[0:n, 20:24], ACT.Exp, scale=-0.5).then_inc(*D_("rk"))
                elif ph == "gb":
                    act.wait_ge(*gdn_pe.at(c, "gb"))
                    act.wait_ge(*gdn_dve.at(c, "klast"))
                    f(small[:, 32:36], a[:, :, n - 1], ACT.Exp).then_inc(*D_("gl"))
                    f(small[0:n, 40:44], small[0:n, 36:40], ACT.Exp).then_inc(*D_("kds"))
                    f(T(5)[0:n, :, 0:n], T(5)[0:n, :, 0:n], ACT.Exp, scale=-1.0).then_inc(*D_("G"))
                elif ph == "back":
                    act.wait_ge(*gdn_pe.at(c, "back"))
                    f(T(7)[:, :, 0:n], b[:, :, 0:n], ACT.Copy).then_inc(*D_("qnT"))
                    f(T(8)[:, :, 0:n], cc[:, :, 0:n], ACT.Copy).then_inc(*D_("knT"))
                    f(T(9)[:, :, 0:n], a[:, :, 0:n], ACT.Copy).then_inc(*D_("qdT"))
                elif ph == "turn":
                    act.wait_ge(*gdn_pe.at(c, "turnL"))
                    f(T(10)[0:n, :, 0:n], a[0:n, :, 0:n], ACT.Copy).then_inc(*D_("LT"))
                    act.wait_ge(*gdn_pe.at(c, "turnQ"))
                    f(T(11)[0:n, :, 0:n], b[0:n, :, 0:n], ACT.Copy).then_inc(*D_("QKT"))
                elif ph.startswith("level"):
                    l = int(ph[5:])
                    act.wait_ge(*gdn_pe.at(c, f"T{l}"))
                    act.wait_ge(*gdn_dve.at(c, "Xt"))
                    f(T(0)[0:n, :, 0:n], a[0:n, :, 0:n], ACT.Copy).then_inc(*D_(f"T{l}"))
                elif ph == "vnew":
                    act.wait_ge(*gdn_pe.at(c, "vnew"))
                    f(T(7)[0:n], b[0:n], ACT.Copy).then_inc(*D_("vn"))
                elif ph == "o":
                    act.wait_ge(*gdn_pe.at(c, "o"))
                    f(qkvT[:, 0:4, t0:t0 + n], cc[:, :, 0:n], ACT.Copy).then_inc(*D_("o"))
                    if c >= TILES - 2:
                        r, to = (0, pa_S) if c == TILES - 2 else (1, sa_S)
                        act.wait_ge(*gdn_dve.at(c, "S"))
                        act.dma_start(to[0, 0].rearrange("h k v -> k h v"), heads(Sa[:, r, :])).then_inc(stored, 16)

            def hg(c, ph):
                n, t0 = tile_len(c), tile_at(c)
                D_ = lambda name: hg_act.did(c, name)
                d4 = DD.rearrange("p (a b i) -> p a b i", a=2, b=2)
                d2 = DD[:, 0:256].rearrange("p (a i) -> p a i", a=2)
                if ph == "v":
                    act.wait_ge(*hg_pe.at(c, "v"))
                    act.wait_ge(const_ready, CONSTS)
                    f(vpad[0:n, :, 0, 0:64], d2[0:n, :, 0:64], ACT.Copy).then_inc(*D_("v0"))
                    f(vpad[0:n, :, 1, 64:128], d2[0:n, :, 64:128], ACT.Copy).then_inc(*D_("v1"))
                elif ph.startswith("level") and ph != "level0":
                    l = int(ph[5:])
                    act.wait_ge(*hg_dve.at(c, f"dq{l}"))
                    f(hE[:, :, 0:n], hE[:, :, 0:n], ACT.Exp).then_inc(*D_(f"E{l}"))
                elif ph == "kd":
                    act.wait_ge(*hg_pool.at(c, f"k{levels_of(c)}"))
                    act.wait_ge(*hg_dve.at(c, f"qb{levels_of(c)}"))
                    for i in range(2):
                        f(hE[:, i, 0:n], cbT[:, i, t0:t0 + n], ACT.Exp, scale=-1.0, bias=cbT[:, i, t0 + n - 1:t0 + n]).then_inc(*D_(f"ek{i}"))
                    act.wait_ge(*hg_pe.at(c, "kd"))
                    f(kdt[0:n], d2[0:n], ACT.Copy).then_inc(*D_("kdt"))
                    f(hE[:, :, 0:n], cbT[:, :, t0:t0 + n], ACT.Exp).then_inc(*D_("eq"))
                    f(small[:, 60:62], cbT[:, :, t0 + n - 1], ACT.Exp).then_inc(*D_("eb"))
                elif ph == "o":
                    act.wait_ge(*hg_pe.at(c, "o"))
                    act.wait_ge(*hg_pe.at(c, "S"))
                    f(cqT[:, :, t0:t0 + n], d4[:, 0, :, 0:n], ACT.Copy).then_inc(*D_("o"))
                    if c >= TILES - 2:
                        r, to = (0, pc_S) if c == TILES - 2 else (1, sc_S)
                        act.wait_ge(*hg_dve.at(c, "S11"))
                        for par_ in range(2):
                            s = slice(64 * par_, 64 * par_ + 64)
                            act.dma_start(to[0, 0].rearrange("(i q) k v -> q k i v", q=2)[par_], Sc[s, r, :, s]).then_inc(stored, 16)

            def mixed(j):
                return qkvT[:, j, :] if j < 4 else gateT[:, j - 4, :] if j < 6 else cqT[:, j - 6, :]

            def mix_out():
                act.wait_ge(*post_dve.at(G_LAST_IN, "evac"))
                f(zT[:], zT[:], ACT.Silu).then_inc(*mo_act.did(0, "siluz"))
                f(cgT[:], cgT[:], ACT.Silu).then_inc(*mo_act.did(0, "silug"))
                act.wait_ge(*gdn_act.at(TILES - 1, "o"))
                act.wait_ge(*hg_act.at(TILES - 1, "o"))
                act.wait_ge(*gdn_pe.at(TILES - 1, "S"))
                act.wait_ge(*gdn_dve.at(TILES - 1, "S"))
                for i in range(6):
                    if i >= 2:
                        act.wait_ge(*mo_pe.at(i - 2, "ss"))
                    f(SQ[:, i % 2, :], mixed(i if i < 4 else i + 2), ACT.Square).then_inc(*mo_act.did(1 + i, "sq"))
                    act.wait_ge(*mo_pe.at(i, "ss"))
                    f(rg_tmp(i).rearrange("p (h t) -> p h t", h=2), pm[:, 2 * (i % 2):2 * (i % 2) + 2, 0:HALF], ACT.Ln, bias=EPS,
                      scale=1.0 / (P if i < 4 else 64)).then_inc(*mo_act.did(1 + i, "ln"))
                    act.wait_ge(*mo_act.at(1 + i, "ln"))
                    f(rg_tmp(i), rg_tmp(i), ACT.Exp, scale=-0.5).then_inc(*mo_act.did(1 + i, "exp"))
                act.wait_ge(slot_done, LAST_SLOT[G_LAST_IN] + 1)
                for j in range(8):
                    if j < 4:
                        act.wait_ge(*mo_dve.at(j, "oz"))
                    elif j < 6:
                        act.wait_ge(*rg_dve.at(j - 1, "y"))
                    else:
                        act.wait_ge(*mo_dve.at(j - 2, "oz"))
                    f(XH[:, j, :], mixed(j), ACT.Copy).then_inc(*mo_act.did(7 + j, "hi"))
                act.wait_ge(*mo_pe.at(6, "st"))
                act.wait_ge(*mo_dve.at(5, "oz"))
                rows = st_rows[0:44, 0:256].rearrange("p (r n) -> p r n", r=2)
                f(rows, pm[0:44, 0:2, 0:P], ACT.Copy).then_inc(*mo_act.did(15, "st"))
                act.wait_ge(*mo_act.at(15, "st"))
                for r, (ta, tb, th) in enumerate(((pa_conv, pb_conv, pb_h), (sa_conv, sb_conv, sb_h))):
                    act.dma_start(ta[0, 0].rearrange("t (i p) -> (t i) p", p=P), rows[0:36, r, :]).then_inc(stored, 16)
                    act.dma_start(tb[0, 0].rearrange("t (i p) -> (t i) p", p=P), rows[36:42, r, :]).then_inc(stored, 16)
                    act.dma_start(th[0, 0].rearrange("(i p) -> i p", p=P), rows[42:44, r, :]).then_inc(stored, 16)

            def mem():
                act.wait_ge(mem_loaded, 16)
                act.wait_ge(stored, 16 * MIX_STORES)
                act.wait_ge(*mo_dve.at(13, "lo"))
                for t in range(2):
                    f(Kn[:, t, :], nat[:, t, :], ACT.Square, accum_out=mstat[:, t:t + 1]).then_inc(*mem_act.did(0, f"sq{t}"))
                act.wait_ge(*mem_act.at(0, "sq1"))
                f(mstat[:, 2:4], mstat[:, 0:2], ACT.Ln, bias=EPS, scale=1.0 / D).then_inc(*mem_act.did(0, "ln"))
                act.wait_ge(*mem_act.at(0, "ln"))
                f(mstat[:, 4:6], mstat[:, 2:4], ACT.Exp, scale=-0.5).then_inc(*mem_act.did(0, "exp"))
                for k in range(KC):
                    act.wait_ge(*mem_pe.at(k, "t"))
                    f(memH[:, k, :], pm[:, 2 + k % 2, 0:N_MEM], ACT.Identity, scale=col("mem", k)).then_inc(*mem_act.did(1 + k, "hi"))

            def kt():
                act.wait_ge(*post_dve.at(G_OF[("w_v", 3)], "evac"))
                act.dma_start(mem_k_out[0, 0].rearrange("(c p) h d -> p c (h d)", p=P), Kn[:]).then_inc(stored, 16)
                act.dma_start(mem_v_out[0, 0].rearrange("(c p) h d -> p c (h d)", p=P), Vn[:]).then_inc(stored, 16)
                for j in range(8):
                    act.wait_ge(*kt_pe.at(j, "t"))
                    d = 2 * (j % 4)
                    f(kT[:, j // 4, d:d + 2, :], pm[:, j % 4, :].rearrange("p (d m) -> p d m", d=2), ACT.Copy).then_inc(*kt_act.did(j, "t"))

            def attention(c):
                n = tile_len(c)
                act.wait_ge(*at_dve.at(c, "nmax"))
                if c:
                    act.wait_ge(*at_pe.at(c - 1, "t"))
                for h in range(HEADS):
                    f(prob[0:n, h, :], pm[0:n, h // 2, (h % 2) * 256:(h % 2 + 1) * 256], ACT.Exp, scale=1.0 / 16,
                      bias=astat[0:n, c, 4 + h:5 + h], accum_out=astat[0:n, c, 8 + h:9 + h]).then_inc(*at_act.did(c, f"exp{h}"))
                act.wait_ge(*at_pe.at(c, "t"))
                for t in range(2):
                    q = f(PT[:, t, :, c * P:c * P + n], heads(pm[:, 2 + t, :])[:, :, 0:n], ACT.Copy)
                q.then_inc(*at_act.did(c, "pt"))

            def pv():
                act.wait_ge(slot_done, LAST_SLOT[G_WO - 1] + 1)
                for j in range(8):
                    b = 2 * (j % 2)
                    act.wait_ge(*pv_pe.at(j, "o"))
                    f(XH[:, j, 0:PROMPT], pm[:, b, 0:PROMPT], ACT.Copy).then_inc(*pv_act.did(j, "hi"))
                    f(XH[:, j, S0:TOK], pm[:, b + 1, 0:SAMPLE], ACT.Copy).then_inc(*pv_act.did(j, "his"))

            def finish():
                act.wait_ge(*fin_pe.at(0, "ss"))
                act.wait_ge(slot_done, len(SLOTS))
                parts = [(slice(0, P), slice(0, 4)), (slice(0, SAMPLE), slice(4, 5))]
                sums = A[:, 0:2 * TILES].rearrange("p (c e) -> p c e", e=2)[:, :, 0]
                for p, c in parts:
                    q = f(fstat[p, c], sums[p, c], ACT.Ln, bias=EPS, scale=1.0 / D)
                q.then_inc(*fin_act.did(0, "ln"))
                act.wait_ge(*fin_act.at(0, "ln"))
                for p, c in parts:
                    q = f(fstat[p, c], fstat[p, c], ACT.Exp, scale=-0.5)
                q.then_inc(*fin_act.did(0, "exp"))
                act.wait_ge(*fin_dve.at(0, "st"))
                for r, to in enumerate((pf_conv, sf_conv)):
                    act.dma_start(to[0, 0].rearrange("t (c p) -> (t c) p", p=P), frows[0:88, r, :]).then_inc(stored, 16)
                act.wait_ge(*fin_act.at(0, "exp"))
                for c in range(TILES):
                    n = tile_len(c)
                    act.wait_ge(*fin_pe.at(1 + c, "y"))
                    f(yrow[0:n, c, :].rearrange("p (b n) -> p b n", b=2), pg[c % 2][0:n], ACT.Identity,
                      scale=fstat[0:n, c:c + 1]).then_inc(*fin_act.did(1 + c, "y"))
                    act.wait_ge(*fin_act.at(1 + c, "y"))
                    to = y_prompt[0, c * P:c * P + n, :] if c < TILES - 1 else y_sample[0]
                    act.dma_start(to, yrow[0:n, c, :]).then_inc(stored, 16)

            handlers = {"start": start, "square": square, "split": split, "norm": norm, "product": post,
                        "gate_rows": gate_rows, "rg": rg, "hg_prep": hg_prep, "gdn": gdn, "hg": hg, "mix_out": mix_out,
                        "mem": mem, "kt": kt, "att": attention, "pv": pv, "finish": finish}
            for what, *args in SCHED:
                handlers[what](*args)

        @block.gpsimd
        def _(pool):
            made = [0]

            def link(ins):
                ins.then_inc(const_ready, 1)
                made[0] += 1
                pool.wait_ge(const_ready, made[0])

            done_slots = [0]

            def split_weights(last):
                while done_slots[0] <= min(last, len(SLOTS) - 1):
                    n = done_slots[0]
                    size = P * SLOT_K["down"][SLOTS[n][1]] if OUTS[SLOTS[n][0]][0] == "down" else KC * P
                    pool.wait_ge(w_high, n + 1)
                    pool.tensor_tensor(WL[:, n % HL, 0:size], raw[:, n % RAW, 0:size], WH[:, n % HL, 0:size].bitcast(F32),
                                       ALU.subtract).then_inc(w_low, 1)
                    done_slots[0] += 1

            def select(ap, op, fill, base, pattern, cm):
                return pool.affine_select(out=ap, in_=ap, compare_op=op, fill=fill, base=base, pattern=pattern, channel_multiplier=cm)

            def start():
                link(pool.memset(ident[:], 0.0))
                link(select(ident[:], ALU.not_equal, 1.0, 0, [[-1, P]], 1))
                link(pool.memset(xT[:, :, PROMPT:S0], 0.0))
                link(pool.memset(ones[:], 1.0))
                link(pool.memset(half_ones[:], 0.0))
                link(pool.memset(half_ones[0:64, 0:64], 1.0))
                link(pool.memset(half_ones[64:128, 64:128], 1.0))
                link(pool.memset(upto_m[:], 1.0))
                link(select(upto_m[:], ALU.is_ge, 0.0, 0, [[1, P]], -1))
                link(pool.memset(lower[:], 1.0))
                link(select(lower[:], ALU.is_ge, 0.0, 0, [[-1, P]], 1))
                link(pool.memset(pre_m[:, :, 0:PRE], 0.0))
                link(pool.memset(wr_bd[:], 0.0))
                link(pool.memset(Sa[:, 0, :], 0.0))
                link(pool.memset(Sc[:], 0.0))
                link(pool.memset(hK[:], 0.0))
                link(pool.memset(lev[:], 0.0))
                link(pool.memset(lev0n[:], 0.0))
                odd = lev0n[:].rearrange("p (b h) -> p b h", h=2)[:, :, 0]
                link(pool.memset(odd, 1.0))
                link(select(odd, ALU.is_equal, 0.0, -1, [[-2, 64]], 1))
                for l in range(LEVELS):
                    s = 1 << l
                    w = lev[:, l, :].rearrange("p (b h r) -> p b h r", h=2, r=s)[:, :, 1, :]
                    nb = P // (2 * s)
                    link(pool.memset(w, 1.0))
                    link(select(w, ALU.is_ge, 0.0, 0, [[-2 * s, nb], [0, s]], 1))
                    link(select(w, ALU.is_ge, 0.0, s - 1, [[2 * s, nb], [0, s]], -1))
                assert made[0] == CONSTS, made[0]
                for q in range(2):
                    r = slice(64 * q, 64 * q + 64)
                    for gate, w in enumerate((b_w_r, b_w_i)):
                        pool.dma_start(wr_bd[r, gate, :, r], w[0].rearrange("(i q) a b -> q a i b", q=2)[q]).then_inc(state_loaded, 16)
                    pool.dma_start(Sc[r, 1, :, r], state_c_S[0, 0].rearrange("(i q) k v -> q k i v", q=2)[q]).then_inc(state_loaded, 16)
                pool.dma_start(heads(Sa[:, 1, :]), state_a_S[0, 0].rearrange("h k v -> k h v")).then_inc(state_loaded, 16)
                split_weights(1)

            def post(g):
                split_weights(LAST_SLOT[g] + HL)
                kind, i = OUTS[g]
                if kind == "up_val":
                    pool.wait_ge(*post_act.at(g, "hi"))
                    pool.tensor_tensor(FL[:, i, :], fv[:], FH[:, i, :].bitcast(F32), ALU.subtract).then_inc(*post_pool.did(g, "lo"))

            def gdn(c, ph):
                n = tile_len(c)
                g4 = slice(4 * c, 4 * c + 4)

                def T(i):
                    return heads(tmp[:, i, :])

                def D_(name):
                    return gdn_pool.did(c, name)

                if ph == "rows":
                    if c == 0:
                        pool.wait_ge(*gate_act.at(0, "egc"))
                    pool.wait_ge(*gdn_dve.at(c, "ssk"))
                    pool.tensor_tensor(heads(SQ[:, 1, 0:512])[0:n, :, 0:n], over(ident[0:n, 0:n], HEADS), cols(gv[0:n, 2, g4], n), ALU.mult)\
                        .then_inc(*D_("diag"))
                    pool.wait_ge(*gdn_dve.at(c, "qn"))
                    pool.tensor_tensor(T(2)[0:n], T(0)[0:n], cols(gv[0:n, 3, g4], P), ALU.mult).then_inc(*D_("qd"))
                elif ph == "gb":
                    pool.wait_ge(*gdn_act.at(c, "kds"))
                    pool.tensor_tensor(T(3)[0:n], T(1)[0:n], cols(small[0:n, 40:44], P), ALU.mult).then_inc(*D_("kd"))
                    pool.wait_ge(*gdn_act.at(c, "G"))
                    pool.tensor_tensor(T(5)[0:n, :, 0:n], T(5)[0:n, :, 0:n], over(lower[0:n, 0:n], HEADS), ALU.mult).then_inc(*D_("Pm"))
                    pool.wait_ge(*gdn_pool.at(c, "Pm"))
                    pool.tensor_tensor(T(6)[0:n, :, 0:n], T(5)[0:n, :, 0:n], cols(gv[0:n, 0, g4], n), ALU.mult).then_inc(*D_("bP"))
                elif ph.startswith("level"):
                    l = int(ph[5:])
                    pool.wait_ge(*gdn_act.at(c, "QKT"))
                    if l > 1:
                        pool.wait_ge(*gdn_pe.at(c, f"T{l - 1}"))
                    pool.tensor_tensor(T(1)[0:n, :, 0:n], T(10)[0:n, :, 0:n], over(lev[0:n, l, 0:n], HEADS), ALU.mult).then_inc(*D_(f"B{l}"))
                elif ph == "o":
                    pool.wait_ge(*gdn_pe.at(c, "o"))
                    S = heads(Sa[:, 1 if c == TILES - 1 else 0, :])
                    pool.tensor_tensor(S, S, cols(small[:, 32:36], P), ALU.mult).then_inc(*D_("Sgl"))

            def hg(c, ph):
                n, t0 = tile_len(c), tile_at(c)
                D_ = lambda name: hg_pool.did(c, name)
                if ph == "level0":
                    if c:
                        pool.wait_ge(*hg_pe.at(c - 1, "S"))
                    else:
                        pool.wait_ge(*hgp_dve.at(1, f"b1_{TILES - 1}"))
                    pool.tensor_scalar(hK[:, :, 0:n], ckT[:, :, t0:t0 + n], 1.0, 1.0, ALU.mult, ALU.mult).then_inc(*D_("k0"))
                elif ph.startswith("level"):
                    l = int(ph[5:])
                    s = 1 << (l - 1)

                    def first(ap):
                        return ap.rearrange("p i (b h r) -> p i b h r", h=2, r=s)[:, :, :, 0, :]

                    pool.wait_ge(*hg_act.at(c, f"E{l}"))
                    pool.wait_ge(*hg_pe.at(c, f"A{l - 1}"))
                    pool.tensor_tensor(first(hK[:, :, 0:n]), first(ckT[:, :, t0:t0 + n]), first(hE[:, :, 0:n]), ALU.mult).then_inc(*D_(f"k{l}"))
                elif ph == "kd":
                    pool.wait_ge(*hg_act.at(c, "ek1"))
                    pool.wait_ge(*hg_pe.at(c, f"A{levels_of(c)}"))
                    pool.tensor_tensor(hK[:, :, 0:n], ckT[:, :, t0:t0 + n], hE[:, :, 0:n], ALU.mult).then_inc(*D_("kd"))
                    pool.wait_ge(*hg_act.at(c, "eq"))
                    pool.tensor_tensor(hE[:, :, 0:n], cqT[:, :, t0:t0 + n], hE[:, :, 0:n], ALU.mult).then_inc(*D_("qe"))

            handlers = {"start": start, "product": post, "gdn": gdn, "hg": hg}
            for what, *args in SCHED:
                if what in handlers:
                    handlers[what](*args)


LN_SCALE = -2.4260151319598084


_INS = ['x_prompt', 'x_sample', 'cache_mem_k', 'cache_mem_v', 'state_a_conv', 'state_a_S', 'state_b_conv', 'state_b_h',
        'state_c_S', 'state_ffn_conv', 'mem_prompt', 'norm_mix', 'w_in', 'a_conv_w', 'a_A_log', 'a_dt_bias', 'a_norm',
        'b_conv_w', 'b_conv_b', 'b_w_r', 'b_b_r', 'b_w_i', 'b_b_i', 'b_lambda', 'c_lb_logits', 'c_norm', 'w_out',
        'norm_attn', 'norm_mem', 'w_q', 'w_k', 'w_v', 'w_o', 'norm_ffn', 'w_up', 'ffn_conv_w', 'ffn_conv_b', 'w_down',
        'norm_final']
_STATES = [(1, 1, 3, 1536), (1, 1, 4, 128, 128), (1, 1, 3, 256), (1, 1, 256), (1, 1, 4, 64, 64), (1, 1, 2, 5632)]
_OUTS = [(1, 512, 1024), (1, 64, 1024), (1, 1, 256, 4, 256), (1, 1, 256, 4, 256)] + _STATES + _STATES


def kernel(**inputs):
    import numpy as _np
    import concourse.bacc as _bacc
    from concourse import mybir as _mybir
    from concourse.bass_utils import run_bass_kernel_spmd as _run

    nc = _bacc.Bacc("TRN2", target_bir_lowering=False, num_devices=1)
    arrays, args = {}, []
    for name in _INS:
        a = _np.ascontiguousarray(inputs[name])
        arrays[f"in_{name}_dram"] = a
        args.append(nc.dram_tensor(f"in_{name}_dram", a.shape, _mybir.dt.from_np(a.dtype), kind="ExternalInput").ap())
    for i, shape in enumerate(_OUTS):
        args.append(nc.dram_tensor(f"out_{i}_dram", shape, _mybir.dt.float32, kind="ExternalOutput").ap())
    build(nc, *args)
    r = _run(nc, [arrays], core_ids=[0])
    return tuple(r.results[0][f"out_{i}_dram"] for i in range(len(_OUTS)))
```

```python
from contextlib import ExitStack

import concourse.bass as bass
from concourse import mybir

F32 = mybir.dt.float32
F32R = mybir.dt.float32r
U32 = mybir.dt.uint32
ALU = mybir.AluOpType
ACT = mybir.ActivationFunctionType
AX_X = mybir.AxisListType.X

P = 128
D = 1024
KC = D // P
PROMPT = 512
SAMPLE = 64
GAP = 4
TOK = PROMPT + GAP + SAMPLE
HALF = TOK // 2
S0 = PROMPT + GAP
PRE = 3
N_A, N_G, N_B, N_C = 512, 4, 256, 256
HEADS = 4
N_MEM = 256
D_FF = 2816
NF = D_FF // P
EPS = 1e-6
TILES = 5
LEVELS = 7


class Steps:

    def __init__(self, sem, rounds):
        self.sem, self.value, self.made = sem, {}, 0
        for r, names in rounds:
            for name in names:
                assert (r, name) not in self.value
                self.value[(r, name)] = len(self.value) + 1

    def at(self, r, name):
        return self.sem, self.value[(r, name)]

    def did(self, r, name):
        self.made += 1
        assert self.value[(r, name)] == self.made, (r, name)
        return self.sem, 1


def tile_len(c):
    return P if c < TILES - 1 else SAMPLE


def tile_at(c):
    return c * P if c < TILES - 1 else S0


def levels_of(c):
    return LEVELS if c < TILES - 1 else LEVELS - 1


COL = {"mix": 0, "attn": 8, "ffn": 16, "mem": 24, "final": 32, "a_w": 40, "b_w": 88, "b_b": 96, "b_r": 98, "b_i": 100,
       "lam": 102, "lb": 104, "b_h": 106, "a_norm": 108, "c_norm": 109,
       "a_st": 128, "b_st": 164, "f_b": 170, "f_w": 256, "f_w2": 384, "f_st0": 428, "f_st1": 512}
PAR_ROWS = [110, 86, 88, 88, 44]


def outputs_of_products():
    outs = [("gates", 0)]
    outs += [("qkv", i) for i in range(12)]
    for kind in ("c_q", "b_gate", "b_x", "c_f", "c_i"):
        outs += [(kind, i) for i in range(2)]
    outs += [("z", i) for i in range(4)] + [("c_g", i) for i in range(2)]
    outs += [("w_out", i) for i in range(8)]
    outs += [("w_k", i) for i in range(4)] + [("w_v", i) for i in range(4)]
    outs += [("w_q", i) for i in range(8)] + [("w_o", i) for i in range(8)]
    for f in range(NF):
        outs += [("up_gate", f), ("up_val", f)]
    outs += [("down", i) for i in range(8)]
    return outs


OUTS = outputs_of_products()
G_OF = {o: g for g, o in enumerate(OUTS)}
SLOT_K = {"down": [8, 8, 6], "w_k": [4, 4], "w_v": [4, 4]}
SLOTS = [(g, j) for g, (kind, i) in enumerate(OUTS) for j in range(len(SLOT_K.get(kind, [8])))]
FIRST_SLOT, LAST_SLOT = {}, {}
for _n, (_g, _j) in enumerate(SLOTS):
    FIRST_SLOT.setdefault(_g, _n)
    LAST_SLOT[_g] = _n
W_IN_COL = {"gates": 2048, "qkv": 0, "z": 1536, "b_x": 2056, "b_gate": 2312, "c_q": 2568, "c_f": 2824, "c_i": 3080,
            "c_g": 3336}
RAW, HL = 2, 2
CONV = {"qkv": 4, "b_x": 4, "up_gate": 3, "up_val": 3}


PAIR = {}
for _g, (_kind, _i) in enumerate(OUTS):
    PAIR[_g] = 0 if _kind in ("z", "c_g") else _g % 2
PREV = {g: max([x for x in range(g) if PAIR[x] == PAIR[g]], default=None) for g in PAIR}


def gdn_phases(c):
    out = ["rows", "decay", "mask", "L", "turn"]
    for l in range(1, levels_of(c)):
        out += [f"T{l}", f"X{l}"]
    return out + ["vnew", "o", "ss", "on"]


def hg_phases(c):
    out = ["v", "a0"]
    for l in range(1, levels_of(c) + 1):
        out += [f"b{l}", f"a{l}"]
    return out + ["kd", "kdt", "o", "ss", "on"]


def schedule():
    out = [("start",)] + [("split", 0, k) for k in range(KC)] + [("square", 0, k) for k in range(KC)]
    prod = list(range(len(OUTS)))

    def parts(g):
        return [("part", g, n, k) for n in range(FIRST_SLOT[g], LAST_SLOT[g] + 1)
                for k in range(SLOT_K.get(OUTS[g][0], [8])[n - FIRST_SLOT[g]])]

    def upto(kind, i):
        n = G_OF[(kind, i)] + 1
        part = [x for x in prod if x < n]
        del prod[:len(part)]
        return [y for g in part for y in parts(g) + [("post", g)]]

    def with_norm(s, kind):
        got = upto(kind, 0)
        return got[:-1] + [("norm", s), got[-1]]

    out += with_norm(0, "gates") + upto("qkv", 0) + [("gate_rows",)]
    for i in range(1, 12):
        got = upto("qkv", i)
        out += got[:-1] + [("l2", i - 3)] * (0 <= i - 3 < 8) + got[-1:] + [("l2sq", i - 1)] * (i - 1 < 8)
    out += upto("b_x", 0) + [("l2exp",)] + upto("b_x", 1) + upto("b_gate", 1)
    out += [("rg", 0)] + upto("c_q", 0) + [("rg", 1)] + upto("c_q", 1) + [("rg", 2)] + upto("c_f", 0) + [("rg", 3)] + upto("c_f", 1)
    out += upto("c_i", 1) + [("hg_prep",)]
    fill = upto("c_g", 1)
    seq = [(c, ph) for c in range(TILES) for ph in gdn_phases(c)]
    hg = [(c, ph) for c in range(TILES) for ph in hg_phases(c)]
    lag = 10
    out += [("gdn", 0, p, "diag") for p in range(2)]
    total, h, f = len(seq) + lag, 0, 0
    for i in range(total):
        for p, at in enumerate((i, i - lag)):
            if 0 <= at < len(seq):
                c, ph = seq[at]
                if ph == "o" and c:
                    out.append(("gdn", c - 1, p, "oz"))
                out.append(("gdn", c, p, ph))
                if ph == f"T{levels_of(c) - 1}" and c < TILES - 1:
                    out.append(("gdn", c + 1, p, "diag"))
                if at == len(seq) - 1:
                    out.append(("gdn", c, p, "oz"))
            for _ in range(FILL_RATE[p]):
                if f < len(fill):
                    out.append(fill[f])
                    f += 1
        while h < len(hg) and h * total < (i + 1) * len(hg):
            c, ph = hg[h]
            if ph == "o" and c:
                out.append(("hg", c - 1, "oz"))
            out.append(("hg", c, ph))
            h += 1
    out += [("hg", TILES - 1, "oz"), ("mix_out",)]
    for i in range(8):
        out += upto("w_out", i) + [("square", 1, i)]
    out += [("mem",)]
    for i in range(8):
        out += upto(("w_k", "w_v")[i // 4], i % 4) + [("split", 1, i)]
    out += [("norm", 1), ("kt",)]
    out += upto("w_q", 7)
    out += [("att", c) for c in range(TILES)]
    out += [("pv",)]
    for i in range(8):
        out += upto("w_o", i) + [("square", 2, i)]
    out += [("split", 2, i) for i in range(8)] + with_norm(2, "up_gate")
    out += upto("up_val", NF - 1)
    for i in range(8):
        out += upto("down", i) + [("square", 3, i)]
    out += [("finish",)]
    assert not prod
    return out


FILL_RATE = (1, 1)
LN_SCALE = -2.4260151319598084


def build(nc, x_prompt, x_sample, cache_mem_k, cache_mem_v, state_a_conv, state_a_S, state_b_conv, state_b_h, state_c_S,
          state_ffn_conv, mem_prompt, norm_mix, w_in, a_conv_w, a_A_log, a_dt_bias, a_norm, b_conv_w, b_conv_b, b_w_r,
          b_b_r, b_w_i, b_b_i, b_lambda, c_lb_logits, c_norm, w_out, norm_attn, norm_mem, w_q, w_k, w_v, w_o, norm_ffn,
          w_up, ffn_conv_w, ffn_conv_b, w_down, norm_final,
          y_prompt, y_sample, mem_k_out, mem_v_out, pa_conv, pa_S, pb_conv, pb_h, pc_S, pf_conv,
          sa_conv, sa_S, sb_conv, sb_h, sc_S, sf_conv):
    ctx = ExitStack()
    with ctx:
        def sb(name, shape, dt=F32, into=ctx):
            return into.enter_context(nc.sbuf_tensor("t_" + name, shape, dt))

        def sem(name):
            return ctx.enter_context(nc.semaphore(name))

        xT = sb("xT", [P, KC, TOK])
        XH = sb("XH", [P, KC, TOK], F32R)
        XL = sb("XL", [P, KC, TOK], F32R)
        raw = sb("raw", [P, RAW, KC * P])
        WH = sb("WH", [P, HL, KC * P], F32R)
        WL = sb("WL", [P, HL, KC * P], F32R)
        ident = sb("ident", [P, P])
        ones = sb("ones", [P, P])
        half_ones = sb("half_ones", [P, P])
        upto_m = sb("upto_m", [P, P])
        lev = sb("lev", [P, LEVELS, P])
        par = sb("par", [P, 556])
        NS = sb("NS", [P, TOK])
        R = sb("R", [P, TOK])
        SQ = sb("SQ", [P, 2, TOK])
        tails = sb("tails", [P, 2, 44])

        mix_ctx = ExitStack()
        qkvT = sb("qkvT", [P, 12, TOK], into=mix_ctx)
        zT = sb("zT", [P, 4, TOK], into=mix_ctx)
        xbT = sb("xbT", [P, 2, TOK], into=mix_ctx)
        gateT = sb("gateT", [P, 2, TOK], into=mix_ctx)
        cqT = sb("cqT", [P, 2, TOK], into=mix_ctx)
        ckT = sb("ckT", [P, 2, TOK], into=mix_ctx)
        cbT = sb("cbT", [P, 2, TOK], into=mix_ctx)
        cvT = sb("cvT", [P, 2, TOK], into=mix_ctx)
        cgT = sb("cgT", [P, 2, TOK], into=mix_ctx)
        pre_m = sb("pre_m", [P, 2, TOK + PRE], into=mix_ctx)
        NT = 12
        tmp = sb("tmp", [P, NT, 512], into=mix_ctx)
        Sa = sb("Sa", [P, 2, 512], into=mix_ctx)
        gT = sb("gT", [8, TOK], into=mix_ctx)
        gv = sb("gv", [P, 7, TILES * HEADS], into=mix_ctx)
        gv8 = gv[:, 5:7, :].rearrange("p a b -> p (a b)")
        hE = sb("hE", [P, 2, P], into=mix_ctx)
        hK = sb("hK", [P, 2, P], into=mix_ctx)
        kdt = sb("kdt", [P, 2, P], into=mix_ctx)
        Sc = sb("Sc", [P, 2, 2, P], into=mix_ctx)
        wr_bd = sb("wr_bd", [P, 2, 2, P], into=mix_ctx)
        small = sb("small", [P, 64], into=mix_ctx)
        row8 = sb("row8", [1, 8], into=mix_ctx)
        hQ, att = (xbT[:].rearrange("p a b -> p (a b)")[:, i * 512:(i + 1) * 512].rearrange("p (a b i) -> p a b i", a=2, b=2)
                   for i in range(2))
        vpad = wr_bd
        x_nat = qkvT[:].rearrange("p a b -> p (a b)")[:, 0:TILES * D].rearrange("p (c d) -> p c d", c=TILES)
        par_nat = cqT[:].rearrange("p a b -> p (a b)")[:, 0:640].rearrange("p (a b) -> p a b", a=5)
        st_rows = zT[:].rearrange("p a b -> p (a b)")
        mix_ctx.close()

        att_ctx = ExitStack()
        memH = sb("memH", [P, KC, N_MEM], F32R, into=att_ctx)
        memL = sb("memL", [P, KC, N_MEM], F32R, into=att_ctx)
        nat = sb("nat", [P, 2, D], into=att_ctx)
        Kn = sb("Kn", [P, 2, D], into=att_ctx)
        Vn = sb("Vn", [P, 2, D], into=att_ctx)
        sV = sb("sV", [P, 2, D], into=att_ctx)
        kT = sb("kT", [P, 2, KC, N_MEM], into=att_ctx)
        qT = sb("qT", [P, KC, TOK], into=att_ctx)
        PT = sb("PT", [P, 2, HEADS, PROMPT + SAMPLE], into=att_ctx)
        prob = sb("prob", [P, HEADS, N_MEM], into=att_ctx)
        mstat = sb("mstat", [P, 16], into=att_ctx)
        astat = sb("astat", [P, TILES, 12], into=att_ctx)
        att_ctx.close()

        ffn_ctx = ExitStack()
        FH = sb("FH", [P, NF, TOK], F32R, into=ffn_ctx)
        FL = sb("FL", [P, NF, TOK], F32R, into=ffn_ctx)
        pre_f = sb("pre_f", [P, 1, TOK + PRE], into=ffn_ctx)
        fg = sb("fg", [P, TOK], into=ffn_ctx)
        fv = sb("fv", [P, TOK], into=ffn_ctx)
        tail_f = sb("tail_f", [P, 2, 2, 44], into=ffn_ctx)
        ffn_ctx.close()
        fin_ctx = ExitStack()
        yrow = sb("yrow", [P, TILES, D], into=fin_ctx)
        fstat = sb("fstat", [P, 8], into=fin_ctx)
        frows = sb("frows", [P, 2, P], into=fin_ctx)
        fin_ctx.close()

        pg = [ctx.enter_context(nc.psum_tensor(f"pg{i}", [P, 2, 512], F32)) for i in range(2)]
        pm = ctx.enter_context(nc.psum_tensor("pm", [P, 4, 512], F32))
        A, B, C, DD = (pm[:, i, :] for i in range(4))

        PAIR_BANKS = ((pm[:, 0, :], pm[:, 1, :]), (pm[:, 2, :], pg[1][:, 1, :]))

        def half_of(bank, i):
            return bank[:, 256 * i:256 * i + 256].rearrange("p (h i) -> p h i", h=2)

        def level_banks(p, l):
            b = PAIR_BANKS[p]
            return (b[1], b[0]) if l % 2 else (b[0], b[1])

        def Tp(i, p):
            return heads(tmp[:, i, :])[:, 2 * p:2 * p + 2, :]

        def heads(ap):
            return ap.rearrange("p (h i) -> p h i", h=HEADS)

        def cols(v, n):
            return v.unsqueeze(2).to_broadcast([v.shape[0], v.shape[1], n])

        def over(m, h):
            return m.unsqueeze(1).to_broadcast([m.shape[0], h, m.shape[1]])

        def col(name, i=0, n=1):
            return par[:, COL[name] + i:COL[name] + i + n]

        const_ready = sem("const_ready")
        x_loaded = sem("x_loaded")
        par_loaded = sem("par_loaded")
        state_loaded = sem("state_loaded")
        mem_loaded = sem("mem_loaded")
        cache_loaded = sem("cache_loaded")
        cv_loaded = sem("cv_loaded")
        w_loaded = [sem(f"w_loaded{i}") for i in range(RAW)]
        stored = sem("stored")
        w_high = sem("w_high")
        w_low = sem("w_low")
        slot_done = sem("slot_done")

        SCHED = schedule()
        names = {
            "start_pe": [(0, ["par"] + [f"x{k}" for k in range(KC)] + ["row8"])],
            "start_dve": [(0, ["par"] + [f"x{k}" for k in range(KC)] + ["pad"])],
            "feed_act": [(0, [f"hi{k}" for k in range(KC)] + [f"sq{k}" for k in range(KC)])] + [
                (s, [f"sq{k}" for k in range(KC)] + [f"hi{k}" for k in range(KC) if s < 3]) for s in range(1, 4)],
            "feed_dve": [(0, [f"lo{k}" for k in range(KC)] + [f"ns{k}" for k in range(1, KC)])] + [
                (s, [f"ns{k}" for k in range(1, KC)] + [("lo" if s < 3 else "xw") + str(k) for k in range(KC)]) for s in range(1, 4)],
            "norm_pe": [(s, ["ss"]) for s in range(4)],
            "norm_act": [(s, ["ln", "exp"]) for s in range(3)],
        }
        order = {}
        for key, rounds in names.items():
            order[key] = Steps(sem(key), rounds)
        start_pe, start_dve, feed_act, feed_dve, norm_pe, norm_act = (order[k] for k in (
            "start_pe", "start_dve", "feed_act", "feed_dve", "norm_pe", "norm_act"))

        def post_dve_names(kind, i):
            taps = [f"tap{j}" for j in range(CONV.get(kind, 0))]
            return ((["zero"] if (kind, i) == ("up_gate", 0) else []) + ["evac"] + (["state", "tail"] if kind in CONV else []) + taps + (["prod"] if kind == "up_val" else []))

        post_dve = Steps(sem("post_dve"), [(g, post_dve_names(*OUTS[g])) for g in range(len(OUTS))])
        post_act = Steps(sem("post_act"), [(g, {"qkv": ["silu"], "c_q": ["silu"], "b_gate": ["gelu"], "up_gate": ["silu"],
                                                "up_val": ["hi"], "z": ["silu"], "c_g": ["silu"], "c_f": ["sig"]}.get(OUTS[g][0], [])) for g in range(len(OUTS))])
        post_pool = Steps(sem("post_pool"), [(G_OF[("up_val", f)], ["lo"]) for f in range(NF)])
        gate_pe = Steps(sem("gate_pe"), [(0, ["turn", "gl"])])
        gate_dve = Steps(sem("gate_dve"), [(0, ["clear", "rows", "rows4", "arg", "pos", "neg", "g0", "g", "gc", "gl", "kd", "be"])])
        gate_act = Steps(sem("gate_act"), [(0, ["beta", "eA", "exp", "ln", "egc", "ekd"])])
        rg_pe = Steps(sem("rg_pe"), [(i, ["gates"]) for i in range(2)])
        rg_dve = Steps(sem("rg_dve"), [(0, ["nlam", "abs", "sp", "c8", "c8n"])] + [
            (1 + i, ["a2", "m2", "gx"]) for i in range(2)] + [(3 + i, ["gap", "u", "scan", "scan_s", "ht", "y"]) for i in range(2)])
        rg_act = Steps(sem("rg_act"), [(0, ["exp", "ln"])] + [(1 + i, ["r", "i"]) for i in range(2)] + [
            (4 + i, ["a", "th"]) for i in range(2)] + [(6, ["mult"])])
        l2_pe = Steps(sem("l2_pe"), [(i, ["ss"]) for i in range(8)])
        l2_act = Steps(sem("l2_act"), [x for i in range(1, 12) for x in [(i - 3, ["ln"])] * (0 <= i - 3 < 8) + [(i - 1, ["sq"])] * (i - 1 < 8)] + [
            (8, ["exp0", "exp1"])])
        l2_dve = Steps(sem("l2_dve"), [(i, ["n"]) for i in range(8)])

        def per_level(c, first, last):
            return [x + str(l) for l in range(1, levels_of(c) - 1) for x in first] + [
                x + str(levels_of(c) - 1) if x in "TXUB" else x for x in last]

        gdn_pe = [Steps(sem(f"gdn_pe{p}"), [(c, ["rows", "gb", "kk", "X0"] + per_level(c, "TXU", ("T", "ks", "U")) + [
            "vnew", "o", "S", "ss"]) for c in range(TILES)]) for p in range(2)]
        gdn_dve = [Steps(sem(f"gdn_dve{p}"), [(c, ["vb", "kd", "gd", "LT", "QKT", "Ut", "U0"] + per_level(c, "XU", ("r", "U")) + [
            "S", "on"]) for c in range(TILES)]) for p in range(2)]
        gdn_oz = [Steps(sem(f"gdn_oz{p}"), [(c, ["oz"]) for c in range(TILES)]) for p in range(2)]
        gdn_act = [Steps(sem(f"gdn_act{p}"), [(c, ["gbe", "PT", "egb", "X0"] + per_level(c, "T", "T") + [
            "vn", "o", "osq", "ln", "exp"]) for c in range(TILES)]) for p in range(2)]
        gdn_pool = [Steps(sem(f"gdn_pool{p}"), [(c, ["dg", "db", "PTm", "bPT", "B1", "qd"] + per_level(c, "B", "B")[1:])
                                                for c in range(TILES)]) for p in range(2)]
        hg_oz = Steps(sem("hg_oz"), [(c, ["oz"]) for c in range(TILES)])
        hgp_dve = Steps(sem("hgp_dve"), [(0, ["e0", "rec", "sm", "lb", "oml", "q", "v"]), (1, ["f", "k"] + [f"b{i}_{c}" for i in range(2) for c in range(TILES)])])
        hgp_act = Steps(sem("hgp_act"), [(0, ["e"]), (1, ["lf"])])
        hg_pe = Steps(sem("hg_pe"), [(c, ["v"] + [f"A{l}" for l in range(levels_of(c) + 1)] + ["kd", "o", "S", "ss"]) for c in range(TILES)])
        hg_dve = Steps(sem("hg_dve"), [(c, ["q0", "dk1", "dq1"] + [
            x for l in range(1, levels_of(c) + 1) for x in [f"qa{l}", f"qb{l}", f"att{l - 1}"] + (
                [f"dk{l + 1}", f"dq{l + 1}"] if l < levels_of(c) else [f"att{l}"])] + [
            "S00", "S10", "S01", "S11", "on"]) for c in range(TILES)])
        hg_act = Steps(sem("hg_act"), [(c, ["v0", "v1"] + [f"E{l}" for l in range(1, levels_of(c) + 1)] + [
            "ek0", "ek1", "eq", "eb", "kdt", "o", "osq", "ln", "exp"]) for c in range(TILES)])
        hg_pool = Steps(sem("hg_pool"), [(c, ["k0"] + [f"k{l}" for l in range(1, levels_of(c) + 1)] + ["kd", "qe"]) for c in range(TILES)])
        mo_pe = Steps(sem("mo_pe"), [(0, ["st"])])
        mo_act = Steps(sem("mo_act"), [(j, ["hi"]) for j in range(8)] + [(8, ["st"])])
        mo_dve = Steps(sem("mo_dve"), [(j, ["lo"]) for j in range(8)])
        mem_pe = Steps(sem("mem_pe"), [(k, ["t"]) for k in range(KC)])
        mem_act = Steps(sem("mem_act"), [(0, ["sq0", "sq1", "ln", "exp"])] + [(1 + k, ["hi"]) for k in range(KC)])
        mem_dve = Steps(sem("mem_dve"), [(k, ["lo"]) for k in range(KC)])
        kt_pe = Steps(sem("kt_pe"), [(j, ["t"]) for j in range(8)])
        kt_act = Steps(sem("kt_act"), [(j, ["t"]) for j in range(8)])
        at_pe = Steps(sem("at_pe"), [(c, ["s", "t"]) for c in range(TILES)])
        at_dve = Steps(sem("at_dve"), [(c, ["max", "nmax", "rec", "norm"]) for c in range(TILES)])
        at_act = Steps(sem("at_act"), [(c, ["exp0", "exp1", "exp2", "exp3", "pt"]) for c in range(TILES)])
        pv_pe = Steps(sem("pv_pe"), [(j, ["o"]) for j in range(8)])
        pv_act = Steps(sem("pv_act"), [(j, ["hi", "his"]) for j in range(8)])
        pv_dve = Steps(sem("pv_dve"), [(j, ["lo", "los"]) for j in range(8)])
        fin_pe = Steps(sem("fin_pe"), [(0, ["ss", "st"])] + [(1 + c, ["y"]) for c in range(TILES)])
        fin_act = Steps(sem("fin_act"), [(0, ["ln", "exp"])] + [(1 + c, ["y"]) for c in range(TILES)])
        fin_dve = Steps(sem("fin_dve"), [(0, ["st"])])

        block = ctx.enter_context(nc.Block())
        G_WOUT, G_WK, G_WQ, G_WO, G_UP, G_DOWN = (G_OF[(k, 0)] for k in ("w_out", "w_k", "w_q", "w_o", "up_gate", "down"))
        G_LAST_IN = G_WOUT - 1

        MIX_STORES = 14
        ALL_STORES = MIX_STORES + 2 + 2 + TILES
        CONSTS, STATE_READY = 36, 16 * 7

        def rows_of(v):
            return v.rearrange("(k p) -> k p", p=P)

        def rows_of2(v):
            return v.rearrange("j (k p) -> (j k) p", p=P)

        PARAMS = [(0, COL["mix"], rows_of(norm_mix[0])), (0, COL["attn"], rows_of(norm_attn[0])),
                  (0, COL["ffn"], rows_of(norm_ffn[0])), (0, COL["mem"], rows_of(norm_mem[0])),
                  (0, COL["final"], rows_of(norm_final)), (0, COL["a_w"], rows_of2(a_conv_w[0])),
                  (0, COL["b_w"], rows_of2(b_conv_w[0])), (0, COL["b_b"], rows_of(b_conv_b[0])),
                  (0, COL["b_r"], rows_of(b_b_r[0])), (0, COL["b_i"], rows_of(b_b_i[0])),
                  (0, COL["lam"], rows_of(b_lambda[0])), (0, COL["lb"], rows_of(c_lb_logits[0])),
                  (0, COL["b_h"], rows_of(state_b_h[0, 0])), (0, COL["a_norm"], a_norm),
                  (1, 0, rows_of2(state_a_conv[0, 0])), (1, 36, rows_of2(state_b_conv[0, 0])), (1, 42, rows_of(ffn_conv_b[0])),
                  (2, 0, rows_of2(ffn_conv_w[0, 0:2])), (3, 0, rows_of(ffn_conv_w[0, 2])),
                  (3, 44, rows_of(state_ffn_conv[0, 0, 0])), (4, 0, rows_of(state_ffn_conv[0, 0, 1]))]
        PAR_DMAS = len(PARAMS) + 4


        @block.sync
        def _(sp):
            sp.dma_start(x_nat[:, 0:4, :], x_prompt[0].rearrange("(c p) d -> p c d", p=P)).then_inc(x_loaded, 16)
            sp.dma_start(x_nat[0:SAMPLE, 4, :], x_sample[0]).then_inc(x_loaded, 16)

            def source(n):
                g, j = SLOTS[n]
                kind, i = OUTS[g]
                if kind in W_IN_COL:
                    c0 = W_IN_COL[kind] + i * P
                    return w_in[0][:, c0:c0 + P].rearrange("(k p) n -> p k n", p=P), KC * P
                if kind in ("w_k", "w_v"):
                    w = {"w_k": w_k, "w_v": w_v}[kind][0]
                    return w[4 * j * P:4 * (j + 1) * P, i * 256:(i + 1) * 256].rearrange("(k p) n -> p k n", p=P), KC * P
                if kind in ("up_gate", "up_val"):
                    c0 = i * P + (D_FF if kind == "up_val" else 0)
                    return w_up[0][:, c0:c0 + P].rearrange("(k p) n -> p k n", p=P), KC * P
                if kind == "down":
                    nk = SLOT_K["down"][j]
                    return w_down[0][8 * j * P:(8 * j + nk) * P, i * P:(i + 1) * P].rearrange("(k p) n -> p k n", p=P), nk * P
                w = {"w_out": w_out, "w_q": w_q, "w_o": w_o}[kind][0]
                return w[:, i * P:(i + 1) * P].rearrange("(k p) n -> p k n", p=P), KC * P

            for n in range(len(SLOTS)):
                if n >= RAW:
                    sp.wait_ge(w_low, n - RAW + 1)
                src, size = source(n)
                nk = src.shape[1]
                sp.dma_start(raw[:, n % RAW, 0:size].rearrange("p (k n) -> p k n", k=nk), src).then_inc(w_loaded[n % RAW], 16)
                g = SLOTS[n][0]
                if OUTS[g] == ("w_out", 4):
                    sp.wait_ge(*mo_dve.at(7, "lo"))
                    sp.wait_ge(*mo_act.at(8, "st"))
                    for p in range(2):
                        sp.wait_ge(*gdn_dve[p].at(TILES - 1, "S"))
                    sp.wait_ge(*hg_dve.at(TILES - 1, "S11"))
                    sp.wait_ge(stored, 16 * MIX_STORES)
                    sp.dma_start(nat[:], mem_prompt[0].rearrange("(c p) d -> p c d", p=P)).then_inc(mem_loaded, 16)
                    sp.dma_start(sV[:], cache_mem_v[0, 0].rearrange("(c p) h d -> p c (h d)", p=P)).then_inc(cv_loaded, 16)
                if OUTS[g] == ("w_q", 0):
                    sp.wait_ge(*mem_pe.at(KC - 1, "t"))
                    sp.wait_ge(*mem_act.at(0, "sq1"))
                    sp.dma_start(nat[:], cache_mem_k[0, 0].rearrange("(c p) h d -> p c (h d)", p=P)).then_inc(cache_loaded, 16)
            sp.wait_ge(stored, 16 * ALL_STORES)

        @block.tensor
        def _(pe):
            def mm(out, lhsT, rhs, start=True, stop=True):
                return pe.matmul(out, lhsT, rhs, start=start, stop=stop)

            def part(g, n, k):
                kind, i = OUTS[g]
                ps = pg[PAIR[g]]
                j = n - FIRST_SLOT[g]
                nk = SLOT_K.get(kind, [8])[j]
                begins, ends = n == FIRST_SLOT[g] and k == 0, n == LAST_SLOT[g] and k == nk - 1
                if begins:
                    if PREV[g] is None:
                        pe.wait_ge(*start_dve.at(0, f"x{KC - 1}"))
                    else:
                        pe.wait_ge(*post_dve.at(PREV[g], "evac"))
                    if g == G_WK:
                        pe.wait_ge(*mem_dve.at(KC - 1, "lo"))
                    if g == G_WQ:
                        pe.wait_ge(*feed_dve.at(1, f"lo{KC - 1}"))
                    if g == G_WO:
                        pe.wait_ge(*pv_dve.at(7, "los"))
                    if g == G_DOWN:
                        pe.wait_ge(*post_pool.at(G_OF[("up_val", NF - 1)], "lo"))
                    if g == G_WOUT + 1 or g == G_WOUT:
                        pe.wait_ge(*gdn_act[1].at(TILES - 1, "ln"))
                        pe.wait_ge(*gdn_dve[1].at(TILES - 1, "S"))
                if k == 0:
                    pe.wait_ge(w_low, n + 1)
                if kind in ("w_k", "w_v"):
                    wh, wl = (w[:, n % HL, :].rearrange("p (k n) -> p k n", k=4) for w in (WH, WL))
                    for t in range(2):
                        o = ps[:, t, 0:N_MEM]
                        mh, ml = (m[:, 4 * j + k, t * P:(t + 1) * P] for m in (memH, memL))
                        mm(o, mh, wh[:, k, :], begins, False)
                        mm(o, mh, wl[:, k, :], False, False)
                        q = mm(o, ml, wh[:, k, :], False, ends)
                else:
                    wh, wl = (w[:, n % HL, :].rearrange("p (k n) -> p k n", k=KC) for w in (WH, WL))
                    xh, xl = (FH, FL) if kind == "down" else (XH, XL)
                    kk = 8 * j + k
                    if g in (0, G_UP):
                        pe.wait_ge(*feed_dve.at(0 if g == 0 else 2, f"lo{k}"))
                    if g == G_WOUT:
                        pe.wait_ge(*mo_dve.at(k, "lo"))
                    for w, x, s0, s1 in ((wh, xh, begins, False), (wh, xl, False, False), (wl, xh, False, ends)):
                        for h in range(2):
                            q = mm(ps[:, h, 0:HALF], w[:, k, :], x[:, kk, h * HALF:(h + 1) * HALF], s0, s1)
                if k == nk - 1:
                    q.then_inc(slot_done, 1)

            def norm(s):
                pe.wait_ge(*feed_dve.at(s, f"ns{KC - 1}"))
                if s == 1:
                    pe.wait_ge(*mo_act.at(8, "st"))
                if s == 2:
                    pe.wait_ge(*pv_dve.at(7, "los"))
                    pe.wait_ge(*pv_act.at(7, "his"))
                if s == 0:
                    pe.wait_ge(*start_dve.at(0, "pad"))
                for h in range(2):
                    q = mm(pm[:, h, 0:HALF], ones[:], NS[:, h * HALF:(h + 1) * HALF])
                q.then_inc(*norm_pe.did(s, "ss"))

            def start():
                pe.wait_ge(const_ready, CONSTS)
                pe.wait_ge(par_loaded, 16 * PAR_DMAS)
                c0 = 0
                for t, rows in enumerate(PAR_ROWS):
                    dst = pg[0][:, 0, t * P:t * P + rows] if t < 4 else pg[0][:, 1, 0:rows]
                    q = pe.transpose(dst, par_nat[0:rows, t, :], ident[0:rows, 0:rows])
                q.then_inc(*start_pe.did(0, "par"))
                pe.wait_ge(x_loaded, 32)
                for k in range(KC):
                    ps = pg[(k + 1) % 2]
                    if k == 1:
                        pe.wait_ge(*start_dve.at(0, "par"))
                    if k >= 2:
                        pe.wait_ge(*start_dve.at(0, f"x{k - 2}"))
                    for c in range(4):
                        pe.transpose(ps[:, 0, c * P:(c + 1) * P], x_nat[:, c, k * P:(k + 1) * P], ident[:])
                    pe.transpose(ps[:, 1, 0:SAMPLE], x_nat[0:SAMPLE, 4, k * P:(k + 1) * P],
                                 ident[0:SAMPLE, 0:SAMPLE]).then_inc(*start_pe.did(0, f"x{k}"))
                mm(A[:, 0:8], ones[0:1, :], row8[0:1, :]).then_inc(*start_pe.did(0, "row8"))

            def gate_rows():
                pe.wait_ge(*post_dve.at(0, "evac"))
                for c in range(TILES):
                    n = tile_len(c)
                    q = pe.transpose(C[0:n, c * 8:(c + 1) * 8], gT[:, tile_at(c):tile_at(c) + n], ident[0:8, 0:8])
                q.then_inc(*gate_pe.did(0, "turn"))
                pe.wait_ge(*gate_dve.at(0, "g"))
                mm(DD[:, 0:TILES * 4], upto_m[:], gv[:, 1, 0:TILES * 4])
                mm(DD[:, 32:48], ones[:], gv[:, 1, 0:16])
                mm(DD[:, 48:52], ones[0:SAMPLE, :], gv[0:SAMPLE, 1, 16:20]).then_inc(*gate_pe.did(0, "gl"))

            def l2(i):
                pe.wait_ge(*l2_act.at(i, "sq"))
                if i >= 2:
                    pe.wait_ge(*l2_act.at(i - 2, "ln"))
                else:
                    pe.wait_ge(*gate_dve.at(0, "gl"))
                for h in range(2):
                    q = mm(pm[:, 2 * (i % 2) + h, 0:HALF], ones[:], SQ[:, i % 2, h * HALF:(h + 1) * HALF])
                q.then_inc(*l2_pe.did(i, "ss"))

            def rg(part):
                if part:
                    return
                for i in range(2):
                    pe.wait_ge(*post_dve.at(G_OF[("b_x", i)], "tap3"))
                    pe.wait_ge(state_loaded, STATE_READY)
                    if i:
                        pe.wait_ge(*rg_act.at(1, "i"))
                    else:
                        pe.wait_ge(*l2_act.at(7, "ln"))
                    for gate in range(2):
                        for h in range(2):
                            q = mm(pm[:, 2 * gate + h, 0:HALF], wr_bd[:, gate, i, :], xbT[:, i, h * HALF:(h + 1) * HALF])
                    q.then_inc(*rg_pe.did(i, "gates"))

            def gdn(c, p, ph):
                n, t0 = tile_len(c), tile_at(c)
                last = levels_of(c) - 1
                did, dve, act_, pool_ = gdn_pe[p].did, gdn_dve[p], gdn_act[p], gdn_pool[p]

                def T(i):
                    return Tp(i, p)

                def each(out, lhs, rhs):
                    for h in range(2):
                        q = mm(out(h), lhs(h), rhs(h))
                    return q

                S = heads(Sa[:, 1 if c == TILES - 1 else 0, :])[:, 2 * p:2 * p + 2, :]
                qT_, kT_ = (qkvT[:, 4 * x + 2 * p:4 * x + 2 * p + 2, t0:t0 + n] for x in range(2))
                Pb, Qb = PAIR_BANKS[p]
                if ph == "rows":
                    if c == 0:
                        pe.wait_ge(*l2_dve.at(7, "n"))
                        pe.wait_ge(*post_act.at(G_OF[("qkv", 11)], "silu"))
                        pe.wait_ge(*rg_act.at(2, "i"))
                        if p:
                            pe.wait_ge(*post_dve.at(PREV[G_WOUT + 1] if PAIR[G_WOUT + 1] else PREV[G_WOUT], "evac"))
                    else:
                        pe.wait_ge(*dve.at(c - 1, "S"))
                        pe.wait_ge(*act_.at(c - 1, "ln"))
                    for x in range(2):
                        for h in range(2):
                            q = pe.transpose(half_of(Pb, x)[0:n, h, :], qkvT[:, 4 * (1 + x) + 2 * p + h, t0:t0 + n], ident[:])
                    q.then_inc(*did(c, "rows"))
                    pe.wait_ge(*pool_.at(c, "db"))
                    for x in range(2):
                        for h in range(2):
                            q = mm(half_of(Qb, x)[:, h, 0:n], ones[0:n, :], half_of(SQ[:, p, :], x)[0:n, h, 0:n])
                    q.then_inc(*did(c, "gb"))
                elif ph == "mask":
                    pe.wait_ge(*dve.at(c, "kd"))
                    each(lambda h: half_of(Pb, 0)[0:n, h, 0:n], lambda h: kT_[:, h, :], lambda h: kT_[:, h, :])
                    each(lambda h: half_of(Pb, 1)[0:n, h, 0:n], lambda h: kT_[:, h, :], lambda h: qT_[:, h, :])\
                        .then_inc(*did(c, "kk"))
                elif ph == "turn":
                    pe.wait_ge(*dve.at(c, "U0"))
                    for h in range(2):
                        q = pe.transpose(half_of(Qb, 0)[0:n, h, 0:n], T(5)[0:n, h, 0:n], ident[0:n, 0:n])
                    q.then_inc(*did(c, "X0"))
                elif ph[0] in "TX":
                    l = int(ph[1:])
                    Rt, Rx = (half_of(b, 0) for b in level_banks(p, l))
                    if ph[0] == "T":
                        pe.wait_ge(*pool_.at(c, f"B{l}"))
                        pe.wait_ge(*(dve.at(c, f"X{l - 1}") if l > 1 else act_.at(c, "X0")))
                        each(lambda h: Rt[0:n, h, 0:n], lambda h: T(1)[0:n, h, 0:n], lambda h: T(2)[0:n, h, 0:n])\
                            .then_inc(*did(c, f"T{l}"))
                        return
                    pe.wait_ge(*dve.at(c, f"U{l - 1}"))
                    if l < last:
                        pe.wait_ge(*act_.at(c, f"T{l}"))
                        each(lambda h: Rx[0:n, h, 0:n], lambda h: T(5)[0:n, h, 0:n], lambda h: T(0)[0:n, h, 0:n])\
                            .then_inc(*did(c, f"X{l}"))
                    else:
                        each(lambda h: Rx[0:n, h, :], lambda h: kT_[:, h, :], lambda h: S[:, h, :]).then_inc(*did(c, "ks"))
                        pe.wait_ge(*act_.at(c, f"T{l}"))
                    each(lambda h: Rt[0:n, h, 0:n], lambda h: T(0)[0:n, h, 0:n], lambda h: T(5)[0:n, h, 0:n])\
                        .then_inc(*did(c, f"U{l}"))
                elif ph == "vnew":
                    Rx = half_of(level_banks(p, last)[1], 0)
                    pe.wait_ge(*dve.at(c, f"U{last}"))
                    each(lambda h: Rx[0:n, h, :], lambda h: T(5)[0:n, h, 0:n], lambda h: T(6)[0:n, h, :]).then_inc(*did(c, "vnew"))
                elif ph == "o":
                    Rt, Rx = (half_of(b, 0) for b in level_banks(p, last))
                    pe.wait_ge(*act_.at(c, "vn"))
                    for h in range(2):
                        mm(Rt[:, h, 0:n], S[:, h, :], T(9)[:, h, 0:n], True, False)
                        q = mm(Rt[:, h, 0:n], T(7)[0:n, h, :], T(11)[0:n, h, 0:n], False, True)
                    q.then_inc(*did(c, "o"))
                    each(lambda h: Rx[:, h, :], lambda h: T(3)[0:n, h, :], lambda h: T(7)[0:n, h, :]).then_inc(*did(c, "S"))
                elif ph == "ss":
                    pe.wait_ge(*act_.at(c, "osq"))
                    mm(half_of(level_banks(p, last)[0], 1)[:, :, 0:n], ones[:], T(0)[:, :, 0:n]).then_inc(*did(c, "ss"))

            def hg(c, ph):
                n, t0 = tile_len(c), tile_at(c)
                d4 = DD.rearrange("p (a b i) -> p a b i", a=2, b=2)
                d2 = DD[:, 0:256].rearrange("p (a i) -> p a i", a=2)
                if ph == "v":
                    pe.wait_ge(*post_dve.at(G_OF[("c_i", 1)], "evac"))
                    if c == 0:
                        pe.wait_ge(*rg_act.at(2, "i"))
                    else:
                        pe.wait_ge(*hg_act.at(c - 1, "ln"))
                    for i in range(2):
                        q = pe.transpose(d2[0:n, i, :], cvT[:, i, t0:t0 + n], ident[:])
                    q.then_inc(*hg_pe.did(c, "v"))
                elif ph[0] == "a":
                    l = int(ph[1:])
                    pe.wait_ge(*hg_pool.at(c, f"k{l}"))
                    pe.wait_ge(*hg_dve.at(c, f"qb{l}" if l else "q0"))
                    if l:
                        pe.wait_ge(*hg_dve.at(c, f"att{l - 1}"))
                    else:
                        pe.wait_ge(*hg_act.at(c, "v1"))
                    for i in range(2):
                        q = mm(d4[0:n, i, :, 0:n], hK[:, i, 0:n], hQ[:, i, :, 0:n])
                    q.then_inc(*hg_pe.did(c, f"A{l}"))
                elif ph == "kdt":
                    pe.wait_ge(*hg_pool.at(c, "kd"))
                    pe.wait_ge(*hg_dve.at(c, f"att{levels_of(c)}"))
                    for i in range(2):
                        q = pe.transpose(d2[0:n, i, :], hK[:, i, 0:n], ident[:])
                    q.then_inc(*hg_pe.did(c, "kd"))
                elif ph == "o":
                    Sx = Sc[:, 1 if c == TILES - 1 else 0]
                    pe.wait_ge(*hg_pool.at(c, "qe"))
                    pe.wait_ge(*hg_act.at(c, "kdt"))
                    if c in (0, TILES - 1):
                        pe.wait_ge(state_loaded, STATE_READY)
                    for i in range(2):
                        mm(d4[:, 0, i, 0:n], Sx[:, i, :], hE[:, i, 0:n], True, False)
                        mm(d4[:, 0, i, 0:n], vpad[0:n, i, 0, :], att[0:n, i, 0, 0:n], False, False)
                        q = mm(d4[:, 0, i, 0:n], vpad[0:n, i, 1, :], att[0:n, i, 1, 0:n], False, True)
                    q.then_inc(*hg_pe.did(c, "o"))
                    for i in range(2):
                        mm(d4[:, 1, i, :], kdt[0:n, i, :], vpad[0:n, i, 0, :], True, False)
                        q = mm(d4[:, 1, i, :], kdt[0:n, i, :], vpad[0:n, i, 1, :], False, True)
                    q.then_inc(*hg_pe.did(c, "S"))

                elif ph == "ss":
                    pe.wait_ge(*hg_dve.at(c, "S11"))
                    pe.wait_ge(*hg_act.at(c, "osq"))
                    mm(d4[:, 0, :, 0:n], half_ones[:], hE[:, :, 0:n]).then_inc(*hg_pe.did(c, "ss"))

            def mix_out():
                pe.wait_ge(*gdn_dve[0].at(TILES - 1, "S"))
                pe.wait_ge(*gdn_act[0].at(TILES - 1, "ln"))
                for r in range(2):
                    q = pe.transpose(pm[0:44, r, 0:P], tails[:, r, :], ident[:])
                q.then_inc(*mo_pe.did(0, "st"))

            def mem():
                pe.wait_ge(mem_loaded, 16)
                for k in range(KC):
                    if k >= 2:
                        pe.wait_ge(*mem_dve.at(k - 2, "lo"))
                    else:
                        pe.wait_ge(*mo_act.at(8, "st"))
                    for t in range(2):
                        q = pe.transpose(pm[:, 2 + k % 2, t * P:(t + 1) * P], nat[:, t, k * P:(k + 1) * P], ident[:])
                    q.then_inc(*mem_pe.did(k, "t"))

            def kt():
                for j in range(8):
                    src = Kn if j < 4 else nat
                    if j == 0:
                        pe.wait_ge(*post_dve.at(G_OF[("w_k", 3)], "evac"))
                        pe.wait_ge(*mem_dve.at(KC - 1, "lo"))
                        pe.wait_ge(*norm_act.at(1, "ln"))
                    if j == 4:
                        pe.wait_ge(cache_loaded, 16)
                    if j >= 4:
                        pe.wait_ge(*kt_act.at(j - 4, "t"))
                    for d in range(2):
                        for t in range(2):
                            ch = 2 * (j % 4) + d
                            q = pe.transpose(pm[:, j % 4, d * 256 + t * P:d * 256 + (t + 1) * P], src[:, t, ch * P:(ch + 1) * P], ident[:])
                    q.then_inc(*kt_pe.did(j, "t"))

            def attention(c):
                n, t0 = tile_len(c), tile_at(c)
                kx = kT[:, 1 if c == TILES - 1 else 0]
                if c == 0:
                    pe.wait_ge(*kt_act.at(7, "t"))
                    pe.wait_ge(*post_dve.at(G_OF[("w_q", 7)], "evac"))
                else:
                    pe.wait_ge(*at_act.at(c - 1, "exp3"))
                for h in range(HEADS):
                    o = pm[0:n, h // 2, (h % 2) * 256:(h % 2 + 1) * 256]
                    mm(o, qT[:, 2 * h, t0:t0 + n], kx[:, 2 * h, :], True, False)
                    q = mm(o, qT[:, 2 * h + 1, t0:t0 + n], kx[:, 2 * h + 1, :], False, True)
                q.then_inc(*at_pe.did(c, "s"))
                pe.wait_ge(*at_dve.at(c, "norm"))
                if c:
                    pe.wait_ge(*at_act.at(c - 1, "pt"))
                for t in range(2):
                    for h in range(HEADS):
                        q = pe.transpose(pm[:, 2 + t, h * P:h * P + n], prob[0:n, h, t * P:(t + 1) * P], ident[0:n, 0:n])
                q.then_inc(*at_pe.did(c, "t"))

            def pv():
                pe.wait_ge(*at_act.at(TILES - 1, "pt"))
                pe.wait_ge(cv_loaded, 16)
                pe.wait_ge(*post_dve.at(G_OF[("w_v", 3)], "evac"))
                for j in range(8):
                    h = j // 2
                    if j >= 2:
                        pe.wait_ge(*pv_dve.at(j - 2, "los"))
                    for (v, b, s0, s1) in ((Vn, 0, 0, PROMPT), (sV, 1, PROMPT, PROMPT + SAMPLE)):
                        for t in range(2):
                            q = mm(pm[:, 2 * (j % 2) + b, 0:s1 - s0], v[:, t, j * P:(j + 1) * P], PT[:, t, h, s0:s1], t == 0, t == 1)
                    q.then_inc(*pv_pe.did(j, "o"))

            def finish():
                pe.wait_ge(*feed_dve.at(3, f"ns{KC - 1}"))
                for c in range(TILES):
                    n, t0 = tile_len(c), tile_at(c)
                    q = mm(A[0:n, 2 * c:2 * c + 2], NS[:, t0:t0 + n], ones[:, 0:2])
                q.then_inc(*fin_pe.did(0, "ss"))
                for r in range(2):
                    q = pe.transpose(B[0:88, r * P:(r + 1) * P], tail_f[:, r].rearrange("p a b -> p (a b)"), ident[:])
                q.then_inc(*fin_pe.did(0, "st"))
                for c in range(TILES):
                    n, t0 = tile_len(c), tile_at(c)
                    if c >= 2:
                        pe.wait_ge(*fin_act.at(1 + c - 2, "y"))
                    else:
                        pe.wait_ge(*post_dve.at(len(OUTS) - 1, "evac"))
                        pe.wait_ge(*feed_dve.at(3, f"xw{KC - 1}"))
                    ps = pg[c % 2]
                    for k in range(KC):
                        q = pe.transpose(ps[0:n, k // 4, (k % 4) * P:(k % 4 + 1) * P], xT[:, k, t0:t0 + n], ident[:])
                    q.then_inc(*fin_pe.did(1 + c, "y"))

            handlers = {"start": start, "part": part, "norm": norm, "gate_rows": gate_rows, "l2": l2, "rg": rg, "gdn": gdn,
                        "hg": hg, "mix_out": mix_out, "mem": mem, "kt": kt, "att": attention, "pv": pv, "finish": finish}
            for what, *args in SCHED:
                if what in handlers:
                    handlers[what](*args)

        @block.vector
        def _(v):
            def halves(ap):
                return ap.rearrange("p (h t) -> p h t", h=2)

            Rh = halves(R[:])
            conv_no = [0]

            def settle(steps):
                if steps.made:
                    v.wait_ge(steps.sem, steps.made)

            def start():
                v.wait_ge(*start_pe.at(0, "par"))
                for t, rows in enumerate(PAR_ROWS):
                    src = pg[0][:, 0, t * P:t * P + rows] if t < 4 else pg[0][:, 1, 0:rows]
                    q = v.tensor_copy(par[:, t * P:t * P + rows], src)
                q.then_inc(*start_dve.did(0, "par"))
                for k in range(KC):
                    v.wait_ge(*start_pe.at(0, f"x{k}"))
                    ps = pg[(k + 1) % 2]
                    v.tensor_copy(xT[:, k, 0:PROMPT], ps[:, 0, 0:PROMPT])
                    v.tensor_copy(xT[:, k, S0:TOK], ps[:, 1, 0:SAMPLE]).then_inc(*start_dve.did(0, f"x{k}"))
                v.wait_ge(*start_pe.at(0, "row8"))
                v.tensor_copy(small[:, 0:8], A[:, 0:8]).then_inc(*start_dve.did(0, "pad"))

            def square(s, k):
                if k:
                    v.wait_ge(*feed_act.at(s, f"sq{k}"))
                    settle(feed_dve)
                    v.tensor_tensor(NS[:], NS[:], SQ[:, k % 2, :], ALU.add).then_inc(*feed_dve.did(s, f"ns{k}"))
                if s == 3 and k == KC - 1:
                    for j in range(KC):
                        v.tensor_scalar(xT[:, j, :], xT[:, j, :], col("final", j), None, ALU.mult)\
                            .then_inc(*feed_dve.did(3, f"xw{j}"))

            def split(s, k):
                name = ("mix", "attn", "ffn")[s]
                v.wait_ge(*feed_act.at(s, f"hi{k}"))
                v.scalar_tensor_tensor(XL[:, k, :], xT[:, k, :], col(name, k), XH[:, k, :].bitcast(F32), ALU.mult,
                                       ALU.subtract).then_inc(*feed_dve.did(s, f"lo{k}"))

            def post(g):
                kind, i = OUTS[g]
                ps = pg[PAIR[g]]
                if (kind, i) == ("up_gate", 0):
                    v.wait_ge(*pv_pe.at(7, "o"))
                    v.memset(pre_f[:, 0, 0:PRE], 0.0).then_inc(*post_dve.did(g, "zero"))
                v.wait_ge(slot_done, LAST_SLOT[g] + 1)
                if kind in ("w_out", "w_o", "down"):
                    if kind == "down":
                        pass
                    v.tensor_tensor(halves(xT[:, i, :]), ps[:, :, 0:HALF], halves(xT[:, i, :]), ALU.add)\
                        .then_inc(*post_dve.did(g, "evac"))
                    return
                if kind in ("w_k", "w_v"):
                    v.wait_ge(*mem_act.at(0, "exp"))
                    to = (Kn if kind == "w_k" else Vn)
                    for t in range(2):
                        q = v.tensor_scalar(to[:, t, i * 256:(i + 1) * 256], ps[:, t, 0:N_MEM], mstat[:, 4 + t:5 + t], None, ALU.mult)
                    q.then_inc(*post_dve.did(g, "evac"))
                    return
                v.wait_ge(*norm_act.at(0 if g < G_WOUT else 1 if kind == "w_q" else 2, "exp"))
                if kind == "gates":
                    v.tensor_tensor(halves(gT[:]), ps[0:8, :, 0:HALF], Rh[0:8], ALU.mult).then_inc(*post_dve.did(g, "evac"))
                    return
                if kind not in CONV:
                    to = {"z": zT, "b_gate": gateT, "c_q": cqT, "c_f": ckT, "c_i": cvT, "c_g": cgT, "w_q": qT}[kind]
                    v.tensor_tensor(halves(to[:, i, :]), ps[:, :, 0:HALF], Rh, ALU.mult).then_inc(*post_dve.did(g, "evac"))
                    return
                taps, b = CONV[kind], conv_no[0] % 2
                conv_no[0] += 1
                pre = pre_m[:, b, :] if kind in ("qkv", "b_x") else pre_f[:, 0, :]
                settle(post_dve)
                v.tensor_tensor(halves(pre[:, PRE:PRE + TOK]), ps[:, :, 0:HALF], Rh, ALU.mult).then_inc(*post_dve.did(g, "evac"))
                settle(post_dve)
                ch = i + (NF if kind == "up_val" else 0)
                past = {"qkv": par[:, COL["a_st"] + i:COL["a_st"] + i + 25:12], "b_x": par[:, COL["b_st"] + i:COL["b_st"] + i + 5:2],
                        }.get(kind, par[:, COL["f_st0"] + ch:COL["f_st0"] + ch + 85:84])
                v.tensor_copy(pre[:, PRE + S0 - taps + 1:PRE + S0], past).then_inc(*post_dve.did(g, "state"))
                for r, end in enumerate((PRE + PROMPT, PRE + TOK)):
                    if kind == "qkv":
                        to = tails[:, r, i:i + 25:12]
                    elif kind == "b_x":
                        to = tails[:, r, 36 + i:36 + i + 5:2]
                    else:
                        to = tail_f[:, r, :, ch]
                    q = v.tensor_copy(to, pre[:, end - taps + 1:end])
                q.then_inc(*post_dve.did(g, "tail"))
                acc = {"qkv": qkvT, "b_x": xbT}[kind][:, i, :] if kind in ("qkv", "b_x") else fg[:] if kind == "up_gate" else fv[:]
                wcol = {"qkv": [COL["a_w"] + 12 * j + i for j in range(4)], "b_x": [COL["b_w"] + 2 * j + i for j in range(4)]}.get(
                    kind, [COL["f_w"] + ch, COL["f_w"] + 44 + ch, COL["f_w2"] + ch])
                bias = {"b_x": col("b_b", i)}.get(kind, None if kind == "qkv" else col("f_b", ch))
                if kind == "up_val" and i:
                    v.wait_ge(*post_pool.at(g - 2, "lo"))
                off = PRE + 1 - taps
                settle(post_dve)
                w0 = par[:, wcol[0]:wcol[0] + 1]
                if bias is None:
                    v.tensor_scalar(acc, pre[:, off:off + TOK], w0, None, ALU.mult).then_inc(*post_dve.did(g, "tap0"))
                else:
                    v.tensor_scalar(acc, pre[:, off:off + TOK], w0, bias, ALU.mult, ALU.add).then_inc(*post_dve.did(g, "tap0"))
                for j in range(1, taps):
                    settle(post_dve)
                    v.scalar_tensor_tensor(acc, pre[:, off + j:off + j + TOK], par[:, wcol[j]:wcol[j] + 1], acc, ALU.mult,
                                           ALU.add).then_inc(*post_dve.did(g, f"tap{j}"))
                if kind == "up_val":
                    v.wait_ge(*post_act.at(g - 1, "silu"))
                    settle(post_dve)
                    v.tensor_tensor(fv[:], fg[:], fv[:], ALU.mult).then_inc(*post_dve.did(g, "prod"))

            def gv_(r):
                return gv[:, r, 0:TILES * HEADS]

            def gate_rows():
                g8 = gv8
                v.memset(gv8, 0.0).then_inc(*gate_dve.did(0, "clear"))
                v.wait_ge(*gate_pe.at(0, "turn"))
                settle(gate_dve)
                v.tensor_copy(g8[:, 0:32], C[:, 0:32]).then_inc(*gate_dve.did(0, "rows"))
                v.tensor_copy(g8[0:SAMPLE, 32:40], C[0:SAMPLE, 32:40]).then_inc(*gate_dve.did(0, "rows4"))
                settle(gate_dve)
                z = gv_(2).rearrange("p (c h) -> p c h", h=4)
                v.tensor_tensor(z, g8.rearrange("p (c h) -> p c h", h=8)[:, :, 4:8], over(small[:, 4:8], TILES), ALU.add)\
                    .then_inc(*gate_dve.did(0, "arg"))
                settle(gate_dve)
                v.tensor_scalar(gv_(3), gv_(2), 0.0, None, ALU.max).then_inc(*gate_dve.did(0, "pos"))
                v.scalar_tensor_tensor(gv_(4), gv_(2), -1.0, gv_(2), ALU.mult, ALU.max).then_inc(*gate_dve.did(0, "neg"))
                v.wait_ge(*gate_act.at(0, "ln"))
                settle(gate_dve)
                v.tensor_tensor(gv_(3), gv_(3), gv_(4), ALU.add).then_inc(*gate_dve.did(0, "g0"))
                settle(gate_dve)
                v.scalar_tensor_tensor(gv_(1).rearrange("p (c h) -> p c h", h=4), gv_(3).rearrange("p (c h) -> p c h", h=4), -1.0,
                                       over(small[:, 44:48], TILES), ALU.mult, ALU.mult).then_inc(*gate_dve.did(0, "g"))
                v.wait_ge(*gate_pe.at(0, "gl"))
                v.tensor_copy(gv_(2), DD[:, 0:TILES * HEADS]).then_inc(*gate_dve.did(0, "gc"))
                v.tensor_copy(gv_(5), DD[:, 32:32 + TILES * HEADS]).then_inc(*gate_dve.did(0, "gl"))
                settle(gate_dve)
                v.tensor_tensor(gv_(6), gv_(5), gv_(2), ALU.subtract).then_inc(*gate_dve.did(0, "kd"))
                v.wait_ge(*gate_act.at(0, "egc"))
                v.tensor_tensor(gv_(4), gv_(0), gv_(3), ALU.mult).then_inc(*gate_dve.did(0, "be"))

            def rg_tmp(i):
                return tmp[:].rearrange("p a b -> p (a b)")[:, i * TOK:(i + 1) * TOK]

            def l2exp():
                v.wait_ge(*l2_act.at(8, "exp1"))
                for i in range(8):
                    v.tensor_tensor(qkvT[:, i, :], qkvT[:, i, :], rg_tmp(i), ALU.mult).then_inc(*l2_dve.did(i, "n"))

            def rg(part):
                if part == 0:
                    v.tensor_scalar(small[:, 48:50], col("lam", 0, 2), -1.0, None, ALU.mult).then_inc(*rg_dve.did(0, "nlam"))
                    v.scalar_tensor_tensor(small[:, 50:52], col("lam", 0, 2), -1.0, col("lam", 0, 2), ALU.mult, ALU.max)\
                        .then_inc(*rg_dve.did(0, "abs"))
                    v.wait_ge(*rg_act.at(0, "ln"))
                    settle(rg_dve)
                    v.scalar_tensor_tensor(small[:, 48:50], small[:, 48:50], 0.0, small[:, 50:52], ALU.max, ALU.add)\
                        .then_inc(*rg_dve.did(0, "sp"))
                    settle(rg_dve)
                    v.tensor_scalar(small[:, 52:54], small[:, 48:50], -8.0, None, ALU.mult).then_inc(*rg_dve.did(0, "c8"))
                    v.tensor_scalar(small[:, 54:56], small[:, 48:50], 8.0, None, ALU.mult).then_inc(*rg_dve.did(0, "c8n"))
                if part == 1:
                    for i in range(2):
                        v.wait_ge(*rg_act.at(4 + i, "th"))
                        settle(rg_dve)
                        v.tensor_tensor(rg_tmp(8), rg_tmp(4 + i), rg_tmp(4 + i), ALU.mult).then_inc(*rg_dve.did(1 + i, "a2"))
                        settle(rg_dve)
                        v.scalar_tensor_tensor(rg_tmp(6 + i), rg_tmp(8), 1.0, rg_tmp(6 + i), ALU.add, ALU.mult)\
                            .then_inc(*rg_dve.did(1 + i, "m2"))
                        v.tensor_tensor(rg_tmp(2 + i), rg_tmp(2 + i), xbT[:, i, :], ALU.mult).then_inc(*rg_dve.did(1 + i, "gx"))
                if part < 2:
                    return
                i = part - 2
                v.wait_ge(*rg_act.at(6, "mult"))
                v.memset(rg_tmp(i)[:, PROMPT:S0], 0.0).then_inc(*rg_dve.did(3 + i, "gap"))
                settle(rg_dve)
                v.tensor_tensor(rg_tmp(2 + i), rg_tmp(2 + i), rg_tmp(6 + i), ALU.mult).then_inc(*rg_dve.did(3 + i, "u"))
                settle(rg_dve)
                v.tensor_tensor_scan(rg_tmp(i)[:, 0:PROMPT], rg_tmp(4 + i)[:, 0:PROMPT], rg_tmp(2 + i)[:, 0:PROMPT], 0.0,
                                     ALU.mult, ALU.add).then_inc(*rg_dve.did(3 + i, "scan"))
                v.tensor_tensor_scan(rg_tmp(i)[:, S0:TOK], rg_tmp(4 + i)[:, S0:TOK], rg_tmp(2 + i)[:, S0:TOK],
                                     col("b_h", i), ALU.mult, ALU.add).then_inc(*rg_dve.did(3 + i, "scan_s"))
                settle(rg_dve)
                v.tensor_copy(tails[:, 0, 42 + i:43 + i], rg_tmp(i)[:, PROMPT - 1:PROMPT])
                v.tensor_copy(tails[:, 1, 42 + i:43 + i], rg_tmp(i)[:, TOK - 1:TOK]).then_inc(*rg_dve.did(3 + i, "ht"))
                v.wait_ge(*post_act.at(G_OF[("b_gate", i)], "gelu"))
                v.tensor_tensor(gateT[:, i, :], gateT[:, i, :], rg_tmp(i), ALU.mult).then_inc(*rg_dve.did(3 + i, "y"))

            def hg_prep():
                lb = small[:, 56:58]
                v.tensor_tensor(lb, col("lb", 0, 2), col("lb", 0, 2), ALU.subtract).then_inc(*hgp_dve.did(0, "e0"))
                v.wait_ge(*hgp_act.at(0, "e"))
                v.reciprocal(small[:, 58:60], lb).then_inc(*hgp_dve.did(0, "rec"))
                settle(hgp_dve)
                v.tensor_tensor(small[:, 58:60], small[:, 58:60], lb, ALU.mult).then_inc(*hgp_dve.did(0, "sm"))
                settle(hgp_dve)
                v.tensor_tensor(lb, small[:, 58:60], small[:, 58:60], ALU.subtract).then_inc(*hgp_dve.did(0, "lb"))
                settle(hgp_dve)
                v.tensor_scalar(small[:, 58:60], lb, -1.0, 1.0, ALU.mult, ALU.add).then_inc(*hgp_dve.did(0, "oml"))
                v.wait_ge(*rg_dve.at(2, "gx"))
                v.memset(hQ, 0.0).then_inc(*hgp_dve.did(0, "q"))
                v.memset(vpad[:], 0.0).then_inc(*hgp_dve.did(0, "v"))
                v.wait_ge(*post_act.at(G_OF[("c_f", 1)], "sig"))
                settle(hgp_dve)
                for i in range(2):
                    q = v.tensor_scalar(ckT[:, i, :], ckT[:, i, :], small[:, 58 + i:59 + i], small[:, 56 + i:57 + i], ALU.mult, ALU.add)
                q.then_inc(*hgp_dve.did(1, "f"))
                v.wait_ge(*hgp_act.at(1, "lf"))
                v.tensor_scalar(ckT[:], ckT[:], -1.0, 1.0, ALU.mult, ALU.add).then_inc(*hgp_dve.did(1, "k"))
                for i in range(2):
                    for c in range(TILES):
                        n, t0 = tile_len(c), tile_at(c)
                        v.tensor_tensor_scan(cbT[:, i, t0:t0 + n], ones[:, 0:n], cbT[:, i, t0:t0 + n], 0.0, ALU.mult, ALU.add)\
                            .then_inc(*hgp_dve.did(1, f"b{i}_{c}"))

            def gdn(c, p, ph):
                n, t0 = tile_len(c), tile_at(c)
                last = levels_of(c) - 1
                pe_, act_, pool_ = gdn_pe[p], gdn_act[p], gdn_pool[p]
                g2 = slice(4 * c + 2 * p, 4 * c + 2 * p + 2)
                Pb, Qb = PAIR_BANKS[p]

                def T(i):
                    return Tp(i, p)

                def did(name):
                    return gdn_dve[p].did(c, name)

                def ready():
                    settle(gdn_dve[p])

                def gate(r, h):
                    return gv[0:n, r, g2.start + h:g2.start + h + 1]

                if ph == "rows":
                    v.wait_ge(*pe_.at(c, "rows"))
                    ready()
                    v.tensor_tensor(T(4)[0:n], half_of(Pb, 1)[0:n], cols(gv[0:n, 0, g2], P), ALU.mult).then_inc(*did("vb"))
                    v.wait_ge(*gate_act.at(0, "ekd"))
                    v.tensor_tensor(T(3)[0:n], half_of(Pb, 0)[0:n], cols(gv[0:n, 6, g2], P), ALU.mult).then_inc(*did("kd"))
                elif ph == "decay":
                    v.wait_ge(*act_.at(c, "gbe"))
                    ready()
                    for h in range(2):
                        q = v.tensor_scalar(T(0)[0:n, h, 0:n], T(6)[0:n, h, 0:n], gate(2, h), 0.0, ALU.subtract, ALU.min)
                    q.then_inc(*did("gd"))
                elif ph == "L":
                    v.wait_ge(*pe_.at(c, "kk"))
                    v.wait_ge(*pool_.at(c, "bPT"))
                    v.tensor_tensor(T(10)[0:n, :, 0:n], half_of(Pb, 0)[0:n, :, 0:n], T(1)[0:n, :, 0:n], ALU.mult).then_inc(*did("LT"))
                    v.tensor_tensor(T(11)[0:n, :, 0:n], half_of(Pb, 1)[0:n, :, 0:n], T(0)[0:n, :, 0:n], ALU.mult).then_inc(*did("QKT"))
                    ready()
                    v.tensor_tensor(T(5)[0:n, :, 0:n], T(10)[0:n, :, 0:n], over(lev[0:n, 0, 0:n], 2), ALU.mult).then_inc(*did("Ut"))
                    ready()
                    v.tensor_tensor(T(5)[0:n, :, 0:n], over(ident[0:n, 0:n], 2), T(5)[0:n, :, 0:n], ALU.subtract).then_inc(*did("U0"))
                elif ph[0] == "X":
                    l = int(ph[1:])
                    Rt, Rx = (half_of(b, 0) for b in level_banks(p, l))
                    if l < last:
                        v.wait_ge(*pe_.at(c, f"X{l}"))
                        ready()
                        v.scalar_tensor_tensor(T(2)[0:n, :, 0:n], Rx[0:n, :, 0:n], -1.0, T(2)[0:n, :, 0:n], ALU.mult, ALU.add)\
                            .then_inc(*did(f"X{l}"))
                    else:
                        v.wait_ge(*pe_.at(c, "ks"))
                        ready()
                        for h in range(2):
                            q = v.scalar_tensor_tensor(T(6)[0:n, h, :], Rx[0:n, h, :], gate(4, h), T(4)[0:n, h, :], ALU.mult, ALU.subtract)
                        q.then_inc(*did("r"))
                    v.wait_ge(*pe_.at(c, f"U{l}"))
                    v.scalar_tensor_tensor(T(5)[0:n, :, 0:n], Rt[0:n, :, 0:n], -1.0, T(5)[0:n, :, 0:n], ALU.mult, ALU.add)\
                        .then_inc(*did(f"U{l}"))
                elif ph == "o":
                    S = heads(Sa[:, 1 if c == TILES - 1 else 0, :])[:, 2 * p:2 * p + 2, :]
                    Rx = half_of(level_banks(p, last)[1], 0)
                    v.wait_ge(*pe_.at(c, "S"))
                    for h in range(2):
                        q = v.scalar_tensor_tensor(S[:, h, :], S[:, h, :], gv[:, 5, g2.start + h:g2.start + h + 1], Rx[:, h, :], ALU.mult, ALU.add)
                    q.then_inc(*did("S"))
                elif ph == "on":
                    o = qkvT[:, 2 * p:2 * p + 2, t0:t0 + n]
                    v.wait_ge(*act_.at(c, "exp"))
                    v.scalar_tensor_tensor(o, o, col("a_norm"), T(6)[:, :, 0:n], ALU.mult, ALU.mult).then_inc(*did("on"))
                elif ph == "oz":
                    o = qkvT[:, 2 * p:2 * p + 2, t0:t0 + n]
                    v.wait_ge(*gdn_dve[p].at(c, "on"))
                    v.wait_ge(*post_act.at(G_OF[("z", 2 * p + 1)], "silu"))
                    v.tensor_tensor(o, o, zT[:, 2 * p:2 * p + 2, t0:t0 + n], ALU.mult).then_inc(*gdn_oz[p].did(c, "oz"))

            def hg(c, ph):
                n, t0 = tile_len(c), tile_at(c)
                d4 = DD.rearrange("p (a b i) -> p a b i", a=2, b=2)
                aq = att.rearrange("p a b i -> p (a b) i")[0:n, :, 0:n]
                dq = heads(DD)[0:n, :, 0:n]
                D_ = lambda name: hg_dve.did(c, name)
                def parts(ap, s):
                    return ap.rearrange("p i (b h r) -> p i b h r", h=2, r=s)

                def exponents(l):
                    s = 1 << (l - 1)
                    bb, E = parts(cbT[:, :, t0:t0 + n], s), parts(hE[:, :, 0:n], s)
                    ref = bb[:, :, :, 0, s - 1:s].to_broadcast([P, 2, n // (2 * s), s])
                    if l > 1:
                        v.wait_ge(*hg_pool.at(c, f"k{l - 1}"))
                    settle(hg_dve)
                    v.tensor_tensor(E[:, :, :, 0, :], ref, bb[:, :, :, 0, :], ALU.subtract).then_inc(*D_(f"dk{l}"))
                    v.tensor_tensor(E[:, :, :, 1, :], bb[:, :, :, 1, :], ref, ALU.subtract).then_inc(*D_(f"dq{l}"))

                def keep(l):
                    v.wait_ge(*hg_pe.at(c, f"A{l}"))
                    settle(hg_dve)
                    if l:
                        v.copy_predicated(aq, over(lev[0:n, l - 1, 0:n].bitcast(U32), HEADS), dq).then_inc(*D_(f"att{l}"))
                    else:
                        v.tensor_tensor(aq, dq, over(ident[0:n, 0:n], HEADS), ALU.mult).then_inc(*D_("att0"))

                if ph == "v":
                    if c:
                        v.wait_ge(*hg_pe.at(c - 1, "S"))
                    else:
                        v.wait_ge(*hgp_dve.at(1, f"b1_{TILES - 1}"))
                        v.wait_ge(const_ready, CONSTS)
                        v.wait_ge(*post_act.at(G_OF[("c_q", 1)], "silu"))
                    for par_ in range(2):
                        r = slice(64 * par_, 64 * par_ + 64)
                        q = v.tensor_copy(hQ[r, :, par_, 0:n], cqT[r, :, t0:t0 + n])
                    q.then_inc(*D_("q0"))
                    exponents(1)
                elif ph[0] == "b":
                    l = int(ph[1:])
                    s = 1 << (l - 1)
                    v.wait_ge(*hg_act.at(c, f"E{l}"))
                    v.wait_ge(*hg_pe.at(c, f"A{l - 1}"))
                    for par_, nm in enumerate(("qa", "qb")):
                        r = slice(64 * par_, 64 * par_ + 64)
                        dst = parts(hQ[r, :, par_, 0:n], s)[:, :, :, 1, :]
                        src = parts(cqT[r, :, t0:t0 + n], s)[:, :, :, 1, :]
                        v.tensor_tensor(dst, src, parts(hE[r, :, 0:n], s)[:, :, :, 1, :], ALU.mult).then_inc(*D_(f"{nm}{l}"))
                    keep(l - 1)
                elif ph[0] == "a" and ph != "a0" and int(ph[1:]) < levels_of(c):
                    exponents(int(ph[1:]) + 1)
                elif ph == "kd":
                    keep(levels_of(c))
                elif ph == "o":
                    v.wait_ge(*hg_act.at(c, "osq"))
                    Sx = Sc[:, 1 if c == TILES - 1 else 0]
                    for i in range(2):
                        for par_ in range(2):
                            r = slice(64 * par_, 64 * par_ + 64)
                            v.scalar_tensor_tensor(Sx[r, i, r], Sx[r, i, r], small[r, 60 + i:61 + i], d4[r, 1, i, r], ALU.mult,
                                                   ALU.add).then_inc(*D_(f"S{par_}{i}"))

                elif ph == "on":
                    o = cqT[:, :, t0:t0 + n]
                    v.wait_ge(*hg_act.at(c, "exp"))
                    v.scalar_tensor_tensor(o, o, col("c_norm"), hE[:, :, 0:n], ALU.mult, ALU.mult).then_inc(*D_("on"))
                elif ph == "oz":
                    o = cqT[:, :, t0:t0 + n]
                    v.wait_ge(*hg_dve.at(c, "on"))
                    v.wait_ge(*post_act.at(G_OF[("c_g", 1)], "silu"))
                    v.tensor_tensor(o, o, cgT[:, :, t0:t0 + n], ALU.mult).then_inc(*hg_oz.did(c, "oz"))

            def mixed(j):
                return qkvT[:, j, :] if j < 4 else gateT[:, j - 4, :] if j < 6 else cqT[:, j - 6, :]

            def mix_out():
                for j in range(8):
                    v.wait_ge(*mo_act.at(j, "hi"))
                    v.tensor_tensor(XL[:, j, :], mixed(j), XH[:, j, :].bitcast(F32), ALU.subtract).then_inc(*mo_dve.did(j, "lo"))

            def mem():
                for k in range(KC):
                    v.wait_ge(*mem_act.at(1 + k, "hi"))
                    v.scalar_tensor_tensor(memL[:, k, :], pm[:, 2 + k % 2, 0:N_MEM], col("mem", k), memH[:, k, :].bitcast(F32),
                                           ALU.mult, ALU.subtract).then_inc(*mem_dve.did(k, "lo"))

            def attention(c):
                n = tile_len(c)
                s = pm[0:n, 0:2, :].rearrange("p b (h m) -> p (b h) m", m=N_MEM)
                v.wait_ge(*at_pe.at(c, "s"))
                st = astat[0:n, c, :]
                v.reduce_max(st[:, 0:4], s, AX_X).then_inc(*at_dve.did(c, "max"))
                settle(at_dve)
                v.tensor_scalar(st[:, 4:8], st[:, 0:4], -1.0 / 16, None, ALU.mult).then_inc(*at_dve.did(c, "nmax"))
                v.wait_ge(*at_act.at(c, "exp3"))
                v.reciprocal(st[:, 0:4], st[:, 8:12]).then_inc(*at_dve.did(c, "rec"))
                settle(at_dve)
                v.tensor_tensor(prob[0:n], prob[0:n], cols(st[:, 0:4], N_MEM), ALU.mult).then_inc(*at_dve.did(c, "norm"))

            def pv():
                for j in range(8):
                    b = 2 * (j % 2)
                    v.wait_ge(*pv_act.at(j, "hi"))
                    v.tensor_tensor(XL[:, j, 0:PROMPT], pm[:, b, 0:PROMPT], XH[:, j, 0:PROMPT].bitcast(F32), ALU.subtract)\
                        .then_inc(*pv_dve.did(j, "lo"))
                    v.wait_ge(*pv_act.at(j, "his"))
                    v.tensor_tensor(XL[:, j, S0:TOK], pm[:, b + 1, 0:SAMPLE], XH[:, j, S0:TOK].bitcast(F32), ALU.subtract)\
                        .then_inc(*pv_dve.did(j, "los"))

            def finish():
                v.wait_ge(*fin_pe.at(0, "st"))
                v.wait_ge(slot_done, len(SLOTS))
                v.tensor_copy(frows[0:88], B[0:88, 0:256].rearrange("p (r n) -> p r n", r=2)).then_inc(*fin_dve.did(0, "st"))

            handlers = {"start": start, "square": square, "split": split, "post": post, "gate_rows": gate_rows, "l2exp": l2exp,
                        "rg": rg, "hg_prep": hg_prep, "gdn": gdn, "hg": hg, "mix_out": mix_out, "mem": mem, "att": attention,
                        "pv": pv, "finish": finish}
            for what, *args in SCHED:
                if what in handlers:
                    handlers[what](*args)

        @block.scalar
        def _(act):
            def f(out, in_, fn, **kw):
                return act.activation(out, in_, fn, **kw)

            done_slots = [0]

            def split_weights(last):
                while done_slots[0] <= min(last, len(SLOTS) - 1):
                    n = done_slots[0]
                    size = P * SLOT_K["down"][SLOTS[n][1]] if OUTS[SLOTS[n][0]][0] == "down" else KC * P
                    act.wait_ge(w_loaded[n % RAW], 16 * (n // RAW + 1))
                    if n >= HL:
                        act.wait_ge(slot_done, n - HL + 1)
                    f(WH[:, n % HL, 0:size], raw[:, n % RAW, 0:size], ACT.Copy).then_inc(w_high, 1)
                    done_slots[0] += 1

            def start():
                for t, r0, src in PARAMS:
                    act.dma_start(par_nat[r0:r0 + src.shape[0], t, :], src).then_inc(par_loaded, 16)
                for h in range(2):
                    act.dma_start(par_nat[109:110, 0, 64 * h:64 * h + 64], c_norm).then_inc(par_loaded, 16)
                act.dma_start(row8[:, 0:4], a_A_log).then_inc(par_loaded, 16)
                act.dma_start(row8[:, 4:8], a_dt_bias).then_inc(par_loaded, 16)
                split_weights(1)

            def square(s, k):
                if s == 0:
                    act.wait_ge(*start_dve.at(0, f"x{k}"))
                    act.wait_ge(const_ready, CONSTS)
                else:
                    act.wait_ge(*post_dve.at((G_WOUT, G_WO, G_DOWN)[s - 1] + k, "evac"))
                if k == 0:
                    if s:
                        act.wait_ge(*norm_pe.at(s - 1, "ss"))
                    f(NS[:], xT[:, k, :], ACT.Square).then_inc(*feed_act.did(s, f"sq{k}"))
                else:
                    if k >= 2:
                        act.wait_ge(*feed_dve.at(s, f"ns{k - 1}" if k == 2 else f"ns{k - 2}"))
                    f(SQ[:, k % 2, :], xT[:, k, :], ACT.Square).then_inc(*feed_act.did(s, f"sq{k}"))

            def split(s, k):
                if s == 0:
                    act.wait_ge(*start_dve.at(0, f"x{k}"))
                    act.wait_ge(const_ready, CONSTS)
                if k == 0:
                    if s == 1:
                        act.wait_ge(slot_done, LAST_SLOT[G_WK - 1] + 1)
                    if s == 2:
                        act.wait_ge(slot_done, LAST_SLOT[G_UP - 1] + 1)
                        act.wait_ge(stored, 16 * (MIX_STORES + 2))
                f(XH[:, k, :], xT[:, k, :], ACT.Identity, scale=col(("mix", "attn", "ffn")[s], k)).then_inc(*feed_act.did(s, f"hi{k}"))

            def norm(s):
                act.wait_ge(*norm_pe.at(s, "ss"))
                if s:
                    act.wait_ge(*post_dve.at((0, G_WOUT, G_WO)[s] - 1, "evac"))
                f(R[:].rearrange("p (h t) -> p h t", h=2), pm[:, 0:2, 0:HALF], ACT.Ln, bias=EPS, scale=1.0 / D).then_inc(*norm_act.did(s, "ln"))
                act.wait_ge(*norm_act.at(s, "ln"))
                f(R[:], R[:], ACT.Exp, scale=-0.5).then_inc(*norm_act.did(s, "exp"))

            def post(g):
                kind, i = OUTS[g]
                split_weights(LAST_SLOT[g] + HL)
                if kind == "qkv":
                    act.wait_ge(*post_dve.at(g, "tap3"))
                    f(qkvT[:, i, :], qkvT[:, i, :], ACT.Silu).then_inc(*post_act.did(g, "silu"))
                if kind == "c_q":
                    act.wait_ge(*post_dve.at(g, "evac"))
                    f(cqT[:, i, :], cqT[:, i, :], ACT.Silu).then_inc(*post_act.did(g, "silu"))
                if kind == "c_f":
                    act.wait_ge(*post_dve.at(g, "evac"))
                    f(ckT[:, i, :], ckT[:, i, :], ACT.Sigmoid).then_inc(*post_act.did(g, "sig"))
                if kind in ("z", "c_g"):
                    act.wait_ge(*post_dve.at(g, "evac"))
                    to = {"z": zT, "c_g": cgT}[kind][:, i, :]
                    f(to, to, ACT.Silu).then_inc(*post_act.did(g, "silu"))
                if kind == "b_gate":
                    act.wait_ge(*post_dve.at(g, "evac"))
                    f(gateT[:, i, :], gateT[:, i, :], ACT.Gelu_apprx_tanh).then_inc(*post_act.did(g, "gelu"))
                if kind == "up_gate":
                    act.wait_ge(*post_dve.at(g, "tap2"))
                    f(fg[:], fg[:], ACT.Silu).then_inc(*post_act.did(g, "silu"))
                if kind == "up_val":
                    act.wait_ge(*post_dve.at(g, "prod"))
                    f(FH[:, i, :], fv[:], ACT.Copy).then_inc(*post_act.did(g, "hi"))

            def gv_(r):
                return gv[:, r, 0:TILES * HEADS]

            def gate_rows():
                act.wait_ge(*gate_dve.at(0, "rows4"))
                f(gv_(0).rearrange("p (c h) -> p c h", h=4), gv8.rearrange("p (c h) -> p c h", h=8)[:, :, 0:4], ACT.Sigmoid)\
                    .then_inc(*gate_act.did(0, "beta"))
                act.wait_ge(*start_dve.at(0, "pad"))
                f(small[:, 44:48], small[:, 0:4], ACT.Exp).then_inc(*gate_act.did(0, "eA"))
                act.wait_ge(*gate_dve.at(0, "neg"))
                f(gv_(4), gv_(4), ACT.Exp, scale=-1.0).then_inc(*gate_act.did(0, "exp"))
                act.wait_ge(*gate_act.at(0, "exp"))
                f(gv_(4), gv_(4), ACT.Ln, bias=1.0).then_inc(*gate_act.did(0, "ln"))
                act.wait_ge(*gate_dve.at(0, "gc"))
                f(gv_(3), gv_(2), ACT.Exp).then_inc(*gate_act.did(0, "egc"))
                act.wait_ge(*gate_dve.at(0, "kd"))
                f(gv8, gv8, ACT.Exp).then_inc(*gate_act.did(0, "ekd"))

            def rg_tmp(i, n=1):
                return tmp[:].rearrange("p a b -> p (a b)")[:, i * TOK:(i + n) * TOK]

            def l2sq(i):
                if i >= 2:
                    act.wait_ge(*l2_pe.at(i - 2, "ss"))
                else:
                    act.wait_ge(*feed_dve.at(0, f"ns{KC - 1}"))
                act.wait_ge(*post_act.at(G_OF[("qkv", i)], "silu"))
                f(SQ[:, i % 2, :], qkvT[:, i, :], ACT.Square).then_inc(*l2_act.did(i, "sq"))

            def l2(i):
                act.wait_ge(*l2_pe.at(i, "ss"))
                f(rg_tmp(i).rearrange("p (h t) -> p h t", h=2), pm[:, 2 * (i % 2):2 * (i % 2) + 2, 0:HALF], ACT.Ln, bias=EPS)\
                    .then_inc(*l2_act.did(i, "ln"))

            def l2exp():
                act.wait_ge(*l2_act.at(7, "ln"))
                f(rg_tmp(0, 4), rg_tmp(0, 4), ACT.Exp, scale=-0.5, bias=LN_SCALE).then_inc(*l2_act.did(8, "exp0"))
                f(rg_tmp(4, 4), rg_tmp(4, 4), ACT.Exp, scale=-0.5).then_inc(*l2_act.did(8, "exp1"))

            def rg(part):
                if part == 0:
                    act.wait_ge(*rg_dve.at(0, "abs"))
                    f(small[:, 50:52], small[:, 50:52], ACT.Exp, scale=-1.0).then_inc(*rg_act.did(0, "exp"))
                    act.wait_ge(*rg_act.at(0, "exp"))
                    f(small[:, 50:52], small[:, 50:52], ACT.Ln, bias=1.0).then_inc(*rg_act.did(0, "ln"))
                    act.wait_ge(*l2_dve.at(7, "n"))
                    for i in range(2):
                        act.wait_ge(*rg_pe.at(i, "gates"))
                        f(rg_tmp(i).rearrange("p (h t) -> p h t", h=2), pm[:, 0:2, 0:HALF], ACT.Sigmoid, bias=col("b_r", i)).then_inc(*rg_act.did(1 + i, "r"))
                        f(rg_tmp(2 + i).rearrange("p (h t) -> p h t", h=2), pm[:, 2:4, 0:HALF], ACT.Sigmoid, bias=col("b_i", i)).then_inc(*rg_act.did(1 + i, "i"))
                if part == 1:
                    act.wait_ge(*rg_dve.at(0, "c8n"))
                    act.wait_ge(*rg_act.at(2, "i"))
                    for i in range(2):
                        f(rg_tmp(4 + i), rg_tmp(i), ACT.Exp, scale=small[:, 52 + i:53 + i]).then_inc(*rg_act.did(4 + i, "a"))
                        f(rg_tmp(6 + i), rg_tmp(i), ACT.Tanh, scale=small[:, 54 + i:55 + i]).then_inc(*rg_act.did(4 + i, "th"))
                if part == 2:
                    act.wait_ge(*rg_dve.at(2, "m2"))
                    f(rg_tmp(6, 2), rg_tmp(6, 2), ACT.Sqrt).then_inc(*rg_act.did(6, "mult"))

            def hg_prep():
                act.wait_ge(*hgp_dve.at(0, "e0"))
                f(small[:, 56:58], small[:, 56:58], ACT.Exp).then_inc(*hgp_act.did(0, "e"))
                act.wait_ge(*hgp_dve.at(1, "f"))
                f(cbT[:], ckT[:], ACT.Ln).then_inc(*hgp_act.did(1, "lf"))

            def gdn(c, p, ph):
                n, t0 = tile_len(c), tile_at(c)
                last = levels_of(c) - 1
                pe_, dve, own = gdn_pe[p], gdn_dve[p], gdn_act[p]

                def T(i):
                    return Tp(i, p)

                if ph == "rows":
                    act.wait_ge(*pe_.at(c, "gb"))
                    if c:
                        act.wait_ge(*dve.at(c - 1, "on"))
                    else:
                        act.wait_ge(*rg_dve.at(4, "y"))
                    to = tmp[:, 6:9:2, 256 * p:256 * p + 256].rearrange("p x (h i) -> p x h i", h=2)
                    src = PAIR_BANKS[p][1].rearrange("p (x h i) -> p x h i", x=2, h=2)
                    if n == P:
                        f(tmp[:, 6:9:2, 256 * p:256 * p + 256], PAIR_BANKS[p][1].rearrange("p (x i) -> p x i", x=2), ACT.Copy)\
                            .then_inc(*own.did(c, "gbe"))
                    else:
                        f(to[:, :, :, 0:n], src[:, :, :, 0:n], ACT.Copy).then_inc(*own.did(c, "gbe"))
                elif ph == "decay":
                    act.wait_ge(*dve.at(c, "gd"))
                    f(T(0)[0:n, :, 0:n], T(0)[0:n, :, 0:n], ACT.Exp).then_inc(*own.did(c, "PT"))
                    f(T(9)[:, :, 0:n], T(6)[:, :, 0:n], ACT.Exp).then_inc(*own.did(c, "egb"))
                elif ph == "turn":
                    act.wait_ge(*pe_.at(c, "X0"))
                    f(T(2)[0:n, :, 0:n], half_of(PAIR_BANKS[p][1], 0)[0:n, :, 0:n], ACT.Copy).then_inc(*own.did(c, "X0"))
                elif ph[0] == "T":
                    l = int(ph[1:])
                    act.wait_ge(*pe_.at(c, f"T{l}"))
                    act.wait_ge(*dve.at(c, "U0"))
                    f(T(0)[0:n, :, 0:n], half_of(level_banks(p, l)[0], 0)[0:n, :, 0:n], ACT.Copy).then_inc(*own.did(c, f"T{l}"))
                elif ph == "vnew":
                    act.wait_ge(*pe_.at(c, "vnew"))
                    f(T(7)[0:n], half_of(level_banks(p, last)[1], 0)[0:n], ACT.Copy, scale=-1.0).then_inc(*own.did(c, "vn"))
                elif ph == "o":
                    Rt = half_of(level_banks(p, last)[0], 0)
                    act.wait_ge(*pe_.at(c, "o"))
                    f(qkvT[:, 2 * p:2 * p + 2, t0:t0 + n], Rt[:, :, 0:n], ACT.Copy).then_inc(*own.did(c, "o"))
                    f(T(0)[:, :, 0:n], Rt[:, :, 0:n], ACT.Square).then_inc(*own.did(c, "osq"))
                    if c >= TILES - 2:
                        r, to = (0, pa_S) if c == TILES - 2 else (1, sa_S)
                        act.wait_ge(*dve.at(c, "S"))
                        act.dma_start(to[0, 0, 2 * p:2 * p + 2].rearrange("h k v -> k h v"), heads(Sa[:, r, :])[:, 2 * p:2 * p + 2])\
                            .then_inc(stored, 16)
                elif ph == "ss":
                    act.wait_ge(*pe_.at(c, "ss"))
                    f(T(6)[:, :, 0:n], half_of(level_banks(p, last)[0], 1)[:, :, 0:n], ACT.Ln, bias=EPS, scale=1.0 / P).then_inc(*own.did(c, "ln"))
                    act.wait_ge(*own.at(c, "ln"))
                    f(T(6)[:, :, 0:n], T(6)[:, :, 0:n], ACT.Exp, scale=-0.5).then_inc(*own.did(c, "exp"))

            def hg(c, ph):
                n, t0 = tile_len(c), tile_at(c)
                D_ = lambda name: hg_act.did(c, name)
                d4 = DD.rearrange("p (a b i) -> p a b i", a=2, b=2)
                d2 = DD[:, 0:256].rearrange("p (a i) -> p a i", a=2)

                def E(l):
                    act.wait_ge(*hg_dve.at(c, f"dq{l}"))
                    f(hE[:, :, 0:n], hE[:, :, 0:n], ACT.Exp).then_inc(*D_(f"E{l}"))

                if ph == "v":
                    act.wait_ge(*hg_pe.at(c, "v"))
                    act.wait_ge(const_ready, CONSTS)
                    f(vpad[0:n, :, 0, 0:64], d2[0:n, :, 0:64], ACT.Copy).then_inc(*D_("v0"))
                    f(vpad[0:n, :, 1, 64:128], d2[0:n, :, 64:128], ACT.Copy).then_inc(*D_("v1"))
                    E(1)
                elif ph[0] == "a" and ph != "a0" and int(ph[1:]) < levels_of(c):
                    E(int(ph[1:]) + 1)
                elif ph == f"a{levels_of(c)}":
                    act.wait_ge(*hg_pool.at(c, f"k{levels_of(c)}"))
                    act.wait_ge(*hg_dve.at(c, f"qb{levels_of(c)}"))
                    for i in range(2):
                        f(hE[:, i, 0:n], cbT[:, i, t0:t0 + n], ACT.Exp, scale=-1.0, bias=cbT[:, i, t0 + n - 1:t0 + n]).then_inc(*D_(f"ek{i}"))
                elif ph == "kdt":
                    act.wait_ge(*hg_pool.at(c, "kd"))
                    f(hE[:, :, 0:n], cbT[:, :, t0:t0 + n], ACT.Exp).then_inc(*D_("eq"))
                    f(small[:, 60:62], cbT[:, :, t0 + n - 1], ACT.Exp).then_inc(*D_("eb"))
                    act.wait_ge(*hg_pe.at(c, "kd"))
                    f(kdt[0:n], d2[0:n], ACT.Copy).then_inc(*D_("kdt"))
                elif ph == "o":
                    act.wait_ge(*hg_pe.at(c, "o"))
                    act.wait_ge(*hg_pe.at(c, "S"))
                    f(cqT[:, :, t0:t0 + n], d4[:, 0, :, 0:n], ACT.Copy).then_inc(*D_("o"))
                    f(hE[:, :, 0:n], d4[:, 0, :, 0:n], ACT.Square).then_inc(*D_("osq"))
                    if c >= TILES - 2:
                        r, to = (0, pc_S) if c == TILES - 2 else (1, sc_S)
                        act.wait_ge(*hg_dve.at(c, "S11"))
                        for par_ in range(2):
                            s = slice(64 * par_, 64 * par_ + 64)
                            act.dma_start(to[0, 0].rearrange("(i q) k v -> q k i v", q=2)[par_], Sc[s, r, :, s]).then_inc(stored, 16)

                elif ph == "ss":
                    act.wait_ge(*hg_pe.at(c, "ss"))
                    f(hE[:, :, 0:n], d4[:, 0, :, 0:n], ACT.Ln, bias=EPS, scale=1.0 / 64).then_inc(*D_("ln"))
                    act.wait_ge(*hg_act.at(c, "ln"))
                    f(hE[:, :, 0:n], hE[:, :, 0:n], ACT.Exp, scale=-0.5).then_inc(*D_("exp"))

            def mixed(j):
                return qkvT[:, j, :] if j < 4 else gateT[:, j - 4, :] if j < 6 else cqT[:, j - 6, :]

            def mix_out():
                act.wait_ge(slot_done, LAST_SLOT[G_LAST_IN] + 1)
                for j in range(8):
                    if j < 4:
                        act.wait_ge(*gdn_oz[j // 2].at(TILES - 1, "oz"))
                    elif j < 6:
                        act.wait_ge(*rg_dve.at(j - 1, "y"))
                    else:
                        act.wait_ge(*hg_oz.at(TILES - 1, "oz"))
                    f(XH[:, j, :], mixed(j), ACT.Copy).then_inc(*mo_act.did(j, "hi"))
                act.wait_ge(*mo_pe.at(0, "st"))
                rows = st_rows[0:44, 0:256].rearrange("p (r n) -> p r n", r=2)
                f(rows, pm[0:44, 0:2, 0:P], ACT.Copy).then_inc(*mo_act.did(8, "st"))
                act.wait_ge(*mo_act.at(8, "st"))
                for r, (ta, tb, th) in enumerate(((pa_conv, pb_conv, pb_h), (sa_conv, sb_conv, sb_h))):
                    act.dma_start(ta[0, 0].rearrange("t (i p) -> (t i) p", p=P), rows[0:36, r, :]).then_inc(stored, 16)
                    act.dma_start(tb[0, 0].rearrange("t (i p) -> (t i) p", p=P), rows[36:42, r, :]).then_inc(stored, 16)
                    act.dma_start(th[0, 0].rearrange("(i p) -> i p", p=P), rows[42:44, r, :]).then_inc(stored, 16)

            def mem():
                act.wait_ge(mem_loaded, 16)
                act.wait_ge(stored, 16 * MIX_STORES)
                act.wait_ge(*mo_dve.at(7, "lo"))
                for t in range(2):
                    f(Kn[:, t, :], nat[:, t, :], ACT.Square, accum_out=mstat[:, t:t + 1]).then_inc(*mem_act.did(0, f"sq{t}"))
                act.wait_ge(*mem_act.at(0, "sq1"))
                f(mstat[:, 2:4], mstat[:, 0:2], ACT.Ln, bias=EPS, scale=1.0 / D).then_inc(*mem_act.did(0, "ln"))
                act.wait_ge(*mem_act.at(0, "ln"))
                f(mstat[:, 4:6], mstat[:, 2:4], ACT.Exp, scale=-0.5).then_inc(*mem_act.did(0, "exp"))
                for k in range(KC):
                    act.wait_ge(*mem_pe.at(k, "t"))
                    f(memH[:, k, :], pm[:, 2 + k % 2, 0:N_MEM], ACT.Identity, scale=col("mem", k)).then_inc(*mem_act.did(1 + k, "hi"))

            def kt():
                act.wait_ge(*post_dve.at(G_OF[("w_v", 3)], "evac"))
                act.dma_start(mem_k_out[0, 0].rearrange("(c p) h d -> p c (h d)", p=P), Kn[:]).then_inc(stored, 16)
                act.dma_start(mem_v_out[0, 0].rearrange("(c p) h d -> p c (h d)", p=P), Vn[:]).then_inc(stored, 16)
                for j in range(8):
                    act.wait_ge(*kt_pe.at(j, "t"))
                    d = 2 * (j % 4)
                    f(kT[:, j // 4, d:d + 2, :], pm[:, j % 4, :].rearrange("p (d m) -> p d m", d=2), ACT.Copy).then_inc(*kt_act.did(j, "t"))

            def attention(c):
                n = tile_len(c)
                act.wait_ge(*at_dve.at(c, "nmax"))
                if c:
                    act.wait_ge(*at_pe.at(c - 1, "t"))
                for h in range(HEADS):
                    f(prob[0:n, h, :], pm[0:n, h // 2, (h % 2) * 256:(h % 2 + 1) * 256], ACT.Exp, scale=1.0 / 16,
                      bias=astat[0:n, c, 4 + h:5 + h], accum_out=astat[0:n, c, 8 + h:9 + h]).then_inc(*at_act.did(c, f"exp{h}"))
                act.wait_ge(*at_pe.at(c, "t"))
                for t in range(2):
                    q = f(PT[:, t, :, c * P:c * P + n], heads(pm[:, 2 + t, :])[:, :, 0:n], ACT.Copy)
                q.then_inc(*at_act.did(c, "pt"))

            def pv():
                act.wait_ge(slot_done, LAST_SLOT[G_WO - 1] + 1)
                for j in range(8):
                    b = 2 * (j % 2)
                    act.wait_ge(*pv_pe.at(j, "o"))
                    f(XH[:, j, 0:PROMPT], pm[:, b, 0:PROMPT], ACT.Copy).then_inc(*pv_act.did(j, "hi"))
                    f(XH[:, j, S0:TOK], pm[:, b + 1, 0:SAMPLE], ACT.Copy).then_inc(*pv_act.did(j, "his"))

            def finish():
                act.wait_ge(*fin_pe.at(0, "ss"))
                act.wait_ge(slot_done, len(SLOTS))
                parts = [(slice(0, P), slice(0, 4)), (slice(0, SAMPLE), slice(4, 5))]
                sums = A[:, 0:2 * TILES].rearrange("p (c e) -> p c e", e=2)[:, :, 0]
                for p, c in parts:
                    q = f(fstat[p, c], sums[p, c], ACT.Ln, bias=EPS, scale=1.0 / D)
                q.then_inc(*fin_act.did(0, "ln"))
                act.wait_ge(*fin_act.at(0, "ln"))
                for p, c in parts:
                    q = f(fstat[p, c], fstat[p, c], ACT.Exp, scale=-0.5)
                q.then_inc(*fin_act.did(0, "exp"))
                act.wait_ge(*fin_dve.at(0, "st"))
                for r, to in enumerate((pf_conv, sf_conv)):
                    act.dma_start(to[0, 0].rearrange("t (c p) -> (t c) p", p=P), frows[0:88, r, :]).then_inc(stored, 16)
                act.wait_ge(*fin_act.at(0, "exp"))
                for c in range(TILES):
                    n = tile_len(c)
                    act.wait_ge(*fin_pe.at(1 + c, "y"))
                    f(yrow[0:n, c, :].rearrange("p (b n) -> p b n", b=2), pg[c % 2][0:n], ACT.Identity,
                      scale=fstat[0:n, c:c + 1]).then_inc(*fin_act.did(1 + c, "y"))
                    act.wait_ge(*fin_act.at(1 + c, "y"))
                    to = y_prompt[0, c * P:c * P + n, :] if c < TILES - 1 else y_sample[0]
                    act.dma_start(to, yrow[0:n, c, :]).then_inc(stored, 16)

            handlers = {"start": start, "square": square, "split": split, "norm": norm, "post": post, "l2": l2, "l2sq": l2sq, "l2exp": l2exp,
                        "gate_rows": gate_rows, "rg": rg, "hg_prep": hg_prep, "gdn": gdn, "hg": hg, "mix_out": mix_out,
                        "mem": mem, "kt": kt, "att": attention, "pv": pv, "finish": finish}
            for what, *args in SCHED:
                if what in handlers:
                    handlers[what](*args)

        @block.gpsimd
        def _(pool):
            made = [0]

            def link(ins):
                ins.then_inc(const_ready, 1)
                made[0] += 1
                pool.wait_ge(const_ready, made[0])

            done_slots = [0]

            def split_weights(last):
                while done_slots[0] <= min(last, len(SLOTS) - 1):
                    n = done_slots[0]
                    size = P * SLOT_K["down"][SLOTS[n][1]] if OUTS[SLOTS[n][0]][0] == "down" else KC * P
                    pool.wait_ge(w_high, n + 1)
                    pool.tensor_tensor(WL[:, n % HL, 0:size], raw[:, n % RAW, 0:size], WH[:, n % HL, 0:size].bitcast(F32),
                                       ALU.subtract).then_inc(w_low, 1)
                    done_slots[0] += 1

            def select(ap, op, fill, base, pattern, cm):
                return pool.affine_select(out=ap, in_=ap, compare_op=op, fill=fill, base=base, pattern=pattern, channel_multiplier=cm)

            def start():
                link(pool.memset(ident[:], 0.0))
                link(select(ident[:], ALU.not_equal, 1.0, 0, [[-1, P]], 1))
                link(pool.memset(xT[:, :, PROMPT:S0], 0.0))
                link(pool.memset(ones[:], 1.0))
                link(pool.memset(half_ones[:], 0.0))
                link(pool.memset(half_ones[0:64, 0:64], 1.0))
                link(pool.memset(half_ones[64:128, 64:128], 1.0))
                link(pool.memset(upto_m[:], 1.0))
                link(select(upto_m[:], ALU.is_ge, 0.0, 0, [[1, P]], -1))
                link(pool.memset(pre_m[:, :, 0:PRE], 0.0))
                link(pool.memset(wr_bd[:], 0.0))
                link(pool.memset(Sa[:, 0, :], 0.0))
                link(pool.memset(Sc[:], 0.0))
                link(pool.memset(hK[:], 0.0))
                link(pool.memset(lev[:], 0.0))
                for l in range(LEVELS):
                    s = 1 << l
                    w = lev[:, l, :].rearrange("p (b h r) -> p b h r", h=2, r=s)[:, :, 1, :]
                    nb = P // (2 * s)
                    link(pool.memset(w, 1.0))
                    link(select(w, ALU.is_ge, 0.0, 0, [[-2 * s, nb], [0, s]], 1))
                    link(select(w, ALU.is_ge, 0.0, s - 1, [[2 * s, nb], [0, s]], -1))
                assert made[0] == CONSTS, made[0]
                for q in range(2):
                    r = slice(64 * q, 64 * q + 64)
                    for gate, w in enumerate((b_w_r, b_w_i)):
                        pool.dma_start(wr_bd[r, gate, :, r], w[0].rearrange("(i q) a b -> q a i b", q=2)[q]).then_inc(state_loaded, 16)
                    pool.dma_start(Sc[r, 1, :, r], state_c_S[0, 0].rearrange("(i q) k v -> q k i v", q=2)[q]).then_inc(state_loaded, 16)
                pool.dma_start(heads(Sa[:, 1, :]), state_a_S[0, 0].rearrange("h k v -> k h v")).then_inc(state_loaded, 16)
                split_weights(1)

            def post(g):
                split_weights(LAST_SLOT[g] + HL)
                kind, i = OUTS[g]
                if kind == "up_val":
                    pool.wait_ge(*post_act.at(g, "hi"))
                    pool.tensor_tensor(FL[:, i, :], fv[:], FH[:, i, :].bitcast(F32), ALU.subtract).then_inc(*post_pool.did(g, "lo"))

            def gdn(c, p, ph):
                n, t0 = tile_len(c), tile_at(c)
                g2 = slice(4 * c + 2 * p, 4 * c + 2 * p + 2)
                own = gdn_pool[p]

                def T(i):
                    return Tp(i, p)[0:n, :, 0:n]

                def blocks(l):
                    pool.tensor_tensor(T(1), T(10), over(lev[0:n, l, 0:n], 2), ALU.mult).then_inc(*own.did(c, f"B{l}"))

                if ph == "diag":
                    if c:
                        pool.wait_ge(*gdn_pe[p].at(c - 1, "gb"))
                    else:
                        pool.wait_ge(*gate_dve.at(0, "gc"))
                        pool.wait_ge(*gate_act.at(0, "beta"))
                        pool.wait_ge(*l2_pe.at(7, "ss"))
                    for x, (r, name) in enumerate(((2, "dg"), (0, "db"))):
                        pool.tensor_tensor(half_of(SQ[:, p, :], x)[0:n, :, 0:n], over(ident[0:n, 0:n], 2), cols(gv[0:n, r, g2], n),
                                           ALU.mult).then_inc(*own.did(c, name))
                elif ph == "mask":
                    pool.wait_ge(*gdn_act[p].at(c, "PT"))
                    pool.tensor_tensor(T(0), T(0), over(upto_m[0:n, 0:n], 2), ALU.mult).then_inc(*own.did(c, "PTm"))
                    pool.wait_ge(*own.at(c, "PTm"))
                    pool.tensor_tensor(T(1), T(0), T(8), ALU.mult).then_inc(*own.did(c, "bPT"))
                elif ph == "turn":
                    pool.wait_ge(*gdn_dve[p].at(c, "QKT"))
                    blocks(1)
                    pool.wait_ge(*gdn_act[p].at(c, "egb"))
                    qd = Tp(9, p)[:, :, 0:n]
                    pool.tensor_tensor(qd, qkvT[:, 2 * p:2 * p + 2, t0:t0 + n], qd, ALU.mult).then_inc(*own.did(c, "qd"))
                elif ph[0] == "X" and int(ph[1:]) < levels_of(c) - 1:
                    l = int(ph[1:])
                    pool.wait_ge(*gdn_pe[p].at(c, f"T{l}"))
                    blocks(l + 1)

            def hg(c, ph):
                n, t0 = tile_len(c), tile_at(c)
                D_ = lambda name: hg_pool.did(c, name)
                if ph == "v":
                    if c:
                        pool.wait_ge(*hg_pe.at(c - 1, "S"))
                    else:
                        pool.wait_ge(*hgp_dve.at(1, f"b1_{TILES - 1}"))
                    pool.tensor_scalar(hK[:, :, 0:n], ckT[:, :, t0:t0 + n], 1.0, 1.0, ALU.mult, ALU.mult).then_inc(*D_("k0"))
                elif ph[0] == "b":
                    l = int(ph[1:])
                    s = 1 << (l - 1)

                    def first(ap):
                        return ap.rearrange("p i (b h r) -> p i b h r", h=2, r=s)[:, :, :, 0, :]

                    pool.wait_ge(*hg_act.at(c, f"E{l}"))
                    pool.wait_ge(*hg_pe.at(c, f"A{l - 1}"))
                    pool.tensor_tensor(first(hK[:, :, 0:n]), first(ckT[:, :, t0:t0 + n]), first(hE[:, :, 0:n]), ALU.mult).then_inc(*D_(f"k{l}"))
                elif ph == "kd":
                    pool.wait_ge(*hg_act.at(c, "ek1"))
                    pool.wait_ge(*hg_pe.at(c, f"A{levels_of(c)}"))
                    pool.tensor_tensor(hK[:, :, 0:n], ckT[:, :, t0:t0 + n], hE[:, :, 0:n], ALU.mult).then_inc(*D_("kd"))
                elif ph == "kdt":
                    pool.wait_ge(*hg_act.at(c, "eq"))
                    pool.tensor_tensor(hE[:, :, 0:n], cqT[:, :, t0:t0 + n], hE[:, :, 0:n], ALU.mult).then_inc(*D_("qe"))

            handlers = {"start": start, "post": post, "gdn": gdn, "hg": hg}
            for what, *args in SCHED:
                if what in handlers:
                    handlers[what](*args)


_INS = ['x_prompt', 'x_sample', 'cache_mem_k', 'cache_mem_v', 'state_a_conv', 'state_a_S', 'state_b_conv', 'state_b_h',
        'state_c_S', 'state_ffn_conv', 'mem_prompt', 'norm_mix', 'w_in', 'a_conv_w', 'a_A_log', 'a_dt_bias', 'a_norm',
        'b_conv_w', 'b_conv_b', 'b_w_r', 'b_b_r', 'b_w_i', 'b_b_i', 'b_lambda', 'c_lb_logits', 'c_norm', 'w_out',
        'norm_attn', 'norm_mem', 'w_q', 'w_k', 'w_v', 'w_o', 'norm_ffn', 'w_up', 'ffn_conv_w', 'ffn_conv_b', 'w_down',
        'norm_final']
_STATES = [(1, 1, 3, 1536), (1, 1, 4, 128, 128), (1, 1, 3, 256), (1, 1, 256), (1, 1, 4, 64, 64), (1, 1, 2, 5632)]
_OUTS = [(1, 512, 1024), (1, 64, 1024), (1, 1, 256, 4, 256), (1, 1, 256, 4, 256)] + _STATES + _STATES


def kernel(**inputs):
    import numpy as _np
    import concourse.bacc as _bacc
    from concourse import mybir as _mybir
    from concourse.bass_utils import run_bass_kernel_spmd as _run

    nc = _bacc.Bacc("TRN2", target_bir_lowering=False, num_devices=1)
    arrays, args = {}, []
    for name in _INS:
        a = _np.ascontiguousarray(inputs[name])
        arrays[f"in_{name}_dram"] = a
        args.append(nc.dram_tensor(f"in_{name}_dram", a.shape, _mybir.dt.from_np(a.dtype), kind="ExternalInput").ap())
    for i, shape in enumerate(_OUTS):
        args.append(nc.dram_tensor(f"out_{i}_dram", shape, _mybir.dt.float32, kind="ExternalOutput").ap())
    build(nc, *args)
    r = _run(nc, [arrays], core_ids=[0])
    return tuple(r.results[0][f"out_{i}_dram"] for i in range(len(_OUTS)))
```

```python
from contextlib import ExitStack

import concourse.bass as bass
from concourse import mybir

F32 = mybir.dt.float32
F32R = mybir.dt.float32r
U32 = mybir.dt.uint32
ALU = mybir.AluOpType
ACT = mybir.ActivationFunctionType
AX_X = mybir.AxisListType.X

P = 128
D = 1024
KC = D // P
PROMPT = 512
SAMPLE = 64
GAP = 4
TOK = PROMPT + GAP + SAMPLE
HALF = TOK // 2
S0 = PROMPT + GAP
PRE = 3
N_A, N_G, N_B, N_C = 512, 4, 256, 256
HEADS = 4
N_MEM = 256
D_FF = 2816
NF = D_FF // P
EPS = 1e-6
TILES = 5
LEVELS = 7


class Steps:

    def __init__(self, sem, rounds):
        self.sem, self.value, self.made = sem, {}, 0
        for r, names in rounds:
            for name in names:
                assert (r, name) not in self.value
                self.value[(r, name)] = len(self.value) + 1

    def at(self, r, name):
        return self.sem, self.value[(r, name)]

    def did(self, r, name):
        self.made += 1
        assert self.value[(r, name)] == self.made, (r, name)
        return self.sem, 1


def tile_len(c):
    return P if c < TILES - 1 else SAMPLE


def tile_at(c):
    return c * P if c < TILES - 1 else S0


def levels_of(c):
    return LEVELS if c < TILES - 1 else LEVELS - 1


COL = {"mix": 0, "attn": 8, "ffn": 16, "mem": 24, "final": 32, "a_w": 40, "b_w": 88, "b_b": 96, "b_r": 98, "b_i": 100,
       "lam": 102, "lb": 104, "b_h": 106, "a_norm": 108, "c_norm": 109,
       "a_st": 128, "b_st": 164, "f_b": 170, "f_w": 256, "f_w2": 384, "f_st0": 428, "f_st1": 512}
PAR_ROWS = [110, 86, 88, 88, 44]


def outputs_of_products():
    outs = [("gates", 0)]
    outs += [("qkv", i) for i in range(12)]
    for kind in ("b_x", "b_gate", "c_q", "c_f", "c_i"):
        outs += [(kind, i) for i in range(2)]
    outs += [("z", i) for i in range(4)] + [("c_g", i) for i in range(2)]
    outs += [("w_out", i) for i in range(8)]
    outs += [("w_k", i) for i in range(4)] + [("w_v", i) for i in range(4)]
    outs += [("w_q", i) for i in range(8)] + [("w_o", i) for i in range(8)]
    for f in range(NF):
        outs += [("up_gate", f), ("up_val", f)]
    outs += [("down", i) for i in range(8)]
    return outs


OUTS = outputs_of_products()
G_OF = {o: g for g, o in enumerate(OUTS)}
SLOT_K = {"down": [8, 8, 6], "w_k": [4, 4], "w_v": [4, 4]}
SLOTS = [(g, j) for g, (kind, i) in enumerate(OUTS) for j in range(len(SLOT_K.get(kind, [8])))]
FIRST_SLOT, LAST_SLOT = {}, {}
for _n, (_g, _j) in enumerate(SLOTS):
    FIRST_SLOT.setdefault(_g, _n)
    LAST_SLOT[_g] = _n
LOW_BY_DVE = {n for n, (g, j) in enumerate(SLOTS) if OUTS[g][0] in ("w_k", "w_v")}
W_IN_COL = {"gates": 2048, "qkv": 0, "z": 1536, "b_x": 2056, "b_gate": 2312, "c_q": 2568, "c_f": 2824, "c_i": 3080,
            "c_g": 3336}
RAW, HL = 2, 2
X_PIECES = 4
CONV = {"qkv": 4, "b_x": 4, "up_gate": 3, "up_val": 3}


PAIR = {}
for _g, (_kind, _i) in enumerate(OUTS):
    PAIR[_g] = 0 if _kind in ("z", "c_g") else _g % 2 if _g < G_OF[("w_out", 0)] else (_g - G_OF[("w_out", 0)]) % 2
PREV = {g: max([x for x in range(g) if PAIR[x] == PAIR[g]], default=None) for g in PAIR}


def gdn_phases(c):
    out = ["rows", "decay", "mask", "L", "turn"]
    for l in range(1, levels_of(c)):
        out += [f"T{l}", f"X{l}"]
    return out + ["vnew", "o", "ss", "on"]


def hg_phases(c):
    out = ["v", "a0"]
    for l in range(1, levels_of(c) + 1):
        out += [f"b{l}", f"a{l}"]
    return out + ["kd", "kdt", "o", "ss", "on"]


def schedule():
    out = [("start",)]
    prod = list(range(len(OUTS)))

    def parts(g):
        return [("part", g, n, k) for n in range(FIRST_SLOT[g], LAST_SLOT[g] + 1)
                for k in range(SLOT_K.get(OUTS[g][0], [8])[n - FIRST_SLOT[g]])]

    def upto(kind, i):
        n = G_OF[(kind, i)] + 1
        part = [x for x in prod if x < n]
        del prod[:len(part)]
        return [y for g in part for y in parts(g) + [("post", g)]]

    def with_norm(s, kind):
        got = upto(kind, 0)
        return got[:-1] + [("norm", s), got[-1]]

    first = upto("gates", 0)
    for k in range(KC):
        out += [("x", k), ("split", 0, k), ("square", 0, k)]
        if k >= 5:
            out += first[k - 5:k - 4]
    out += first[KC - 5:-1] + [("params",)] + upto("qkv", 0)[:-1]
    out += [("norm", 0), first[-1], ("post", 1)]
    for i in range(1, 12):
        got = upto("qkv", i)
        out += got[:-1] + [("l2", i - 3)] * (0 <= i - 3 < 8) + got[-1:] + [("l2sq", i - 1)] * (i - 1 < 8)
        out += [("gate_rows", i - 1)] * (i < 5)
    out += upto("b_x", 0) + [("l2exp",)] + upto("b_x", 1) + upto("b_gate", 1)
    for i, (kind, j) in enumerate([("c_q", 0), ("c_q", 1), ("c_f", 0), ("c_f", 1), ("c_i", 0)]):
        out += [("hg_prep", 0), ("hg_prep", 1)] * (kind == "c_i") + [("rg", i)] + [("gdn", 0, p, "diag") for p in range(2) if p == i] + upto(kind, j)
    out += [("hg_prep", 2)] + upto("c_i", 1) + [("hg_prep", 3)]
    fill = upto("c_g", 1)
    wo = upto("w_out", 0)
    fill += [("mo", 4), ("mo", 5)] + wo[:2]
    seq = [(c, ph) for c in range(TILES) for ph in gdn_phases(c)]
    hg = [(c, ph) for c in range(TILES) for ph in hg_phases(c)]
    lag = 1
    total, h, f = len(seq) + lag, 0, 0
    for i in range(total):
        for p, at in ((0, i), (2, 0), (1, i - lag)):
            if p == 2:
                while h < len(hg) and h * (total - 4) < (i + 1) * len(hg):
                    c, ph = hg[h]
                    if ph == "o" and c:
                        out.append(("hg", c - 1, "oz"))
                    out.append(("hg", c, ph))
                    h += 1
                continue
            if 0 <= at < len(seq):
                c, ph = seq[at]
                if ph == "o" and c:
                    out.append(("gdn", c - 1, p, "oz"))
                out.append(("gdn", c, p, ph))
                if ph == f"T{levels_of(c) - 1}" and c < TILES - 1:
                    out.append(("gdn", c + 1, p, "diag"))
                if at == len(seq) - 1:
                    out += [("gdn", c, p, "oz")] + ([("mo", 0), ("mo", 1)] if p == 0 else [])
            if f < len(fill) and f * FILL_STEPS < (2 * i + p + 1) * len(fill):
                out.append(fill[f])
                f += 1
    out += [("hg", TILES - 1, "oz"), ("mo", 6), ("mo", 7)] + wo[2:6] + [("mo", 2), ("mo", 3)] + wo[6:8] + [("mix_out",)]
    out += wo[8:] + [("square", 1, 0)]
    for i in range(1, 8):
        got = upto("w_out", i)
        if i >= 4:
            m = [("mem", k) for k in range(3 * (i - 4), min(KC, 3 * (i - 3)))]
            got = got[:2] + m[:1] + got[2:5] + m[1:2] + got[5:7] + m[2:] + got[7:]
        out += got + [("square", 1, i)]
        if i == 6:
            out += [("memsq",)]
    for i in range(8):
        out += upto(("w_k", "w_v")[i // 4], i % 4) + [("split", 1, i)]
        if i >= 4:
            out += [("kt", i - 4)]
    out += [("norm", 1)]
    for i in range(8):
        got, h = upto("w_q", i), (i - 2) // 2
        if i == 1:
            got = [("kt", j) for j in range(4, 8)] + got
        if i >= 2:
            a, b = [[("s", "exp"), ("norm",)], [("pt",), ("pv",)]][i % 2]
            got = got[:2] + [("att", h, x) for x in a] + got[2:6] + [("att", h, x) for x in b] + got[6:]
        out += got
    p0, p1 = upto("w_o", 0), upto("w_o", 1)
    ho = [("heads_out", j) for j in range(8)]
    out += ho[:4] + [("att", 3, "s"), ("att", 3, "exp")] + ho[4:6] + p0[:5] + [("att", 3, "norm")] + p0[5:6] + p1[:1]
    out += [("att", 3, "pt")] + p1[1:4] + [("att", 3, "pv")] + ho[6:] + p1[4:6] + p0[6:] + [("square", 2, 0)] + p1[6:] + [("square", 2, 1)]
    for i in range(2, 8):
        out += upto("w_o", i) + [("square", 2, i)]
    out += [("split", 2, i) for i in range(8)] + with_norm(2, "up_gate")
    out += upto("up_val", NF - 1)
    for i in range(8):
        rows, squares = [("y", i - 1)] * (i > 0), [("square", 3, i), ("y_weights", i)]
        out += upto("down", i) + (squares + rows if i == KC - 1 else rows + squares) + [("ends",)] * (i == 1)
    out += [("sums",), ("y", KC - 1), ("finish",)]
    assert not prod
    return out


FILL_STEPS = 80
OUT_ORDER = (4, 5, 0, 1, 6, 7, 2, 3)
LN_SCALE = -2.4260151319598084


def build(nc, x_prompt, x_sample, cache_mem_k, cache_mem_v, state_a_conv, state_a_S, state_b_conv, state_b_h, state_c_S,
          state_ffn_conv, mem_prompt, norm_mix, w_in, a_conv_w, a_A_log, a_dt_bias, a_norm, b_conv_w, b_conv_b, b_w_r,
          b_b_r, b_w_i, b_b_i, b_lambda, c_lb_logits, c_norm, w_out, norm_attn, norm_mem, w_q, w_k, w_v, w_o, norm_ffn,
          w_up, ffn_conv_w, ffn_conv_b, w_down, norm_final,
          y_prompt, y_sample, mem_k_out, mem_v_out, pa_conv, pa_S, pb_conv, pb_h, pc_S, pf_conv,
          sa_conv, sa_S, sb_conv, sb_h, sc_S, sf_conv):
    ctx = ExitStack()
    with ctx:
        def sb(name, shape, dt=F32, into=ctx):
            return into.enter_context(nc.sbuf_tensor("t_" + name, shape, dt))

        def sem(name):
            return ctx.enter_context(nc.semaphore(name))

        xT = sb("xT", [P, KC, TOK])
        in_ctx = ExitStack()
        XH = sb("XH", [P, KC, TOK], F32R, into=in_ctx)
        XL = sb("XL", [P, KC, TOK], F32R, into=in_ctx)
        in_ctx.close()
        y_ctx = ExitStack()
        yrow = sb("yrow", [P, TILES, D], into=y_ctx)
        fstat = sb("fstat", [P, 8], into=y_ctx)
        frows = sb("frows", [P, 2, P], into=y_ctx)
        y_ctx.close()
        sb("place_of_input", [P, 2, KC, TOK])
        raw = sb("raw", [P, RAW, KC * P])
        WH = sb("WH", [P, HL, KC * P], F32R)
        WL = sb("WL", [P, HL, KC * P], F32R)
        ident = sb("ident", [P, P])
        ones = sb("ones", [P, P])
        half_ones = sb("half_ones", [P, P])
        upto_m = sb("upto_m", [P, P])
        lev = sb("lev", [P, LEVELS, P])
        par = sb("par", [P, 556])
        NS = sb("NS", [P, TOK])
        R = sb("R", [P, TOK])
        SQ = sb("SQ", [P, 2, TOK])
        tails = sb("tails", [P, 2, 44])

        mix_ctx = ExitStack()
        qkvT = sb("qkvT", [P, 12, TOK], into=mix_ctx)
        zT = sb("zT", [P, 4, TOK], into=mix_ctx)
        xbT = sb("xbT", [P, 2, TOK], into=mix_ctx)
        gateT = sb("gateT", [P, 2, TOK], into=mix_ctx)
        cqT = sb("cqT", [P, 2, TOK], into=mix_ctx)
        ckT = sb("ckT", [P, 2, TOK], into=mix_ctx)
        cbT = sb("cbT", [P, 2, TOK], into=mix_ctx)
        cvT = sb("cvT", [P, 2, TOK], into=mix_ctx)
        cgT = sb("cgT", [P, 2, TOK], into=mix_ctx)
        pre_m = sb("pre_m", [P, 2, TOK + PRE], into=mix_ctx)
        NT = 12
        tmp = sb("tmp", [P, NT, 512], into=mix_ctx)
        Sa = sb("Sa", [P, 2, 512], into=mix_ctx)
        gT = sb("gT", [8, TOK], into=mix_ctx)
        gv = sb("gv", [P, 7, TILES * HEADS], into=mix_ctx)
        gv8 = gv[:, 5:7, :].rearrange("p a b -> p (a b)")
        hE = sb("hE", [P, 2, P], into=mix_ctx)
        hK = sb("hK", [P, 2, P], into=mix_ctx)
        kdt = sb("kdt", [P, 2, P], into=mix_ctx)
        Sc = sb("Sc", [P, 2, 2, P], into=mix_ctx)
        wr_bd = sb("wr_bd", [P, 2, 2, P], into=mix_ctx)
        small = sb("small", [P, 64], into=mix_ctx)
        row8 = sb("row8", [1, 8], into=mix_ctx)
        hQ, att = (xbT[:].rearrange("p a b -> p (a b)")[:, i * 512:(i + 1) * 512].rearrange("p (a b i) -> p a b i", a=2, b=2)
                   for i in range(2))
        vpad = wr_bd
        x_nat = qkvT[:].rearrange("p a b -> p (a b)")[:, 0:TILES * D].rearrange("p (c d) -> p c d", c=TILES)
        par_nat = cqT[:].rearrange("p a b -> p (a b)")[:, 0:640].rearrange("p (a b) -> p a b", a=5)
        st_rows = zT[:].rearrange("p a b -> p (a b)")
        mix_ctx.close()

        att_ctx = ExitStack()
        memH = sb("memH", [P, KC, N_MEM], F32R, into=att_ctx)
        memL = sb("memL", [P, KC, N_MEM], F32R, into=att_ctx)
        nat = sb("nat", [P, 2, D], into=att_ctx)
        Kn = sb("Kn", [P, 2, D], into=att_ctx)
        Vn = sb("Vn", [P, 2, D], into=att_ctx)
        sV = sb("sV", [P, 2, D], into=att_ctx)
        kT = sb("kT", [P, 2, KC, N_MEM], into=att_ctx)
        qT = sb("qT", [P, KC, TOK], into=att_ctx)
        PT = sb("PT", [P, 2, PROMPT + SAMPLE], into=att_ctx)
        prob = sb("prob", [P, TILES, N_MEM], into=att_ctx)
        mstat = sb("mstat", [P, 16], into=att_ctx)
        astat = sb("astat", [P, 4, TILES], into=att_ctx)
        att_ctx.close()

        ffn_ctx = ExitStack()
        FH = sb("FH", [P, NF, TOK], F32R, into=ffn_ctx)
        FL = sb("FL", [P, NF, TOK], F32R, into=ffn_ctx)
        pre_f = sb("pre_f", [P, 1, TOK + PRE], into=ffn_ctx)
        fg = sb("fg", [P, TOK], into=ffn_ctx)
        fv = sb("fv", [P, TOK], into=ffn_ctx)
        tail_f = sb("tail_f", [P, 2, 2, 44], into=ffn_ctx)
        ffn_ctx.close()

        pg = [ctx.enter_context(nc.psum_tensor(f"pg{i}", [P, 2, 512], F32)) for i in range(2)]
        pm = ctx.enter_context(nc.psum_tensor("pm", [P, 4, 512], F32))
        A, B, C, DD = (pm[:, i, :] for i in range(4))

        PAIR_BANKS = ((pm[:, 0, :], pm[:, 1, :]), (pm[:, 2, :], pg[1][:, 1, :]))

        def half_of(bank, i):
            return bank[:, 256 * i:256 * i + 256].rearrange("p (h i) -> p h i", h=2)

        def hg_bank(l):
            return pg[1][:, 0, :] if l % 2 else DD

        def level_banks(p, l):
            b = PAIR_BANKS[p]
            return (b[1], b[0]) if l % 2 else (b[0], b[1])

        def Tp(i, p):
            return heads(tmp[:, i, :])[:, 2 * p:2 * p + 2, :]

        def heads(ap):
            return ap.rearrange("p (h i) -> p h i", h=HEADS)

        def cols(v, n):
            return v.unsqueeze(2).to_broadcast([v.shape[0], v.shape[1], n])

        def over(m, h):
            return m.unsqueeze(1).to_broadcast([m.shape[0], h, m.shape[1]])

        def col(name, i=0, n=1):
            return par[:, COL[name] + i:COL[name] + i + n]

        const_ready = sem("const_ready")
        x_loaded = [sem(f"x_loaded{i}") for i in range(X_PIECES)]
        mix_loaded = sem("mix_loaded")
        par_loaded = sem("par_loaded")
        state_loaded = sem("state_loaded")
        mem_loaded = sem("mem_loaded")
        cache_loaded = sem("cache_loaded")
        cv_loaded = sem("cv_loaded")
        w_loaded = [sem(f"w_loaded{i}") for i in range(RAW)]
        stored = sem("stored")
        w_high = sem("w_high")
        w_low = sem("w_low")
        slot_done = sem("slot_done")

        SCHED = schedule()
        names = {
            "start_pe": [(0, ["mix"] + [f"x{k}" for k in range(KC)] + ["par", "row8"])],
            "start_dve": [(0, ["mix"] + [f"x{k}" for k in range(KC)] + ["par", "pad"])],
            "start_act": [(0, [f"x{k}" for k in range(KC)])],
            "feed_act": [(0, [x + str(k) for k in range(KC) for x in ("hi", "sq")])] + [
                (s, [f"sq{k}" for k in range(KC)] + [f"hi{k}" for k in range(KC) if s < 3]) for s in range(1, 4)],
            "feed_dve": [(0, ["lo0"] + [x + str(k) for k in range(1, KC) for x in ("lo", "ns")])] + [
                (s, [f"ns{k}" for k in range(1, KC)] + [f"lo{k}" for k in range(KC) if s < 3]) for s in range(1, 4)],
            "norm_pe": [(s, ["ss"]) for s in range(4)],
            "norm_act": [(s, ["ln", "exp"]) for s in range(3)],
        }
        order = {}
        for key, rounds in names.items():
            order[key] = Steps(sem(key), rounds)
        start_pe, start_dve, start_act, feed_act, feed_dve, norm_pe, norm_act = (order[k] for k in (
            "start_pe", "start_dve", "start_act", "feed_act", "feed_dve", "norm_pe", "norm_act"))

        def post_dve_names(kind, i):
            taps = [f"tap{j}" for j in range(CONV.get(kind, 0))]
            return ((["zero"] if (kind, i) == ("up_gate", 0) else []) + ["evac"] + (["state", "tail"] if kind in CONV else []) + taps + (["prod"] if kind == "up_val" else []))

        post_dve = Steps(sem("post_dve"), [(g, post_dve_names(*OUTS[g])) for g in range(len(OUTS))])
        post_act = Steps(sem("post_act"), [(g, {"qkv": ["silu"], "c_q": ["silu"], "b_gate": ["gelu"], "up_gate": ["silu"],
                                                "up_val": ["hi"], "z": ["silu"], "c_g": ["silu"], "c_f": ["sig"]}.get(OUTS[g][0], [])) for g in range(len(OUTS))])
        post_pool = Steps(sem("post_pool"), [(G_OF[("up_val", f)], ["lo"]) for f in range(NF)])
        gate_pe = Steps(sem("gate_pe"), [(0, ["turn", "gl"])])
        gate_dve = Steps(sem("gate_dve"), [(0, ["clear", "rows", "rows4", "arg", "pos", "neg", "g0", "g", "gc", "gl", "kd", "be"])])
        gate_act = Steps(sem("gate_act"), [(0, ["beta", "eA", "exp", "ln", "egc", "ekd"])])
        rg_pe = Steps(sem("rg_pe"), [(i, ["gates"]) for i in range(2)])
        rg_dve = Steps(sem("rg_dve"), [(0, ["nlam", "abs", "sp", "c8", "c8n"])] + [
            (1 + i, ["a2", "m2", "gx"]) for i in range(2)] + [(3 + i, ["gap", "u", "scan", "scan_s", "ht", "y"]) for i in range(2)])
        rg_act = Steps(sem("rg_act"), [(0, ["exp", "ln"])] + [(1 + i, ["r", "i"]) for i in range(2)] + [
            (4 + i, ["a", "th"]) for i in range(2)] + [(6, ["mult"])])
        l2_pe = Steps(sem("l2_pe"), [(i, ["ss"]) for i in range(8)])
        l2_act = Steps(sem("l2_act"), [x for i in range(1, 12) for x in [(i - 3, ["ln"])] * (0 <= i - 3 < 8) + [(i - 1, ["sq"])] * (i - 1 < 8)] + [
            (8, ["exp0", "exp1"])])
        l2_dve = Steps(sem("l2_dve"), [(i, ["n"]) for i in range(8)])

        def per_level(c, first, last):
            return [x + str(l) for l in range(1, levels_of(c) - 1) for x in first] + [
                x + str(levels_of(c) - 1) if x in "TXUB" else x for x in last]

        gdn_pe = [Steps(sem(f"gdn_pe{p}"), [(c, ["rows", "gb", "kk", "X0"] + per_level(c, "TX", ("T", "ks", "U")) + [
            "vnew", "o", "S", "ss"]) for c in range(TILES)]) for p in range(2)]
        gdn_dve = [Steps(sem(f"gdn_dve{p}"), [(c, ["vb", "kd", "gd", "LT", "QKT", "Ut", "U0"] + per_level(c, "X", ("r", "U")) + [
            "S", "on"]) for c in range(TILES)]) for p in range(2)]
        gdn_oz = [Steps(sem(f"gdn_oz{p}"), [(c, ["oz"]) for c in range(TILES)]) for p in range(2)]
        gdn_act = [Steps(sem(f"gdn_act{p}"), [(c, ["gbe", "PT", "egb", "X0"] + per_level(c, "T", "T") + [
            "vn", "o", "osq", "ln", "exp"]) for c in range(TILES)]) for p in range(2)]
        gdn_pool = [Steps(sem(f"gdn_pool{p}"), [(c, ["dg", "db", "PTm", "bPT", "B1", "qd"] + per_level(c, "B", "B")[1:])
                                                for c in range(TILES)]) for p in range(2)]
        hg_oz = Steps(sem("hg_oz"), [(c, ["oz"]) for c in range(TILES)])
        hgp_dve = Steps(sem("hgp_dve"), [(0, ["e0", "q", "v", "rec", "sm", "lb", "oml"]), (1, ["f", "k"] + [f"b{i}_{c}" for i in range(2) for c in range(TILES)])])
        hgp_act = Steps(sem("hgp_act"), [(0, ["e"]), (1, ["lf"])])
        hg_pe = Steps(sem("hg_pe"), [(c, ["v"] + [f"A{l}" for l in range(levels_of(c) + 1)] + ["kd", "o", "S", "ss"]) for c in range(TILES)])
        hg_dve = Steps(sem("hg_dve"), [(c, ["q0", "dk1", "dq1"] + [
            x for l in range(1, levels_of(c) + 1) for x in [f"qa{l}", f"qb{l}", f"att{l - 1}"] + (
                [f"dk{l + 1}", f"dq{l + 1}"] if l < levels_of(c) else [f"att{l}"])] + [
            "S00", "S10", "S01", "S11", "on"]) for c in range(TILES)])
        hg_act = Steps(sem("hg_act"), [(c, ["v0", "v1"] + [f"E{l}" for l in range(1, levels_of(c) + 1)] + [
            "ek0", "ek1", "eq", "eb", "kdt", "o", "osq", "ln", "exp"]) for c in range(TILES)])
        hg_pool = Steps(sem("hg_pool"), [(c, ["k0"] + [f"k{l}" for l in range(1, levels_of(c) + 1)] + ["kd", "qe"]) for c in range(TILES)])
        mo_pe = Steps(sem("mo_pe"), [(0, ["st"])])
        mo_act = Steps(sem("mo_act"), [(j, ["hi"]) for j in OUT_ORDER] + [(8, ["st"])])
        mo_dve = Steps(sem("mo_dve"), [(j, ["lo"]) for j in OUT_ORDER])
        mem_pe = Steps(sem("mem_pe"), [(k, ["t"]) for k in range(KC)])
        mem_act = Steps(sem("mem_act"), [(1 + k, ["hi"]) for k in range(KC)] + [(0, ["sq0", "sq1", "ln", "exp"])])
        mem_dve = Steps(sem("mem_dve"), [(k, ["lo"]) for k in range(KC)])
        kt_pe = Steps(sem("kt_pe"), [(j, ["t"]) for j in range(8)])
        kt_act = Steps(sem("kt_act"), [(j, ["t"]) for j in range(8)])
        at_pe = Steps(sem("at_pe"), [(h, ["s", "t", "pv"]) for h in range(HEADS)])
        at_dve = Steps(sem("at_dve"), [(0, ["clear"])] + [(h, ["max", "max4", "nmax", "rec", "norm", "norm4", "o0", "o1", "os"])
                                                         for h in range(HEADS)])
        at_act = Steps(sem("at_act"), [(h, [f"exp{c}" for c in range(TILES)] + ["pt0", "pt1", "pts"]) for h in range(HEADS)])
        ho_act = Steps(sem("ho_act"), [(j, ["hi"]) for j in range(8)])
        ho_dve = Steps(sem("ho_dve"), [(j, ["lo"]) for j in range(8)])
        y_dve = Steps(sem("y_dve"), [(k, ["w"]) for k in range(KC)] + [(KC, [f"y{c}" for c in (0, 2, 4)])])
        y_pe = Steps(sem("y_pe"), [(k, ["t"]) for k in range(KC)])
        y_act = Steps(sem("y_act"), [(k, ["y", "y4"]) for k in range(KC - 1)] + [
            (KC, ["ln", "exp"]), (KC - 1, ["y", "y4"]), (KC, ["y1", "y3"])])
        ends_pe = Steps(sem("ends_pe"), [(0, ["t"])])
        ends_dve = Steps(sem("ends_dve"), [(0, ["t"])])
        fin_pe = Steps(sem("fin_pe"), [(0, ["ss"])])

        block = ctx.enter_context(nc.Block())
        G_WOUT, G_WK, G_WQ, G_WO, G_UP, G_DOWN = (G_OF[(k, 0)] for k in ("w_out", "w_k", "w_q", "w_o", "up_gate", "down"))
        G_LAST_IN = G_WOUT - 1

        MIX_STORES = 14
        ALL_STORES = MIX_STORES + 2 + 2 + TILES
        EARLY_CONSTS, CONSTS, STATE_READY = 7, 36, 16 * 7

        def rows_of(v):
            return v.rearrange("(k p) -> k p", p=P)

        def rows_of2(v):
            return v.rearrange("j (k p) -> (j k) p", p=P)

        PARAMS = [(0, COL["mix"], rows_of(norm_mix[0])), (0, COL["attn"], rows_of(norm_attn[0])),
                  (0, COL["ffn"], rows_of(norm_ffn[0])), (0, COL["mem"], rows_of(norm_mem[0])),
                  (0, COL["final"], rows_of(norm_final)), (0, COL["a_w"], rows_of2(a_conv_w[0])),
                  (0, COL["b_w"], rows_of2(b_conv_w[0])), (0, COL["b_b"], rows_of(b_conv_b[0])),
                  (0, COL["b_r"], rows_of(b_b_r[0])), (0, COL["b_i"], rows_of(b_b_i[0])),
                  (0, COL["lam"], rows_of(b_lambda[0])), (0, COL["lb"], rows_of(c_lb_logits[0])),
                  (0, COL["b_h"], rows_of(state_b_h[0, 0])), (0, COL["a_norm"], a_norm),
                  (1, 0, rows_of2(state_a_conv[0, 0])), (1, 36, rows_of2(state_b_conv[0, 0])), (1, 42, rows_of(ffn_conv_b[0])),
                  (2, 0, rows_of2(ffn_conv_w[0, 0:2])), (3, 0, rows_of(ffn_conv_w[0, 2])),
                  (3, 44, rows_of(state_ffn_conv[0, 0, 0])), (4, 0, rows_of(state_ffn_conv[0, 0, 1]))]
        PAR_DMAS = len(PARAMS) - 1 + 4


        @block.sync
        def _(sp):
            w = D // X_PIECES
            for i, loaded in enumerate(x_loaded):
                sp.dma_start(x_nat[:, 0:4, i * w:(i + 1) * w], x_prompt[0].rearrange("(c p) d -> p c d", p=P)[:, :, i * w:(i + 1) * w])\
                    .then_inc(loaded, 16)
                sp.dma_start(x_nat[0:SAMPLE, 4, i * w:(i + 1) * w], x_sample[0][:, i * w:(i + 1) * w]).then_inc(loaded, 16)

            def source(n):
                g, j = SLOTS[n]
                kind, i = OUTS[g]
                if kind in W_IN_COL:
                    c0 = W_IN_COL[kind] + i * P
                    return w_in[0][:, c0:c0 + P].rearrange("(k p) n -> p k n", p=P), KC * P
                if kind in ("w_k", "w_v"):
                    w = {"w_k": w_k, "w_v": w_v}[kind][0]
                    return w[4 * j * P:4 * (j + 1) * P, i * 256:(i + 1) * 256].rearrange("(k p) n -> p k n", p=P), KC * P
                if kind in ("up_gate", "up_val"):
                    c0 = i * P + (D_FF if kind == "up_val" else 0)
                    return w_up[0][:, c0:c0 + P].rearrange("(k p) n -> p k n", p=P), KC * P
                if kind == "down":
                    nk = SLOT_K["down"][j]
                    return w_down[0][8 * j * P:(8 * j + nk) * P, i * P:(i + 1) * P].rearrange("(k p) n -> p k n", p=P), nk * P
                w = {"w_out": w_out, "w_q": w_q, "w_o": w_o}[kind][0]
                return w[:, i * P:(i + 1) * P].rearrange("(k p) n -> p k n", p=P), KC * P

            for n in range(len(SLOTS)):
                if n == RAW:
                    for t, r0, src in PARAMS[1:]:
                        sp.dma_start(par_nat[r0:r0 + src.shape[0], t, :], src).then_inc(par_loaded, 16)
                    for h in range(2):
                        sp.dma_start(par_nat[109:110, 0, 64 * h:64 * h + 64], c_norm).then_inc(par_loaded, 16)
                    sp.dma_start(row8[:, 0:4], a_A_log).then_inc(par_loaded, 16)
                    sp.dma_start(row8[:, 4:8], a_dt_bias).then_inc(par_loaded, 16)
                if n >= RAW:
                    sp.wait_ge(w_low, n - RAW + 1)
                src, size = source(n)
                nk = src.shape[1]
                sp.dma_start(raw[:, n % RAW, 0:size].rearrange("p (k n) -> p k n", k=nk), src).then_inc(w_loaded[n % RAW], 16)
                g = SLOTS[n][0]
                if OUTS[g] == ("w_q", 0):
                    sp.wait_ge(*mem_pe.at(KC - 1, "t"))
                    sp.wait_ge(*mem_act.at(0, "sq1"))
                    sp.dma_start(nat[:], cache_mem_k[0, 0].rearrange("(c p) h d -> p c (h d)", p=P)).then_inc(cache_loaded, 16)
            for c in (0, 2, 4):
                sp.wait_ge(*y_dve.at(KC, f"y{c}"))
                n = tile_len(c)
                to = y_prompt[0, c * P:c * P + n, :] if c < TILES - 1 else y_sample[0]
                sp.dma_start(to, yrow[0:n, c, :]).then_inc(stored, 16)
            sp.wait_ge(stored, 16 * ALL_STORES)

        @block.tensor
        def _(pe):
            def mm(out, lhsT, rhs, start=True, stop=True):
                return pe.matmul(out, lhsT, rhs, start=start, stop=stop)

            def part(g, n, k):
                kind, i = OUTS[g]
                ps = pg[PAIR[g]]
                j = n - FIRST_SLOT[g]
                nk = SLOT_K.get(kind, [8])[j]
                begins, ends = n == FIRST_SLOT[g] and k == 0, n == LAST_SLOT[g] and k == nk - 1
                if begins:
                    if PREV[g] is None:
                        pe.wait_ge(*start_dve.at(0, "mix"))
                    else:
                        pe.wait_ge(*post_dve.at(PREV[g], "evac"))
                    if g == G_WK:
                        pe.wait_ge(*mem_dve.at(KC - 1, "lo"))
                    if g == G_WQ:
                        pe.wait_ge(*feed_dve.at(1, f"lo{KC - 1}"))
                    if g == G_WOUT + 1:
                        pe.wait_ge(*hg_dve.at(TILES - 1, "on"))
                        pe.wait_ge(*gdn_act[1].at(TILES - 1, "ln"))
                        pe.wait_ge(*gdn_dve[1].at(TILES - 1, "S"))
                if k == 0:
                    pe.wait_ge(w_low, n + 1)
                if kind in ("w_k", "w_v"):
                    wh, wl = (w[:, n % HL, :].rearrange("p (k n) -> p k n", k=4) for w in (WH, WL))
                    for t in range(2):
                        o = ps[:, t, 0:N_MEM]
                        mh, ml = (m[:, 4 * j + k, t * P:(t + 1) * P] for m in (memH, memL))
                        mm(o, mh, wh[:, k, :], begins, False)
                        mm(o, mh, wl[:, k, :], False, False)
                        q = mm(o, ml, wh[:, k, :], False, ends)
                else:
                    wh, wl = (w[:, n % HL, :].rearrange("p (k n) -> p k n", k=KC) for w in (WH, WL))
                    xh, xl = (FH, FL) if kind == "down" else (XH, XL)
                    kk = OUT_ORDER[k] if g == G_WOUT else 8 * j + k
                    if g in (0, G_UP):
                        pe.wait_ge(*feed_dve.at(0 if g == 0 else 2, f"lo{k}"))
                    if g == G_WOUT:
                        pe.wait_ge(*mo_dve.at(kk, "lo"))
                    if g in (G_WO, G_WO + 1):
                        pe.wait_ge(*ho_dve.at(k, "lo"))
                    if g == G_DOWN:
                        pe.wait_ge(*post_pool.at(G_OF[("up_val", kk)], "lo"))
                    for w, x, s0, s1 in ((wh, xh, begins, False), (wh, xl, False, False), (wl, xh, False, ends)):
                        for h in range(2):
                            q = mm(ps[:, h, 0:HALF], w[:, kk % 8, :], x[:, kk, h * HALF:(h + 1) * HALF], s0, s1)
                if k == nk - 1:
                    q.then_inc(slot_done, 1)

            def norm(s):
                pe.wait_ge(*feed_dve.at(s, f"ns{KC - 1}"))
                if s == 1:
                    pe.wait_ge(*mo_act.at(8, "st"))
                    pe.wait_ge(*kt_act.at(1, "t"))
                if s == 2:
                    pe.wait_ge(*at_dve.at(3, "os"))
                    pe.wait_ge(*at_act.at(3, "pts"))
                if s == 0:
                    pe.wait_ge(*start_dve.at(0, "pad"))
                    pe.wait_ge(*start_act.at(0, f"x{KC - 1}"))
                for h in range(2):
                    q = mm(pm[:, h, 0:HALF], ones[:], NS[:, h * HALF:(h + 1) * HALF])
                q.then_inc(*norm_pe.did(s, "ss"))

            def start():
                pe.wait_ge(const_ready, EARLY_CONSTS)
                pe.wait_ge(mix_loaded, 16)
                pe.transpose(pg[1][:, 0, 0:KC], par_nat[0:KC, 0, :], ident[0:KC, 0:KC]).then_inc(*start_pe.did(0, "mix"))

            def x(k):
                if k % (KC // X_PIECES) == 0:
                    pe.wait_ge(x_loaded[k * X_PIECES // KC], 32)
                if k >= 2:
                    pe.wait_ge(*start_act.at(0, f"x{k - 2}"))
                    pe.wait_ge(*start_dve.at(0, f"x{k - 2}"))
                b = 2 * (k % 2)
                for c in range(4):
                    pe.transpose(pm[:, b, c * P:(c + 1) * P], x_nat[:, c, k * P:(k + 1) * P], ident[:])
                pe.transpose(pm[:, b + 1, 0:SAMPLE], x_nat[0:SAMPLE, 4, k * P:(k + 1) * P],
                             ident[0:SAMPLE, 0:SAMPLE]).then_inc(*start_pe.did(0, f"x{k}"))

            def params():
                pe.wait_ge(par_loaded, 16 * PAR_DMAS)
                pe.wait_ge(*start_act.at(0, f"x{KC - 1}"))
                pe.wait_ge(*start_dve.at(0, f"x{KC - 1}"))
                for t, rows in enumerate(PAR_ROWS):
                    dst = C[:, t * P:t * P + rows] if t < 4 else DD[:, 0:rows]
                    q = pe.transpose(dst, par_nat[0:rows, t, :], ident[0:rows, 0:rows])
                q.then_inc(*start_pe.did(0, "par"))
                mm(A[:, 0:8], ones[0:1, :], row8[0:1, :]).then_inc(*start_pe.did(0, "row8"))

            def gate_rows(part):
                if part == 0:
                    pe.wait_ge(*post_dve.at(0, "evac"))
                    pe.wait_ge(*start_dve.at(0, "par"))
                    for c in range(TILES):
                        n = tile_len(c)
                        q = pe.transpose(C[0:n, c * 8:(c + 1) * 8], gT[:, tile_at(c):tile_at(c) + n], ident[0:8, 0:8])
                    q.then_inc(*gate_pe.did(0, "turn"))
                if part == 2:
                    pe.wait_ge(*gate_dve.at(0, "g"))
                    mm(DD[:, 0:TILES * 4], upto_m[:], gv[:, 1, 0:TILES * 4])
                    mm(DD[:, 32:48], ones[:], gv[:, 1, 0:16])
                    mm(DD[:, 48:52], ones[0:SAMPLE, :], gv[0:SAMPLE, 1, 16:20]).then_inc(*gate_pe.did(0, "gl"))

            def l2(i):
                pe.wait_ge(*l2_act.at(i, "sq"))
                if i >= 2:
                    pe.wait_ge(*l2_act.at(i - 2, "ln"))
                elif i:
                    pe.wait_ge(*gate_dve.at(0, "gl"))
                for h in range(2):
                    q = mm(pm[:, 2 * (i % 2) + h, 0:HALF], ones[:], SQ[:, i % 2, h * HALF:(h + 1) * HALF])
                q.then_inc(*l2_pe.did(i, "ss"))

            def rg(i):
                if i > 1:
                    return
                pe.wait_ge(*post_dve.at(G_OF[("b_x", i)], "tap3"))
                pe.wait_ge(state_loaded, STATE_READY)
                if i:
                    pe.wait_ge(*rg_act.at(1, "i"))
                else:
                    pe.wait_ge(*l2_act.at(7, "ln"))
                for gate in range(2):
                    for h in range(2):
                        q = mm(pm[:, 2 * gate + h, 0:HALF], wr_bd[:, gate, i, :], xbT[:, i, h * HALF:(h + 1) * HALF])
                q.then_inc(*rg_pe.did(i, "gates"))

            def gdn(c, p, ph):
                n, t0 = tile_len(c), tile_at(c)
                last = levels_of(c) - 1
                did, dve, act_, pool_ = gdn_pe[p].did, gdn_dve[p], gdn_act[p], gdn_pool[p]

                def T(i):
                    return Tp(i, p)

                def each(out, lhs, rhs):
                    for h in range(2):
                        q = mm(out(h), lhs(h), rhs(h))
                    return q

                S = heads(Sa[:, 1 if c == TILES - 1 else 0, :])[:, 2 * p:2 * p + 2, :]
                qT_, kT_ = (qkvT[:, 4 * x + 2 * p:4 * x + 2 * p + 2, t0:t0 + n] for x in range(2))
                Pb, Qb = PAIR_BANKS[p]
                if ph == "rows":
                    if c == 0:
                        pe.wait_ge(*l2_dve.at(7, "n"))
                        pe.wait_ge(*post_act.at(G_OF[("qkv", 11)], "silu"))
                        pe.wait_ge(*rg_act.at(2, "i"))
                        if p:
                            pe.wait_ge(*post_dve.at(PREV[G_WOUT + 1], "evac"))
                    else:
                        pe.wait_ge(*dve.at(c - 1, "S"))
                        pe.wait_ge(*act_.at(c - 1, "ln"))
                    for x in range(2):
                        for h in range(2):
                            q = pe.transpose(half_of(Pb, x)[0:n, h, :], qkvT[:, 4 * (1 + x) + 2 * p + h, t0:t0 + n], ident[:])
                    q.then_inc(*did(c, "rows"))
                    pe.wait_ge(*pool_.at(c, "db"))
                    for x in range(2):
                        for h in range(2):
                            q = mm(half_of(Qb, x)[:, h, 0:n], ones[0:n, :], half_of(SQ[:, p, :], x)[0:n, h, 0:n])
                    q.then_inc(*did(c, "gb"))
                elif ph == "mask":
                    pe.wait_ge(*dve.at(c, "kd"))
                    each(lambda h: half_of(Pb, 0)[0:n, h, 0:n], lambda h: kT_[:, h, :], lambda h: kT_[:, h, :])
                    each(lambda h: half_of(Pb, 1)[0:n, h, 0:n], lambda h: kT_[:, h, :], lambda h: qT_[:, h, :])\
                        .then_inc(*did(c, "kk"))
                elif ph == "turn":
                    pe.wait_ge(*dve.at(c, "U0"))
                    for h in range(2):
                        q = pe.transpose(half_of(Qb, 0)[0:n, h, 0:n], T(5)[0:n, h, 0:n], ident[0:n, 0:n])
                    q.then_inc(*did(c, "X0"))
                elif ph[0] in "TX":
                    l = int(ph[1:])
                    Rt, Rx = (half_of(b, 0) for b in level_banks(p, l))
                    if ph[0] == "T":
                        pe.wait_ge(*pool_.at(c, f"B{l}"))
                        pe.wait_ge(*(dve.at(c, f"X{l - 1}") if l > 1 else act_.at(c, "X0")))
                        q = each(lambda h: Rt[0:n, h, 0:n], lambda h: T(1)[0:n, h, 0:n], lambda h: T(2)[0:n, h, 0:n])
                        if l > 1:
                            for h in range(2):
                                q = pe.transpose(half_of(level_banks(p, l)[0], 1)[0:n, h, 0:n], T(2)[0:n, h, 0:n], ident[0:n, 0:n])
                        q.then_inc(*did(c, f"T{l}"))
                        return
                    if l < last:
                        pe.wait_ge(*act_.at(c, f"T{l}"))
                        each(lambda h: Rx[0:n, h, 0:n], lambda h: T(5)[0:n, h, 0:n], lambda h: T(0)[0:n, h, 0:n])\
                            .then_inc(*did(c, f"X{l}"))
                        return
                    else:
                        each(lambda h: Rx[0:n, h, :], lambda h: kT_[:, h, :], lambda h: S[:, h, :]).then_inc(*did(c, "ks"))
                        pe.wait_ge(*act_.at(c, f"T{l}"))
                    each(lambda h: Rt[0:n, h, 0:n], lambda h: T(0)[0:n, h, 0:n], lambda h: T(5)[0:n, h, 0:n])\
                        .then_inc(*did(c, f"U{l}"))
                elif ph == "vnew":
                    Rx = half_of(level_banks(p, last)[1], 0)
                    pe.wait_ge(*dve.at(c, f"U{last}"))
                    each(lambda h: Rx[0:n, h, :], lambda h: T(5)[0:n, h, 0:n], lambda h: T(6)[0:n, h, :]).then_inc(*did(c, "vnew"))
                elif ph == "o":
                    Rt, Rx = (half_of(b, 0) for b in level_banks(p, last))
                    pe.wait_ge(*act_.at(c, "vn"))
                    for h in range(2):
                        mm(Rt[:, h, 0:n], S[:, h, :], T(9)[:, h, 0:n], True, False)
                        q = mm(Rt[:, h, 0:n], T(7)[0:n, h, :], T(11)[0:n, h, 0:n], False, True)
                    q.then_inc(*did(c, "o"))
                    each(lambda h: Rx[:, h, :], lambda h: T(3)[0:n, h, :], lambda h: T(7)[0:n, h, :]).then_inc(*did(c, "S"))
                elif ph == "ss":
                    pe.wait_ge(*act_.at(c, "osq"))
                    mm(half_of(level_banks(p, last)[0], 1)[:, :, 0:n], ones[:], T(0)[:, :, 0:n]).then_inc(*did(c, "ss"))

            def hg(c, ph):
                n, t0 = tile_len(c), tile_at(c)
                d4 = DD.rearrange("p (a b i) -> p a b i", a=2, b=2)
                d2 = DD[:, 0:256].rearrange("p (a i) -> p a i", a=2)
                if ph == "v":
                    pe.wait_ge(*post_dve.at(G_OF[("c_i", 1)], "evac"))
                    if c == 0:
                        pe.wait_ge(*rg_act.at(2, "i"))
                    else:
                        pe.wait_ge(*hg_act.at(c - 1, "ln"))
                    for i in range(2):
                        q = pe.transpose(d2[0:n, i, :], cvT[:, i, t0:t0 + n], ident[:])
                    q.then_inc(*hg_pe.did(c, "v"))
                elif ph[0] == "a":
                    l = int(ph[1:])
                    pe.wait_ge(*hg_pool.at(c, f"k{l}"))
                    pe.wait_ge(*hg_dve.at(c, f"qb{l}" if l else "q0"))
                    if l > 1:
                        pe.wait_ge(*hg_dve.at(c, f"att{l - 2}"))
                    elif l and c == 0:
                        pe.wait_ge(*post_dve.at(PREV[G_WOUT + 1], "evac"))
                    elif l == 0:
                        pe.wait_ge(*hg_act.at(c, "v1"))
                    for i in range(2):
                        q = mm(hg_bank(l).rearrange("p (a b i) -> p a b i", a=2, b=2)[0:n, i, :, 0:n], hK[:, i, 0:n], hQ[:, i, :, 0:n])
                    q.then_inc(*hg_pe.did(c, f"A{l}"))
                elif ph == "kdt":
                    pe.wait_ge(*hg_pool.at(c, "kd"))
                    pe.wait_ge(*hg_dve.at(c, f"att{levels_of(c)}"))
                    for i in range(2):
                        q = pe.transpose(d2[0:n, i, :], hK[:, i, 0:n], ident[:])
                    q.then_inc(*hg_pe.did(c, "kd"))
                elif ph == "o":
                    Sx = Sc[:, 1 if c == TILES - 1 else 0]
                    pe.wait_ge(*hg_pool.at(c, "qe"))
                    pe.wait_ge(*hg_act.at(c, "kdt"))
                    if c in (0, TILES - 1):
                        pe.wait_ge(state_loaded, STATE_READY)
                    for i in range(2):
                        mm(d4[:, 0, i, 0:n], Sx[:, i, :], hE[:, i, 0:n], True, False)
                        mm(d4[:, 0, i, 0:n], vpad[0:n, i, 0, :], att[0:n, i, 0, 0:n], False, False)
                        q = mm(d4[:, 0, i, 0:n], vpad[0:n, i, 1, :], att[0:n, i, 1, 0:n], False, True)
                    q.then_inc(*hg_pe.did(c, "o"))
                    for i in range(2):
                        mm(d4[:, 1, i, :], kdt[0:n, i, :], vpad[0:n, i, 0, :], True, False)
                        q = mm(d4[:, 1, i, :], kdt[0:n, i, :], vpad[0:n, i, 1, :], False, True)
                    q.then_inc(*hg_pe.did(c, "S"))

                elif ph == "ss":
                    pe.wait_ge(*hg_dve.at(c, "S11"))
                    pe.wait_ge(*hg_act.at(c, "osq"))
                    mm(d4[:, 0, :, 0:n], half_ones[:], hE[:, :, 0:n]).then_inc(*hg_pe.did(c, "ss"))

            def mix_out():
                pe.wait_ge(*gdn_dve[0].at(TILES - 1, "S"))
                pe.wait_ge(*gdn_act[0].at(TILES - 1, "ln"))
                for r in range(2):
                    q = pe.transpose(pm[0:44, r, 0:P], tails[:, r, :], ident[:])
                q.then_inc(*mo_pe.did(0, "st"))

            def mem(k):
                pe.wait_ge(mem_loaded, 16)
                if k >= 2:
                    pe.wait_ge(*mem_dve.at(k - 2, "lo"))
                else:
                    pe.wait_ge(*gdn_act[1].at(TILES - 1, "ln"))
                    pe.wait_ge(*gdn_dve[1].at(TILES - 1, "S"))
                    pe.wait_ge(*hg_act.at(TILES - 1, "ln"))
                for t in range(2):
                    q = pe.transpose(pm[:, 2 + k % 2, t * P:(t + 1) * P], nat[:, t, k * P:(k + 1) * P], ident[:])
                q.then_inc(*mem_pe.did(k, "t"))

            def kt(j):
                src = Kn if j < 4 else nat
                if j == 0:
                    pe.wait_ge(*post_dve.at(G_OF[("w_k", 3)], "evac"))
                    pe.wait_ge(*mem_dve.at(KC - 1, "lo"))
                    pe.wait_ge(*mo_act.at(8, "st"))
                if j == 4:
                    pe.wait_ge(cache_loaded, 16)
                    pe.wait_ge(*norm_act.at(1, "ln"))
                if j >= 4:
                    pe.wait_ge(*kt_act.at(j - 4, "t"))
                for d in range(2):
                    for t in range(2):
                        ch = 2 * (j % 4) + d
                        q = pe.transpose(pm[:, j % 4, d * 256 + t * P:d * 256 + (t + 1) * P], src[:, t, ch * P:(ch + 1) * P], ident[:])
                q.then_inc(*kt_pe.did(j, "t"))

            def attention(h, ph):
                if ph == "s":
                    pe.wait_ge(*post_dve.at(G_OF[("w_q", 2 * h + 1)], "evac"))
                    pe.wait_ge(*kt_act.at(7, "t"))
                    if h:
                        pe.wait_ge(*at_dve.at(h - 1, "os"))
                    for c in range(TILES):
                        n, t0 = tile_len(c), tile_at(c)
                        o = pm[0:n, c // 2, (c % 2) * 256:(c % 2 + 1) * 256]
                        kx = kT[:, 1 if c == TILES - 1 else 0]
                        mm(o, qT[:, 2 * h, t0:t0 + n], kx[:, 2 * h, :], True, False)
                        q = mm(o, qT[:, 2 * h + 1, t0:t0 + n], kx[:, 2 * h + 1, :], False, True)
                    q.then_inc(*at_pe.did(h, "s"))
                elif ph == "pt":
                    pe.wait_ge(*at_dve.at(h, "norm4"))
                    for t in range(2):
                        for c in range(TILES - 1):
                            pe.transpose((DD, A)[t][:, c * P:(c + 1) * P], prob[:, c, t * P:(t + 1) * P], ident[:])
                        q = pe.transpose(C[:, t * SAMPLE:(t + 1) * SAMPLE], prob[0:SAMPLE, TILES - 1, t * P:(t + 1) * P],
                                         ident[0:SAMPLE, 0:SAMPLE])
                    q.then_inc(*at_pe.did(h, "t"))
                elif ph == "pv":
                    pe.wait_ge(*at_act.at(h, "pts"))
                    if h == 0:
                        pe.wait_ge(cv_loaded, 16)
                    for d in range(2):
                        j = 2 * h + d
                        for t in range(2):
                            mm((B, DD)[d], Vn[:, t, j * P:(j + 1) * P], PT[:, t, 0:PROMPT], t == 0, t == 1)
                        for t in range(2):
                            q = mm(C[:, 256 + d * SAMPLE:256 + (d + 1) * SAMPLE], sV[:, t, j * P:(j + 1) * P],
                                   PT[:, t, PROMPT:PROMPT + SAMPLE], t == 0, t == 1)
                    q.then_inc(*at_pe.did(h, "pv"))

            def y(k):
                pe.wait_ge(*y_dve.at(k, "w"))
                if k >= 2:
                    pe.wait_ge(*y_act.at(k - 1, "y4"))
                for c in range(TILES - 1):
                    pe.transpose(pm[:, 2 + k % 2, c * P:(c + 1) * P], xT[:, k, c * P:(c + 1) * P], ident[:])
                if k == 1:
                    pe.wait_ge(*y_act.at(0, "y4"))
                pe.transpose(B[0:SAMPLE, 0:P], xT[:, k, S0:TOK], ident[:]).then_inc(*y_pe.did(k, "t"))

            def ends():
                pe.wait_ge(*norm_act.at(2, "ln"))
                for r in range(2):
                    q = pe.transpose(A[0:88, r * P:(r + 1) * P], tail_f[:, r].rearrange("p a b -> p (a b)"), ident[:])
                q.then_inc(*ends_pe.did(0, "t"))

            def sums():
                pe.wait_ge(*feed_dve.at(3, f"ns{KC - 1}"))
                pe.wait_ge(*ends_dve.at(0, "t"))
                for c in range(TILES):
                    n, t0 = tile_len(c), tile_at(c)
                    q = mm(A[0:n, 2 * c:2 * c + 2], NS[:, t0:t0 + n], ones[:, 0:2])
                q.then_inc(*fin_pe.did(0, "ss"))

            handlers = {"start": start, "x": x, "params": params, "part": part, "norm": norm, "gate_rows": gate_rows, "l2": l2, "rg": rg, "gdn": gdn,
                        "hg": hg, "mix_out": mix_out, "mem": mem, "kt": kt, "att": attention, "y": y, "ends": ends, "sums": sums}
            for what, *args in SCHED:
                if what in handlers:
                    handlers[what](*args)

        @block.vector
        def _(v):
            def halves(ap):
                return ap.rearrange("p (h t) -> p h t", h=2)

            Rh = halves(R[:])
            conv_no = [0]

            def settle(steps):
                if steps.made:
                    v.wait_ge(steps.sem, steps.made)

            def start():
                v.wait_ge(*start_pe.at(0, "mix"))
                v.tensor_copy(par[:, 0:KC], pg[1][:, 0, 0:KC]).then_inc(*start_dve.did(0, "mix"))

            def x(k):
                v.wait_ge(*start_pe.at(0, f"x{k}"))
                v.tensor_copy(xT[:, k, S0:TOK], pm[:, 2 * (k % 2) + 1, 0:SAMPLE]).then_inc(*start_dve.did(0, f"x{k}"))

            def params():
                v.wait_ge(*start_pe.at(0, "par"))
                for t, rows in enumerate(PAR_ROWS):
                    r0 = 0 if t else KC
                    src = C[:, t * P + r0:t * P + rows] if t < 4 else DD[:, 0:rows]
                    q = v.tensor_copy(par[:, t * P + r0:t * P + rows], src)
                q.then_inc(*start_dve.did(0, "par"))
                v.wait_ge(*start_pe.at(0, "row8"))
                v.tensor_copy(small[:, 0:8], A[:, 0:8]).then_inc(*start_dve.did(0, "pad"))

            def square(s, k):
                if k:
                    v.wait_ge(*feed_act.at(s, f"sq{k}"))
                    settle(feed_dve)
                    v.tensor_tensor(NS[:], NS[:], SQ[:, k % 2, :], ALU.add).then_inc(*feed_dve.did(s, f"ns{k}"))

            def split(s, k):
                name = ("mix", "attn", "ffn")[s]
                v.wait_ge(*feed_act.at(s, f"hi{k}"))
                v.scalar_tensor_tensor(XL[:, k, :], xT[:, k, :], col(name, k), XH[:, k, :].bitcast(F32), ALU.mult,
                                       ALU.subtract).then_inc(*feed_dve.did(s, f"lo{k}"))

            low_done = [min(LOW_BY_DVE)]

            def split_low(last):
                while low_done[0] <= last and low_done[0] in LOW_BY_DVE:
                    n = low_done[0]
                    v.wait_ge(w_high, n + 1)
                    v.wait_ge(w_low, n)
                    v.tensor_tensor(WL[:, n % HL, :], raw[:, n % RAW, :], WH[:, n % HL, :].bitcast(F32), ALU.subtract).then_inc(w_low, 1)
                    low_done[0] += 1

            def post(g):
                split_low(LAST_SLOT[g] + 1)
                evacuate(g)
                split_low(LAST_SLOT[g] + 2)

            def evacuate(g):
                kind, i = OUTS[g]
                ps = pg[PAIR[g]]
                if (kind, i) == ("up_gate", 0):
                    v.wait_ge(*at_pe.at(3, "pv"))
                    v.memset(pre_f[:, 0, 0:PRE], 0.0).then_inc(*post_dve.did(g, "zero"))
                v.wait_ge(slot_done, LAST_SLOT[g] + 1)
                if kind in ("w_out", "w_o", "down"):
                    if kind == "down":
                        pass
                    v.tensor_tensor(halves(xT[:, i, :]), ps[:, :, 0:HALF], halves(xT[:, i, :]), ALU.add)\
                        .then_inc(*post_dve.did(g, "evac"))
                    return
                if kind in ("w_k", "w_v"):
                    v.wait_ge(*mem_act.at(0, "exp"))
                    to = (Kn if kind == "w_k" else Vn)
                    for t in range(2):
                        q = v.tensor_scalar(to[:, t, i * 256:(i + 1) * 256], ps[:, t, 0:N_MEM], mstat[:, 4 + t:5 + t], None, ALU.mult)
                    q.then_inc(*post_dve.did(g, "evac"))
                    return
                v.wait_ge(*norm_act.at(0 if g < G_WOUT else 1 if kind == "w_q" else 2, "exp"))
                if kind == "gates":
                    v.tensor_tensor(halves(gT[:]), ps[0:8, :, 0:HALF], Rh[0:8], ALU.mult).then_inc(*post_dve.did(g, "evac"))
                    return
                if kind not in CONV:
                    to = {"z": zT, "b_gate": gateT, "c_q": cqT, "c_f": ckT, "c_i": cvT, "c_g": cgT, "w_q": qT}[kind]
                    v.tensor_tensor(halves(to[:, i, :]), ps[:, :, 0:HALF], Rh, ALU.mult).then_inc(*post_dve.did(g, "evac"))
                    return
                taps, b = CONV[kind], conv_no[0] % 2
                conv_no[0] += 1
                pre = pre_m[:, b, :] if kind in ("qkv", "b_x") else pre_f[:, 0, :]
                settle(post_dve)
                v.tensor_tensor(halves(pre[:, PRE:PRE + TOK]), ps[:, :, 0:HALF], Rh, ALU.mult).then_inc(*post_dve.did(g, "evac"))
                settle(post_dve)
                ch = i + (NF if kind == "up_val" else 0)
                past = {"qkv": par[:, COL["a_st"] + i:COL["a_st"] + i + 25:12], "b_x": par[:, COL["b_st"] + i:COL["b_st"] + i + 5:2],
                        }.get(kind, par[:, COL["f_st0"] + ch:COL["f_st0"] + ch + 85:84])
                v.tensor_copy(pre[:, PRE + S0 - taps + 1:PRE + S0], past).then_inc(*post_dve.did(g, "state"))
                for r, end in enumerate((PRE + PROMPT, PRE + TOK)):
                    if kind == "qkv":
                        to = tails[:, r, i:i + 25:12]
                    elif kind == "b_x":
                        to = tails[:, r, 36 + i:36 + i + 5:2]
                    else:
                        to = tail_f[:, r, :, ch]
                    q = v.tensor_copy(to, pre[:, end - taps + 1:end])
                q.then_inc(*post_dve.did(g, "tail"))
                acc = {"qkv": qkvT, "b_x": xbT}[kind][:, i, :] if kind in ("qkv", "b_x") else fg[:] if kind == "up_gate" else fv[:]
                wcol = {"qkv": [COL["a_w"] + 12 * j + i for j in range(4)], "b_x": [COL["b_w"] + 2 * j + i for j in range(4)]}.get(
                    kind, [COL["f_w"] + ch, COL["f_w"] + 44 + ch, COL["f_w2"] + ch])
                bias = {"b_x": col("b_b", i)}.get(kind, None if kind == "qkv" else col("f_b", ch))
                if kind == "up_val" and i:
                    v.wait_ge(*post_pool.at(g - 2, "lo"))
                off = PRE + 1 - taps
                settle(post_dve)
                w0 = par[:, wcol[0]:wcol[0] + 1]
                if bias is None:
                    v.tensor_scalar(acc, pre[:, off:off + TOK], w0, None, ALU.mult).then_inc(*post_dve.did(g, "tap0"))
                else:
                    v.tensor_scalar(acc, pre[:, off:off + TOK], w0, bias, ALU.mult, ALU.add).then_inc(*post_dve.did(g, "tap0"))
                for j in range(1, taps):
                    settle(post_dve)
                    v.scalar_tensor_tensor(acc, pre[:, off + j:off + j + TOK], par[:, wcol[j]:wcol[j] + 1], acc, ALU.mult,
                                           ALU.add).then_inc(*post_dve.did(g, f"tap{j}"))
                if kind == "up_val":
                    v.wait_ge(*post_act.at(g - 1, "silu"))
                    settle(post_dve)
                    v.tensor_tensor(fv[:], fg[:], fv[:], ALU.mult).then_inc(*post_dve.did(g, "prod"))

            def gv_(r):
                return gv[:, r, 0:TILES * HEADS]

            def gate_rows(part):
                if part == 0:
                    v.memset(gv8, 0.0).then_inc(*gate_dve.did(0, "clear"))
                    v.wait_ge(*gate_pe.at(0, "turn"))
                    settle(gate_dve)
                    v.tensor_copy(gv8[:, 0:32], C[:, 0:32]).then_inc(*gate_dve.did(0, "rows"))
                    v.tensor_copy(gv8[0:SAMPLE, 32:40], C[0:SAMPLE, 32:40]).then_inc(*gate_dve.did(0, "rows4"))
                    settle(gate_dve)
                    z = gv_(2).rearrange("p (c h) -> p c h", h=4)
                    v.tensor_tensor(z, gv8.rearrange("p (c h) -> p c h", h=8)[:, :, 4:8], over(small[:, 4:8], TILES), ALU.add)\
                        .then_inc(*gate_dve.did(0, "arg"))
                    settle(gate_dve)
                    v.tensor_scalar(gv_(3), gv_(2), 0.0, None, ALU.max).then_inc(*gate_dve.did(0, "pos"))
                    v.scalar_tensor_tensor(gv_(4), gv_(2), -1.0, gv_(2), ALU.mult, ALU.max).then_inc(*gate_dve.did(0, "neg"))
                if part == 1:
                    v.wait_ge(*gate_act.at(0, "ln"))
                    settle(gate_dve)
                    v.tensor_tensor(gv_(3), gv_(3), gv_(4), ALU.add).then_inc(*gate_dve.did(0, "g0"))
                    settle(gate_dve)
                    v.scalar_tensor_tensor(gv_(1).rearrange("p (c h) -> p c h", h=4), gv_(3).rearrange("p (c h) -> p c h", h=4), -1.0,
                                           over(small[:, 44:48], TILES), ALU.mult, ALU.mult).then_inc(*gate_dve.did(0, "g"))
                if part == 2:
                    v.wait_ge(*gate_pe.at(0, "gl"))
                    v.tensor_copy(gv_(2), DD[:, 0:TILES * HEADS]).then_inc(*gate_dve.did(0, "gc"))
                    v.tensor_copy(gv_(5), DD[:, 32:32 + TILES * HEADS]).then_inc(*gate_dve.did(0, "gl"))
                    settle(gate_dve)
                    v.tensor_tensor(gv_(6), gv_(5), gv_(2), ALU.subtract).then_inc(*gate_dve.did(0, "kd"))
                if part == 3:
                    v.wait_ge(*gate_act.at(0, "egc"))
                    v.tensor_tensor(gv_(4), gv_(0), gv_(3), ALU.mult).then_inc(*gate_dve.did(0, "be"))

            def rg_tmp(i):
                return tmp[:].rearrange("p a b -> p (a b)")[:, i * TOK:(i + 1) * TOK]

            def l2exp():
                v.wait_ge(*l2_act.at(8, "exp1"))
                for i in range(8):
                    v.tensor_tensor(qkvT[:, i, :], qkvT[:, i, :], rg_tmp(i), ALU.mult).then_inc(*l2_dve.did(i, "n"))

            def rg(part):
                if part == 0:
                    v.tensor_scalar(small[:, 48:50], col("lam", 0, 2), -1.0, None, ALU.mult).then_inc(*rg_dve.did(0, "nlam"))
                    v.scalar_tensor_tensor(small[:, 50:52], col("lam", 0, 2), -1.0, col("lam", 0, 2), ALU.mult, ALU.max)\
                        .then_inc(*rg_dve.did(0, "abs"))
                    v.wait_ge(*rg_act.at(0, "ln"))
                    settle(rg_dve)
                    v.scalar_tensor_tensor(small[:, 48:50], small[:, 48:50], 0.0, small[:, 50:52], ALU.max, ALU.add)\
                        .then_inc(*rg_dve.did(0, "sp"))
                    settle(rg_dve)
                    v.tensor_scalar(small[:, 52:54], small[:, 48:50], -8.0, None, ALU.mult).then_inc(*rg_dve.did(0, "c8"))
                    v.tensor_scalar(small[:, 54:56], small[:, 48:50], 8.0, None, ALU.mult).then_inc(*rg_dve.did(0, "c8n"))
                if part == 2:
                    for i in range(2):
                        v.wait_ge(*rg_act.at(4 + i, "th"))
                        settle(rg_dve)
                        v.tensor_tensor(rg_tmp(8), rg_tmp(4 + i), rg_tmp(4 + i), ALU.mult).then_inc(*rg_dve.did(1 + i, "a2"))
                        settle(rg_dve)
                        v.scalar_tensor_tensor(rg_tmp(6 + i), rg_tmp(8), 1.0, rg_tmp(6 + i), ALU.add, ALU.mult)\
                            .then_inc(*rg_dve.did(1 + i, "m2"))
                        v.tensor_tensor(rg_tmp(2 + i), rg_tmp(2 + i), xbT[:, i, :], ALU.mult).then_inc(*rg_dve.did(1 + i, "gx"))
                if part < 3:
                    return
                i = part - 3
                v.wait_ge(*rg_act.at(6, "mult"))
                v.memset(rg_tmp(i)[:, PROMPT:S0], 0.0).then_inc(*rg_dve.did(3 + i, "gap"))
                settle(rg_dve)
                v.tensor_tensor(rg_tmp(2 + i), rg_tmp(2 + i), rg_tmp(6 + i), ALU.mult).then_inc(*rg_dve.did(3 + i, "u"))
                settle(rg_dve)
                v.tensor_tensor_scan(rg_tmp(i)[:, 0:PROMPT], rg_tmp(4 + i)[:, 0:PROMPT], rg_tmp(2 + i)[:, 0:PROMPT], 0.0,
                                     ALU.mult, ALU.add).then_inc(*rg_dve.did(3 + i, "scan"))
                v.tensor_tensor_scan(rg_tmp(i)[:, S0:TOK], rg_tmp(4 + i)[:, S0:TOK], rg_tmp(2 + i)[:, S0:TOK],
                                     col("b_h", i), ALU.mult, ALU.add).then_inc(*rg_dve.did(3 + i, "scan_s"))
                settle(rg_dve)
                v.tensor_copy(tails[:, 0, 42 + i:43 + i], rg_tmp(i)[:, PROMPT - 1:PROMPT])
                v.tensor_copy(tails[:, 1, 42 + i:43 + i], rg_tmp(i)[:, TOK - 1:TOK]).then_inc(*rg_dve.did(3 + i, "ht"))
                v.wait_ge(*post_act.at(G_OF[("b_gate", i)], "gelu"))
                v.tensor_tensor(gateT[:, i, :], gateT[:, i, :], rg_tmp(i), ALU.mult).then_inc(*rg_dve.did(3 + i, "y"))

            def hg_prep(part):
                lb = small[:, 56:58]
                if part == 0:
                    v.tensor_tensor(lb, col("lb", 0, 2), col("lb", 0, 2), ALU.subtract).then_inc(*hgp_dve.did(0, "e0"))
                    v.wait_ge(*rg_dve.at(2, "gx"))
                    v.memset(hQ, 0.0).then_inc(*hgp_dve.did(0, "q"))
                    v.memset(vpad[:], 0.0).then_inc(*hgp_dve.did(0, "v"))
                if part == 1:
                    v.wait_ge(*hgp_act.at(0, "e"))
                    v.reciprocal(small[:, 58:60], lb).then_inc(*hgp_dve.did(0, "rec"))
                    settle(hgp_dve)
                    v.tensor_tensor(small[:, 58:60], small[:, 58:60], lb, ALU.mult).then_inc(*hgp_dve.did(0, "sm"))
                    settle(hgp_dve)
                    v.tensor_tensor(lb, small[:, 58:60], small[:, 58:60], ALU.subtract).then_inc(*hgp_dve.did(0, "lb"))
                    settle(hgp_dve)
                    v.tensor_scalar(small[:, 58:60], lb, -1.0, 1.0, ALU.mult, ALU.add).then_inc(*hgp_dve.did(0, "oml"))
                    v.wait_ge(*post_act.at(G_OF[("c_f", 1)], "sig"))
                    settle(hgp_dve)
                    for i in range(2):
                        q = v.tensor_scalar(ckT[:, i, :], ckT[:, i, :], small[:, 58 + i:59 + i], small[:, 56 + i:57 + i], ALU.mult, ALU.add)
                    q.then_inc(*hgp_dve.did(1, "f"))
                if part == 3:
                    v.wait_ge(*hgp_act.at(1, "lf"))
                    v.tensor_scalar(ckT[:], ckT[:], -1.0, 1.0, ALU.mult, ALU.add).then_inc(*hgp_dve.did(1, "k"))
                    for i in range(2):
                        for c in range(TILES):
                            n, t0 = tile_len(c), tile_at(c)
                            v.tensor_tensor_scan(cbT[:, i, t0:t0 + n], ones[:, 0:n], cbT[:, i, t0:t0 + n], 0.0, ALU.mult, ALU.add)\
                                .then_inc(*hgp_dve.did(1, f"b{i}_{c}"))

            def gdn(c, p, ph):
                n, t0 = tile_len(c), tile_at(c)
                last = levels_of(c) - 1
                pe_, act_, pool_ = gdn_pe[p], gdn_act[p], gdn_pool[p]
                g2 = slice(4 * c + 2 * p, 4 * c + 2 * p + 2)
                Pb, Qb = PAIR_BANKS[p]

                def T(i):
                    return Tp(i, p)

                def did(name):
                    return gdn_dve[p].did(c, name)

                def ready():
                    settle(gdn_dve[p])

                def gate(r, h):
                    return gv[0:n, r, g2.start + h:g2.start + h + 1]

                if ph == "rows":
                    v.wait_ge(*pe_.at(c, "rows"))
                    ready()
                    v.tensor_tensor(T(4)[0:n], half_of(Pb, 1)[0:n], cols(gv[0:n, 0, g2], P), ALU.mult).then_inc(*did("vb"))
                    v.wait_ge(*gate_act.at(0, "ekd"))
                    v.tensor_tensor(T(3)[0:n], half_of(Pb, 0)[0:n], cols(gv[0:n, 6, g2], P), ALU.mult).then_inc(*did("kd"))
                elif ph == "decay":
                    v.wait_ge(*act_.at(c, "gbe"))
                    ready()
                    for h in range(2):
                        q = v.tensor_scalar(T(0)[0:n, h, 0:n], T(6)[0:n, h, 0:n], gate(2, h), 0.0, ALU.subtract, ALU.min)
                    q.then_inc(*did("gd"))
                elif ph == "L":
                    v.wait_ge(*pe_.at(c, "kk"))
                    v.wait_ge(*pool_.at(c, "bPT"))
                    v.tensor_tensor(T(10)[0:n, :, 0:n], half_of(Pb, 0)[0:n, :, 0:n], T(1)[0:n, :, 0:n], ALU.mult).then_inc(*did("LT"))
                    v.tensor_tensor(T(11)[0:n, :, 0:n], half_of(Pb, 1)[0:n, :, 0:n], T(0)[0:n, :, 0:n], ALU.mult).then_inc(*did("QKT"))
                    ready()
                    v.tensor_tensor(T(5)[0:n, :, 0:n], T(10)[0:n, :, 0:n], over(lev[0:n, 0, 0:n], 2), ALU.mult).then_inc(*did("Ut"))
                    ready()
                    v.tensor_tensor(T(5)[0:n, :, 0:n], over(ident[0:n, 0:n], 2), T(5)[0:n, :, 0:n], ALU.subtract).then_inc(*did("U0"))
                elif ph[0] == "X":
                    l = int(ph[1:])
                    Rt, Rx = (half_of(b, 0) for b in level_banks(p, l))
                    if l < last:
                        v.wait_ge(*pe_.at(c, f"X{l}"))
                        ready()
                        v.scalar_tensor_tensor(T(2)[0:n, :, 0:n], Rx[0:n, :, 0:n], -1.0, T(2)[0:n, :, 0:n], ALU.mult, ALU.add)\
                            .then_inc(*did(f"X{l}"))
                        return
                    else:
                        v.wait_ge(*pe_.at(c, "ks"))
                        ready()
                        for h in range(2):
                            q = v.scalar_tensor_tensor(T(6)[0:n, h, :], Rx[0:n, h, :], gate(4, h), T(4)[0:n, h, :], ALU.mult, ALU.subtract)
                        q.then_inc(*did("r"))
                    v.wait_ge(*pe_.at(c, f"U{l}"))
                    v.scalar_tensor_tensor(T(5)[0:n, :, 0:n], Rt[0:n, :, 0:n], -1.0, T(5)[0:n, :, 0:n], ALU.mult, ALU.add)\
                        .then_inc(*did(f"U{l}"))
                elif ph == "o":
                    S = heads(Sa[:, 1 if c == TILES - 1 else 0, :])[:, 2 * p:2 * p + 2, :]
                    Rx = half_of(level_banks(p, last)[1], 0)
                    v.wait_ge(*pe_.at(c, "S"))
                    for h in range(2):
                        q = v.scalar_tensor_tensor(S[:, h, :], S[:, h, :], gv[:, 5, g2.start + h:g2.start + h + 1], Rx[:, h, :], ALU.mult, ALU.add)
                    q.then_inc(*did("S"))
                elif ph == "on":
                    o = qkvT[:, 2 * p:2 * p + 2, t0:t0 + n]
                    v.wait_ge(*act_.at(c, "exp"))
                    v.scalar_tensor_tensor(o, o, col("a_norm"), T(6)[:, :, 0:n], ALU.mult, ALU.mult).then_inc(*did("on"))
                elif ph == "oz":
                    o = qkvT[:, 2 * p:2 * p + 2, t0:t0 + n]
                    v.wait_ge(*gdn_dve[p].at(c, "on"))
                    v.wait_ge(*post_act.at(G_OF[("z", 2 * p + 1)], "silu"))
                    v.tensor_tensor(o, o, zT[:, 2 * p:2 * p + 2, t0:t0 + n], ALU.mult).then_inc(*gdn_oz[p].did(c, "oz"))

            def hg(c, ph):
                n, t0 = tile_len(c), tile_at(c)
                d4 = DD.rearrange("p (a b i) -> p a b i", a=2, b=2)
                aq = att.rearrange("p a b i -> p (a b) i")[0:n, :, 0:n]
                D_ = lambda name: hg_dve.did(c, name)
                def parts(ap, s):
                    return ap.rearrange("p i (b h r) -> p i b h r", h=2, r=s)

                def exponents(l):
                    s = 1 << (l - 1)
                    bb, E = parts(cbT[:, :, t0:t0 + n], s), parts(hE[:, :, 0:n], s)
                    ref = bb[:, :, :, 0, s - 1:s].to_broadcast([P, 2, n // (2 * s), s])
                    if l > 1:
                        v.wait_ge(*hg_pool.at(c, f"k{l - 1}"))
                    settle(hg_dve)
                    v.tensor_tensor(E[:, :, :, 0, :], ref, bb[:, :, :, 0, :], ALU.subtract).then_inc(*D_(f"dk{l}"))
                    v.tensor_tensor(E[:, :, :, 1, :], bb[:, :, :, 1, :], ref, ALU.subtract).then_inc(*D_(f"dq{l}"))

                def keep(l):
                    v.wait_ge(*hg_pe.at(c, f"A{l}"))
                    settle(hg_dve)
                    dq = heads(hg_bank(l))[0:n, :, 0:n]
                    if l:
                        v.copy_predicated(aq, over(lev[0:n, l - 1, 0:n].bitcast(U32), HEADS), dq).then_inc(*D_(f"att{l}"))
                    else:
                        v.tensor_tensor(aq, dq, over(ident[0:n, 0:n], HEADS), ALU.mult).then_inc(*D_("att0"))

                if ph == "v":
                    if c:
                        v.wait_ge(*hg_pe.at(c - 1, "S"))
                    else:
                        v.wait_ge(*hgp_dve.at(1, f"b1_{TILES - 1}"))
                        v.wait_ge(const_ready, CONSTS)
                        v.wait_ge(*post_act.at(G_OF[("c_q", 1)], "silu"))
                    for par_ in range(2):
                        r = slice(64 * par_, 64 * par_ + 64)
                        q = v.tensor_copy(hQ[r, :, par_, 0:n], cqT[r, :, t0:t0 + n])
                    q.then_inc(*D_("q0"))
                    exponents(1)
                elif ph[0] == "b":
                    l = int(ph[1:])
                    s = 1 << (l - 1)
                    v.wait_ge(*hg_act.at(c, f"E{l}"))
                    v.wait_ge(*hg_pe.at(c, f"A{l - 1}"))
                    for par_, nm in enumerate(("qa", "qb")):
                        r = slice(64 * par_, 64 * par_ + 64)
                        dst = parts(hQ[r, :, par_, 0:n], s)[:, :, :, 1, :]
                        src = parts(cqT[r, :, t0:t0 + n], s)[:, :, :, 1, :]
                        v.tensor_tensor(dst, src, parts(hE[r, :, 0:n], s)[:, :, :, 1, :], ALU.mult).then_inc(*D_(f"{nm}{l}"))
                    keep(l - 1)
                elif ph[0] == "a" and ph != "a0" and int(ph[1:]) < levels_of(c):
                    exponents(int(ph[1:]) + 1)
                elif ph == "kd":
                    keep(levels_of(c))
                elif ph == "o":
                    v.wait_ge(*hg_act.at(c, "osq"))
                    Sx = Sc[:, 1 if c == TILES - 1 else 0]
                    for i in range(2):
                        for par_ in range(2):
                            r = slice(64 * par_, 64 * par_ + 64)
                            v.scalar_tensor_tensor(Sx[r, i, r], Sx[r, i, r], small[r, 60 + i:61 + i], d4[r, 1, i, r], ALU.mult,
                                                   ALU.add).then_inc(*D_(f"S{par_}{i}"))

                elif ph == "on":
                    o = cqT[:, :, t0:t0 + n]
                    v.wait_ge(*hg_act.at(c, "exp"))
                    v.scalar_tensor_tensor(o, o, col("c_norm"), hE[:, :, 0:n], ALU.mult, ALU.mult).then_inc(*D_("on"))
                elif ph == "oz":
                    o = cqT[:, :, t0:t0 + n]
                    v.wait_ge(*hg_dve.at(c, "on"))
                    v.wait_ge(*post_act.at(G_OF[("c_g", 1)], "silu"))
                    v.tensor_tensor(o, o, cgT[:, :, t0:t0 + n], ALU.mult).then_inc(*hg_oz.did(c, "oz"))

            def mixed(j):
                return qkvT[:, j, :] if j < 4 else gateT[:, j - 4, :] if j < 6 else cqT[:, j - 6, :]

            def mo(j):
                v.wait_ge(*mo_act.at(j, "hi"))
                v.tensor_tensor(XL[:, j, :], mixed(j), XH[:, j, :].bitcast(F32), ALU.subtract).then_inc(*mo_dve.did(j, "lo"))

            def mem(k):
                v.wait_ge(*mem_act.at(1 + k, "hi"))
                v.scalar_tensor_tensor(memL[:, k, :], pm[:, 2 + k % 2, 0:N_MEM], col("mem", k), memH[:, k, :].bitcast(F32),
                                       ALU.mult, ALU.subtract).then_inc(*mem_dve.did(k, "lo"))

            def attention(h, ph):
                top, low, total, rec = (astat[:, x, :] for x in range(4))
                if ph == "s":
                    if h == 0:
                        v.memset(astat[:], 1.0).then_inc(*at_dve.did(0, "clear"))
                    v.wait_ge(*at_pe.at(h, "s"))
                    settle(at_dve)
                    v.reduce_max(top[:, 0:4], pm[:, 0:2, :].rearrange("p b (c m) -> p (b c) m", m=N_MEM), AX_X).then_inc(*at_dve.did(h, "max"))
                    v.reduce_max(top[0:SAMPLE, 4:5], C[0:SAMPLE, 0:N_MEM], AX_X).then_inc(*at_dve.did(h, "max4"))
                    settle(at_dve)
                    v.tensor_scalar(low, top, -1.0 / 16, None, ALU.mult).then_inc(*at_dve.did(h, "nmax"))
                elif ph == "norm":
                    v.wait_ge(*at_act.at(h, f"exp{TILES - 1}"))
                    v.reciprocal(rec, total).then_inc(*at_dve.did(h, "rec"))
                    settle(at_dve)
                    v.tensor_tensor(prob[:, 0:4, :], prob[:, 0:4, :], cols(rec[:, 0:4], N_MEM), ALU.mult).then_inc(*at_dve.did(h, "norm"))
                    v.tensor_scalar(prob[0:SAMPLE, 4, :], prob[0:SAMPLE, 4, :], rec[0:SAMPLE, 4:5], None, ALU.mult)\
                        .then_inc(*at_dve.did(h, "norm4"))
                elif ph == "pv":
                    v.wait_ge(*at_pe.at(h, "pv"))
                    for d in range(2):
                        v.tensor_copy(qT[:, 2 * h + d, 0:PROMPT], (B, DD)[d]).then_inc(*at_dve.did(h, f"o{d}"))
                    v.tensor_copy(qT[:, 2 * h:2 * h + 2, S0:TOK], C[:, 256:256 + 2 * SAMPLE].rearrange("p (d t) -> p d t", d=2))\
                        .then_inc(*at_dve.did(h, "os"))

            def heads_out(j):
                v.wait_ge(*ho_act.at(j, "hi"))
                v.tensor_tensor(XL[:, j, :], qT[:, j, :], XH[:, j, :].bitcast(F32), ALU.subtract).then_inc(*ho_dve.did(j, "lo"))

            def y_weights(k):
                v.wait_ge(*feed_act.at(3, f"sq{k}"))
                v.tensor_scalar(xT[:, k, :], xT[:, k, :], col("final", k), None, ALU.mult).then_inc(*y_dve.did(k, "w"))

            def ends():
                v.wait_ge(*ends_pe.at(0, "t"))
                v.wait_ge(slot_done, LAST_SLOT[G_DOWN - 1] + 1)
                v.tensor_copy(frows[0:88], A[0:88, 0:256].rearrange("p (r n) -> p r n", r=2)).then_inc(*ends_dve.did(0, "t"))

            def finish():
                v.wait_ge(*y_act.at(KC - 1, "y4"))
                for c in (0, 2, 4):
                    n = tile_len(c)
                    v.tensor_scalar(yrow[0:n, c, :], yrow[0:n, c, :], fstat[0:n, c:c + 1], None, ALU.mult).then_inc(*y_dve.did(KC, f"y{c}"))

            handlers = {"start": start, "x": x, "params": params, "square": square, "split": split, "post": post, "gate_rows": gate_rows, "l2exp": l2exp,
                        "rg": rg, "hg_prep": hg_prep, "gdn": gdn, "hg": hg, "mo": mo, "mem": mem, "att": attention,
                        "heads_out": heads_out, "y_weights": y_weights, "ends": ends, "finish": finish}
            for what, *args in SCHED:
                if what in handlers:
                    handlers[what](*args)

        @block.scalar
        def _(act):
            def f(out, in_, fn, **kw):
                return act.activation(out, in_, fn, **kw)

            done_slots = [0]

            def split_weights(last):
                while done_slots[0] <= min(last, len(SLOTS) - 1):
                    n = done_slots[0]
                    size = P * SLOT_K["down"][SLOTS[n][1]] if OUTS[SLOTS[n][0]][0] == "down" else KC * P
                    act.wait_ge(w_loaded[n % RAW], 16 * (n // RAW + 1))
                    if n >= HL:
                        act.wait_ge(slot_done, n - HL + 1)
                    f(WH[:, n % HL, 0:size], raw[:, n % RAW, 0:size], ACT.Copy).then_inc(w_high, 1)
                    done_slots[0] += 1

            def start():
                t, r0, src = PARAMS[0]
                act.dma_start(par_nat[r0:r0 + src.shape[0], t, :], src).then_inc(mix_loaded, 16)

            def x(k):
                act.wait_ge(*start_pe.at(0, f"x{k}"))
                f(xT[:, k, 0:PROMPT], pm[:, 2 * (k % 2), 0:PROMPT], ACT.Copy).then_inc(*start_act.did(0, f"x{k}"))
                if k == 2:
                    split_weights(0)
                if k == KC - 1:
                    split_weights(1)

            def square(s, k):
                if s:
                    act.wait_ge(*post_dve.at((G_WOUT, G_WO, G_DOWN)[s - 1] + k, "evac"))
                if k == 0:
                    if s:
                        act.wait_ge(*norm_pe.at(s - 1, "ss"))
                    f(NS[:], xT[:, k, :], ACT.Square).then_inc(*feed_act.did(s, f"sq{k}"))
                else:
                    if k >= 2:
                        act.wait_ge(*feed_dve.at(s, f"ns{k - 1}" if k == 2 else f"ns{k - 2}"))
                    f(SQ[:, k % 2, :], xT[:, k, :], ACT.Square).then_inc(*feed_act.did(s, f"sq{k}"))

            def split(s, k):
                if s == 0:
                    act.wait_ge(*start_dve.at(0, f"x{k}"))
                    act.wait_ge(*start_act.at(0, f"x{k}"))
                    act.wait_ge(const_ready, EARLY_CONSTS)
                if k == 0:
                    if s == 1:
                        act.wait_ge(slot_done, LAST_SLOT[G_WK - 1] + 1)
                    if s == 2:
                        act.wait_ge(slot_done, LAST_SLOT[G_UP - 1] + 1)
                        act.wait_ge(stored, 16 * (MIX_STORES + 2))
                f(XH[:, k, :], xT[:, k, :], ACT.Identity, scale=col(("mix", "attn", "ffn")[s], k)).then_inc(*feed_act.did(s, f"hi{k}"))

            def norm(s):
                if s == 0:
                    split_weights(2)
                act.wait_ge(*norm_pe.at(s, "ss"))
                if s:
                    act.wait_ge(*post_dve.at((0, G_WOUT, G_WO)[s] - 1, "evac"))
                f(R[:].rearrange("p (h t) -> p h t", h=2), pm[:, 0:2, 0:HALF], ACT.Ln, bias=EPS, scale=1.0 / D).then_inc(*norm_act.did(s, "ln"))
                act.wait_ge(*norm_act.at(s, "ln"))
                f(R[:], R[:], ACT.Exp, scale=-0.5).then_inc(*norm_act.did(s, "exp"))

            def post(g):
                kind, i = OUTS[g]
                split_weights(LAST_SLOT[g] + HL)
                if kind == "qkv":
                    act.wait_ge(*post_dve.at(g, "tap3"))
                    f(qkvT[:, i, :], qkvT[:, i, :], ACT.Silu).then_inc(*post_act.did(g, "silu"))
                if kind == "c_q":
                    act.wait_ge(*post_dve.at(g, "evac"))
                    f(cqT[:, i, :], cqT[:, i, :], ACT.Silu).then_inc(*post_act.did(g, "silu"))
                if kind == "c_f":
                    act.wait_ge(*post_dve.at(g, "evac"))
                    f(ckT[:, i, :], ckT[:, i, :], ACT.Sigmoid).then_inc(*post_act.did(g, "sig"))
                if kind in ("z", "c_g"):
                    act.wait_ge(*post_dve.at(g, "evac"))
                    to = {"z": zT, "c_g": cgT}[kind][:, i, :]
                    f(to, to, ACT.Silu).then_inc(*post_act.did(g, "silu"))
                if kind == "b_gate":
                    act.wait_ge(*post_dve.at(g, "evac"))
                    f(gateT[:, i, :], gateT[:, i, :], ACT.Gelu_apprx_tanh).then_inc(*post_act.did(g, "gelu"))
                if kind == "up_gate":
                    act.wait_ge(*post_dve.at(g, "tap2"))
                    f(fg[:], fg[:], ACT.Silu).then_inc(*post_act.did(g, "silu"))
                if kind == "up_val":
                    act.wait_ge(*post_dve.at(g, "prod"))
                    f(FH[:, i, :], fv[:], ACT.Copy).then_inc(*post_act.did(g, "hi"))

            def gv_(r):
                return gv[:, r, 0:TILES * HEADS]

            def gate_rows(part):
                if part == 0:
                    act.wait_ge(*gate_dve.at(0, "rows4"))
                    f(gv_(0).rearrange("p (c h) -> p c h", h=4), gv8.rearrange("p (c h) -> p c h", h=8)[:, :, 0:4], ACT.Sigmoid)\
                        .then_inc(*gate_act.did(0, "beta"))
                    act.wait_ge(*start_dve.at(0, "pad"))
                    f(small[:, 44:48], small[:, 0:4], ACT.Exp).then_inc(*gate_act.did(0, "eA"))
                    act.wait_ge(*gate_dve.at(0, "neg"))
                    f(gv_(4), gv_(4), ACT.Exp, scale=-1.0).then_inc(*gate_act.did(0, "exp"))
                    act.wait_ge(*gate_act.at(0, "exp"))
                    f(gv_(4), gv_(4), ACT.Ln, bias=1.0).then_inc(*gate_act.did(0, "ln"))
                if part == 3:
                    act.wait_ge(*gate_dve.at(0, "gc"))
                    f(gv_(3), gv_(2), ACT.Exp).then_inc(*gate_act.did(0, "egc"))
                    act.wait_ge(*gate_dve.at(0, "kd"))
                    f(gv8, gv8, ACT.Exp).then_inc(*gate_act.did(0, "ekd"))

            def rg_tmp(i, n=1):
                return tmp[:].rearrange("p a b -> p (a b)")[:, i * TOK:(i + n) * TOK]

            def l2sq(i):
                if i >= 2:
                    act.wait_ge(*l2_pe.at(i - 2, "ss"))
                else:
                    act.wait_ge(*feed_dve.at(0, f"ns{KC - 1}"))
                act.wait_ge(*post_act.at(G_OF[("qkv", i)], "silu"))
                f(SQ[:, i % 2, :], qkvT[:, i, :], ACT.Square).then_inc(*l2_act.did(i, "sq"))

            def l2(i):
                act.wait_ge(*l2_pe.at(i, "ss"))
                f(rg_tmp(i).rearrange("p (h t) -> p h t", h=2), pm[:, 2 * (i % 2):2 * (i % 2) + 2, 0:HALF], ACT.Ln, bias=EPS)\
                    .then_inc(*l2_act.did(i, "ln"))

            def l2exp():
                act.wait_ge(*l2_act.at(7, "ln"))
                f(rg_tmp(0, 4), rg_tmp(0, 4), ACT.Exp, scale=-0.5, bias=LN_SCALE).then_inc(*l2_act.did(8, "exp0"))
                f(rg_tmp(4, 4), rg_tmp(4, 4), ACT.Exp, scale=-0.5).then_inc(*l2_act.did(8, "exp1"))

            def rg(part):
                if part == 0:
                    act.wait_ge(*rg_dve.at(0, "abs"))
                    f(small[:, 50:52], small[:, 50:52], ACT.Exp, scale=-1.0).then_inc(*rg_act.did(0, "exp"))
                    act.wait_ge(*rg_act.at(0, "exp"))
                    f(small[:, 50:52], small[:, 50:52], ACT.Ln, bias=1.0).then_inc(*rg_act.did(0, "ln"))
                    act.wait_ge(*l2_dve.at(7, "n"))
                if part < 2:
                    i = part
                    act.wait_ge(*rg_pe.at(i, "gates"))
                    f(rg_tmp(i).rearrange("p (h t) -> p h t", h=2), pm[:, 0:2, 0:HALF], ACT.Sigmoid, bias=col("b_r", i)).then_inc(*rg_act.did(1 + i, "r"))
                    f(rg_tmp(2 + i).rearrange("p (h t) -> p h t", h=2), pm[:, 2:4, 0:HALF], ACT.Sigmoid, bias=col("b_i", i)).then_inc(*rg_act.did(1 + i, "i"))
                if part == 2:
                    act.wait_ge(*rg_dve.at(0, "c8n"))
                    act.wait_ge(*rg_act.at(2, "i"))
                    for i in range(2):
                        f(rg_tmp(4 + i), rg_tmp(i), ACT.Exp, scale=small[:, 52 + i:53 + i]).then_inc(*rg_act.did(4 + i, "a"))
                        f(rg_tmp(6 + i), rg_tmp(i), ACT.Tanh, scale=small[:, 54 + i:55 + i]).then_inc(*rg_act.did(4 + i, "th"))
                if part == 3:
                    act.wait_ge(*rg_dve.at(2, "m2"))
                    f(rg_tmp(6, 2), rg_tmp(6, 2), ACT.Sqrt).then_inc(*rg_act.did(6, "mult"))

            def hg_prep(part):
                if part == 0:
                    act.wait_ge(*hgp_dve.at(0, "e0"))
                    f(small[:, 56:58], small[:, 56:58], ACT.Exp).then_inc(*hgp_act.did(0, "e"))
                if part == 2:
                    act.wait_ge(*hgp_dve.at(1, "f"))
                    f(cbT[:], ckT[:], ACT.Ln).then_inc(*hgp_act.did(1, "lf"))

            def gdn(c, p, ph):
                n, t0 = tile_len(c), tile_at(c)
                last = levels_of(c) - 1
                pe_, dve, own = gdn_pe[p], gdn_dve[p], gdn_act[p]

                def T(i):
                    return Tp(i, p)

                if ph == "rows":
                    act.wait_ge(*pe_.at(c, "gb"))
                    if c:
                        act.wait_ge(*dve.at(c - 1, "on"))
                    else:
                        act.wait_ge(*rg_dve.at(4, "y"))
                    to = tmp[:, 6:9:2, 256 * p:256 * p + 256].rearrange("p x (h i) -> p x h i", h=2)
                    src = PAIR_BANKS[p][1].rearrange("p (x h i) -> p x h i", x=2, h=2)
                    if n == P:
                        f(tmp[:, 6:9:2, 256 * p:256 * p + 256], PAIR_BANKS[p][1].rearrange("p (x i) -> p x i", x=2), ACT.Copy)\
                            .then_inc(*own.did(c, "gbe"))
                    else:
                        f(to[:, :, :, 0:n], src[:, :, :, 0:n], ACT.Copy).then_inc(*own.did(c, "gbe"))
                elif ph == "decay":
                    act.wait_ge(*dve.at(c, "gd"))
                    f(T(0)[0:n, :, 0:n], T(0)[0:n, :, 0:n], ACT.Exp).then_inc(*own.did(c, "PT"))
                    f(T(9)[:, :, 0:n], T(6)[:, :, 0:n], ACT.Exp).then_inc(*own.did(c, "egb"))
                elif ph == "turn":
                    act.wait_ge(*pe_.at(c, "X0"))
                    f(T(2)[0:n, :, 0:n], half_of(PAIR_BANKS[p][1], 0)[0:n, :, 0:n], ACT.Copy).then_inc(*own.did(c, "X0"))
                elif ph[0] == "T":
                    l = int(ph[1:])
                    act.wait_ge(*pe_.at(c, f"T{l}"))
                    act.wait_ge(*dve.at(c, "U0"))
                    bank = level_banks(p, l)[0]
                    if l == 1:
                        f(T(0)[0:n, :, 0:n], half_of(bank, 0)[0:n, :, 0:n], ACT.Copy).then_inc(*own.did(c, "T1"))
                        return
                    to, src = tmp[0:n, 0:6:5, 256 * p:256 * p + 256], bank[0:n].rearrange("p (x i) -> p x i", x=2)
                    if n < P:
                        to, src = (a.rearrange("p x (h i) -> p x h i", h=2)[:, :, :, 0:n] for a in (to, src))
                    f(to, src, ACT.Copy).then_inc(*own.did(c, f"T{l}"))
                elif ph == "vnew":
                    act.wait_ge(*pe_.at(c, "vnew"))
                    f(T(7)[0:n], half_of(level_banks(p, last)[1], 0)[0:n], ACT.Copy, scale=-1.0).then_inc(*own.did(c, "vn"))
                elif ph == "o":
                    Rt = half_of(level_banks(p, last)[0], 0)
                    act.wait_ge(*pe_.at(c, "o"))
                    f(qkvT[:, 2 * p:2 * p + 2, t0:t0 + n], Rt[:, :, 0:n], ACT.Copy).then_inc(*own.did(c, "o"))
                    f(T(0)[:, :, 0:n], Rt[:, :, 0:n], ACT.Square).then_inc(*own.did(c, "osq"))
                    if c >= TILES - 2:
                        r, to = (0, pa_S) if c == TILES - 2 else (1, sa_S)
                        act.wait_ge(*dve.at(c, "S"))
                        act.dma_start(to[0, 0, 2 * p:2 * p + 2].rearrange("h k v -> k h v"), heads(Sa[:, r, :])[:, 2 * p:2 * p + 2])\
                            .then_inc(stored, 16)
                elif ph == "ss":
                    act.wait_ge(*pe_.at(c, "ss"))
                    f(T(6)[:, :, 0:n], half_of(level_banks(p, last)[0], 1)[:, :, 0:n], ACT.Ln, bias=EPS, scale=1.0 / P).then_inc(*own.did(c, "ln"))
                    act.wait_ge(*own.at(c, "ln"))
                    f(T(6)[:, :, 0:n], T(6)[:, :, 0:n], ACT.Exp, scale=-0.5).then_inc(*own.did(c, "exp"))

            def hg(c, ph):
                n, t0 = tile_len(c), tile_at(c)
                D_ = lambda name: hg_act.did(c, name)
                d4 = DD.rearrange("p (a b i) -> p a b i", a=2, b=2)
                d2 = DD[:, 0:256].rearrange("p (a i) -> p a i", a=2)

                def E(l):
                    act.wait_ge(*hg_dve.at(c, f"dq{l}"))
                    f(hE[:, :, 0:n], hE[:, :, 0:n], ACT.Exp).then_inc(*D_(f"E{l}"))

                if ph == "v":
                    act.wait_ge(*hg_pe.at(c, "v"))
                    act.wait_ge(const_ready, CONSTS)
                    f(vpad[0:n, :, 0, 0:64], d2[0:n, :, 0:64], ACT.Copy).then_inc(*D_("v0"))
                    f(vpad[0:n, :, 1, 64:128], d2[0:n, :, 64:128], ACT.Copy).then_inc(*D_("v1"))
                    E(1)
                elif ph[0] == "a" and ph != "a0" and int(ph[1:]) < levels_of(c):
                    E(int(ph[1:]) + 1)
                elif ph == f"a{levels_of(c)}":
                    act.wait_ge(*hg_pool.at(c, f"k{levels_of(c)}"))
                    act.wait_ge(*hg_dve.at(c, f"qb{levels_of(c)}"))
                    for i in range(2):
                        f(hE[:, i, 0:n], cbT[:, i, t0:t0 + n], ACT.Exp, scale=-1.0, bias=cbT[:, i, t0 + n - 1:t0 + n]).then_inc(*D_(f"ek{i}"))
                elif ph == "kdt":
                    act.wait_ge(*hg_pool.at(c, "kd"))
                    f(hE[:, :, 0:n], cbT[:, :, t0:t0 + n], ACT.Exp).then_inc(*D_("eq"))
                    f(small[:, 60:62], cbT[:, :, t0 + n - 1], ACT.Exp).then_inc(*D_("eb"))
                    act.wait_ge(*hg_pe.at(c, "kd"))
                    f(kdt[0:n], d2[0:n], ACT.Copy).then_inc(*D_("kdt"))
                elif ph == "o":
                    act.wait_ge(*hg_pe.at(c, "o"))
                    act.wait_ge(*hg_pe.at(c, "S"))
                    f(cqT[:, :, t0:t0 + n], d4[:, 0, :, 0:n], ACT.Copy).then_inc(*D_("o"))
                    f(hE[:, :, 0:n], d4[:, 0, :, 0:n], ACT.Square).then_inc(*D_("osq"))
                    if c >= TILES - 2:
                        r, to = (0, pc_S) if c == TILES - 2 else (1, sc_S)
                        act.wait_ge(*hg_dve.at(c, "S11"))
                        for par_ in range(2):
                            s = slice(64 * par_, 64 * par_ + 64)
                            act.dma_start(to[0, 0].rearrange("(i q) k v -> q k i v", q=2)[par_], Sc[s, r, :, s]).then_inc(stored, 16)

                elif ph == "ss":
                    act.wait_ge(*hg_pe.at(c, "ss"))
                    f(hE[:, :, 0:n], d4[:, 0, :, 0:n], ACT.Ln, bias=EPS, scale=1.0 / 64).then_inc(*D_("ln"))
                    act.wait_ge(*hg_act.at(c, "ln"))
                    f(hE[:, :, 0:n], hE[:, :, 0:n], ACT.Exp, scale=-0.5).then_inc(*D_("exp"))

            def mixed(j):
                return qkvT[:, j, :] if j < 4 else gateT[:, j - 4, :] if j < 6 else cqT[:, j - 6, :]

            def mo(j):
                act.wait_ge(slot_done, LAST_SLOT[G_LAST_IN] + 1)
                if j < 4:
                    act.wait_ge(*gdn_oz[j // 2].at(TILES - 1, "oz"))
                elif j < 6:
                    act.wait_ge(*rg_dve.at(j - 1, "y"))
                else:
                    act.wait_ge(*hg_oz.at(TILES - 1, "oz"))
                f(XH[:, j, :], mixed(j), ACT.Copy).then_inc(*mo_act.did(j, "hi"))

            def mix_out():
                act.wait_ge(*mo_pe.at(0, "st"))
                rows = st_rows[0:44, 0:256].rearrange("p (r n) -> p r n", r=2)
                f(rows, pm[0:44, 0:2, 0:P], ACT.Copy).then_inc(*mo_act.did(8, "st"))
                act.wait_ge(*mo_act.at(8, "st"))
                for r, (ta, tb, th) in enumerate(((pa_conv, pb_conv, pb_h), (sa_conv, sb_conv, sb_h))):
                    act.dma_start(ta[0, 0].rearrange("t (i p) -> (t i) p", p=P), rows[0:36, r, :]).then_inc(stored, 16)
                    act.dma_start(tb[0, 0].rearrange("t (i p) -> (t i) p", p=P), rows[36:42, r, :]).then_inc(stored, 16)
                    act.dma_start(th[0, 0].rearrange("(i p) -> i p", p=P), rows[42:44, r, :]).then_inc(stored, 16)

            def memsq():
                act.wait_ge(mem_loaded, 16)
                act.wait_ge(stored, 16 * MIX_STORES)
                for t in range(2):
                    f(Kn[:, t, :], nat[:, t, :], ACT.Square, accum_out=mstat[:, t:t + 1]).then_inc(*mem_act.did(0, f"sq{t}"))
                act.wait_ge(*mem_act.at(0, "sq1"))
                f(mstat[:, 2:4], mstat[:, 0:2], ACT.Ln, bias=EPS, scale=1.0 / D).then_inc(*mem_act.did(0, "ln"))
                act.wait_ge(*mem_act.at(0, "ln"))
                f(mstat[:, 4:6], mstat[:, 2:4], ACT.Exp, scale=-0.5).then_inc(*mem_act.did(0, "exp"))

            def mem(k):
                act.wait_ge(*mem_pe.at(k, "t"))
                f(memH[:, k, :], pm[:, 2 + k % 2, 0:N_MEM], ACT.Identity, scale=col("mem", k)).then_inc(*mem_act.did(1 + k, "hi"))

            def kt(j):
                if j == 0:
                    act.wait_ge(*post_dve.at(G_OF[("w_k", 3)], "evac"))
                    act.dma_start(mem_k_out[0, 0].rearrange("(c p) h d -> p c (h d)", p=P), Kn[:]).then_inc(stored, 16)
                if j == 4:
                    act.wait_ge(*post_dve.at(G_OF[("w_v", 3)], "evac"))
                    act.dma_start(mem_v_out[0, 0].rearrange("(c p) h d -> p c (h d)", p=P), Vn[:]).then_inc(stored, 16)
                act.wait_ge(*kt_pe.at(j, "t"))
                d = 2 * (j % 4)
                f(kT[:, j // 4, d:d + 2, :], pm[:, j % 4, :].rearrange("p (d m) -> p d m", d=2), ACT.Copy).then_inc(*kt_act.did(j, "t"))

            def attention(h, ph):
                if ph == "exp":
                    act.wait_ge(*at_dve.at(h, "nmax"))
                    for c in range(TILES):
                        n = tile_len(c)
                        f(prob[0:n, c, :], pm[0:n, c // 2, (c % 2) * 256:(c % 2 + 1) * 256], ACT.Exp, scale=1.0 / 16,
                          bias=astat[0:n, 1, c:c + 1], accum_out=astat[0:n, 2, c:c + 1]).then_inc(*at_act.did(h, f"exp{c}"))
                elif ph == "pt":
                    act.wait_ge(*at_pe.at(h, "t"))
                    for t in range(2):
                        f(PT[:, t, 0:PROMPT], (DD, A)[t], ACT.Copy).then_inc(*at_act.did(h, f"pt{t}"))
                    f(PT[:, :, PROMPT:PROMPT + SAMPLE], C[:, 0:2 * SAMPLE].rearrange("p (t n) -> p t n", t=2), ACT.Copy)\
                        .then_inc(*at_act.did(h, "pts"))

            def heads_out(j):
                if j == 0:
                    act.wait_ge(slot_done, LAST_SLOT[G_WO - 1] + 1)
                act.wait_ge(*at_dve.at(j // 2, "os"))
                f(XH[:, j, :], qT[:, j, :], ACT.Copy).then_inc(*ho_act.did(j, "hi"))

            def y(k):
                act.wait_ge(*y_pe.at(k, "t"))
                if k == 0:
                    act.wait_ge(slot_done, LAST_SLOT[G_DOWN - 1] + 1)
                f(yrow[:, 0:4, k * P:(k + 1) * P], heads(pm[:, 2 + k % 2, :]), ACT.Copy).then_inc(*y_act.did(k, "y"))
                f(yrow[0:SAMPLE, 4, k * P:(k + 1) * P], B[0:SAMPLE, 0:P], ACT.Copy).then_inc(*y_act.did(k, "y4"))

            def ends():
                act.wait_ge(*ends_dve.at(0, "t"))
                for r, to in enumerate((pf_conv, sf_conv)):
                    act.dma_start(to[0, 0].rearrange("t (c p) -> (t c) p", p=P), frows[0:88, r, :]).then_inc(stored, 16)

            def sums():
                act.wait_ge(*fin_pe.at(0, "ss"))
                parts = [(slice(0, P), slice(0, 4)), (slice(0, SAMPLE), slice(4, 5))]
                totals = A[:, 0:2 * TILES].rearrange("p (c e) -> p c e", e=2)[:, :, 0]
                for p, c in parts:
                    q = f(fstat[p, c], totals[p, c], ACT.Ln, bias=EPS, scale=1.0 / D)
                q.then_inc(*y_act.did(KC, "ln"))
                act.wait_ge(*y_act.at(KC, "ln"))
                for p, c in parts:
                    q = f(fstat[p, c], fstat[p, c], ACT.Exp, scale=-0.5)
                q.then_inc(*y_act.did(KC, "exp"))

            def finish():
                act.wait_ge(*y_act.at(KC - 1, "y"))
                for c in (1, 3):
                    f(yrow[:, c, :], yrow[:, c, :], ACT.Identity, scale=fstat[:, c:c + 1]).then_inc(*y_act.did(KC, f"y{c}"))
                    act.wait_ge(*y_act.at(KC, f"y{c}"))
                    act.dma_start(y_prompt[0, c * P:(c + 1) * P, :], yrow[:, c, :]).then_inc(stored, 16)

            handlers = {"start": start, "x": x, "square": square, "split": split, "norm": norm, "post": post, "l2": l2, "l2sq": l2sq,
                        "l2exp": l2exp, "gate_rows": gate_rows, "rg": rg, "hg_prep": hg_prep, "gdn": gdn, "hg": hg,
                        "mo": mo, "mix_out": mix_out, "memsq": memsq, "mem": mem, "kt": kt, "att": attention, "heads_out": heads_out,
                        "y": y, "ends": ends, "sums": sums, "finish": finish}
            for what, *args in SCHED:
                if what in handlers:
                    handlers[what](*args)

        @block.gpsimd
        def _(pool):
            made = [0]

            def link(ins):
                ins.then_inc(const_ready, 1)
                made[0] += 1
                pool.wait_ge(const_ready, made[0])

            done_slots = [0]

            def split_weights(last):
                while done_slots[0] <= min(last, len(SLOTS) - 1):
                    n = done_slots[0]
                    if n in LOW_BY_DVE:
                        done_slots[0] += 1
                        continue
                    size = P * SLOT_K["down"][SLOTS[n][1]] if OUTS[SLOTS[n][0]][0] == "down" else KC * P
                    pool.wait_ge(w_high, n + 1)
                    if n - 1 in LOW_BY_DVE:
                        pool.wait_ge(w_low, n)
                    pool.tensor_tensor(WL[:, n % HL, 0:size], raw[:, n % RAW, 0:size], WH[:, n % HL, 0:size].bitcast(F32),
                                       ALU.subtract).then_inc(w_low, 1)
                    done_slots[0] += 1

            def select(ap, op, fill, base, pattern, cm):
                return pool.affine_select(out=ap, in_=ap, compare_op=op, fill=fill, base=base, pattern=pattern, channel_multiplier=cm)

            def start():
                link(pool.memset(ident[:], 0.0))
                link(select(ident[:], ALU.not_equal, 1.0, 0, [[-1, P]], 1))
                link(pool.memset(xT[:, :, PROMPT:S0], 0.0))
                link(pool.memset(ones[:], 1.0))
                link(pool.memset(upto_m[:], 1.0))
                link(select(upto_m[:], ALU.is_ge, 0.0, 0, [[1, P]], -1))
                link(pool.memset(pre_m[:, :, 0:PRE], 0.0))
                assert made[0] == EARLY_CONSTS
                link(pool.memset(half_ones[:], 0.0))
                link(pool.memset(half_ones[0:64, 0:64], 1.0))
                link(pool.memset(half_ones[64:128, 64:128], 1.0))
                link(pool.memset(wr_bd[:], 0.0))
                link(pool.memset(Sa[:, 0, :], 0.0))
                link(pool.memset(Sc[:], 0.0))
                link(pool.memset(hK[:], 0.0))
                split_weights(0)
                link(pool.memset(lev[:], 0.0))
                for l in range(LEVELS):
                    s = 1 << l
                    w = lev[:, l, :].rearrange("p (b h r) -> p b h r", h=2, r=s)[:, :, 1, :]
                    nb = P // (2 * s)
                    link(pool.memset(w, 1.0))
                    link(select(w, ALU.is_ge, 0.0, 0, [[-2 * s, nb], [0, s]], 1))
                    link(select(w, ALU.is_ge, 0.0, s - 1, [[2 * s, nb], [0, s]], -1))
                assert made[0] == CONSTS, made[0]
                split_weights(1)

            def state(i):
                q = i % 2
                r = slice(64 * q, 64 * q + 64)
                if i < 4:
                    gate, w = ((0, b_w_r), (1, b_w_i))[i // 2]
                    pool.dma_start(wr_bd[r, gate, :, r], w[0].rearrange("(i q) a b -> q a i b", q=2)[q]).then_inc(state_loaded, 16)
                elif i < 6:
                    pool.dma_start(Sc[r, 1, :, r], state_c_S[0, 0].rearrange("(i q) k v -> q k i v", q=2)[q]).then_inc(state_loaded, 16)
                else:
                    pool.dma_start(heads(Sa[:, 1, :]), state_a_S[0, 0].rearrange("h k v -> k h v")).then_inc(state_loaded, 16)

            def post(g):
                split_weights(LAST_SLOT[g] + HL)
                kind, i = OUTS[g]
                if 2 <= g < 9:
                    state(g - 2)
                if kind == "up_val":
                    pool.wait_ge(*post_act.at(g, "hi"))
                    pool.tensor_tensor(FL[:, i, :], fv[:], FH[:, i, :].bitcast(F32), ALU.subtract).then_inc(*post_pool.did(g, "lo"))

            def gdn(c, p, ph):
                n, t0 = tile_len(c), tile_at(c)
                g2 = slice(4 * c + 2 * p, 4 * c + 2 * p + 2)
                own = gdn_pool[p]

                def T(i):
                    return Tp(i, p)[0:n, :, 0:n]

                def blocks(l):
                    pool.tensor_tensor(T(1), T(10), over(lev[0:n, l, 0:n], 2), ALU.mult).then_inc(*own.did(c, f"B{l}"))

                if ph == "diag":
                    if c:
                        pool.wait_ge(*gdn_pe[p].at(c - 1, "gb"))
                    else:
                        pool.wait_ge(*gate_dve.at(0, "gc"))
                        pool.wait_ge(*gate_act.at(0, "beta"))
                        pool.wait_ge(*l2_pe.at(7, "ss"))
                    for x, (r, name) in enumerate(((2, "dg"), (0, "db"))):
                        pool.tensor_tensor(half_of(SQ[:, p, :], x)[0:n, :, 0:n], over(ident[0:n, 0:n], 2), cols(gv[0:n, r, g2], n),
                                           ALU.mult).then_inc(*own.did(c, name))
                elif ph == "mask":
                    pool.wait_ge(*gdn_act[p].at(c, "PT"))
                    pool.tensor_tensor(T(0), T(0), over(upto_m[0:n, 0:n], 2), ALU.mult).then_inc(*own.did(c, "PTm"))
                    pool.wait_ge(*own.at(c, "PTm"))
                    pool.tensor_tensor(T(1), T(0), T(8), ALU.mult).then_inc(*own.did(c, "bPT"))
                elif ph == "turn":
                    pool.wait_ge(*gdn_dve[p].at(c, "QKT"))
                    blocks(1)
                    pool.wait_ge(*gdn_act[p].at(c, "egb"))
                    qd = Tp(9, p)[:, :, 0:n]
                    pool.tensor_tensor(qd, qkvT[:, 2 * p:2 * p + 2, t0:t0 + n], qd, ALU.mult).then_inc(*own.did(c, "qd"))
                elif ph[0] == "X" and int(ph[1:]) < levels_of(c) - 1:
                    l = int(ph[1:])
                    pool.wait_ge(*gdn_pe[p].at(c, f"T{l}"))
                    blocks(l + 1)

            def hg(c, ph):
                n, t0 = tile_len(c), tile_at(c)
                D_ = lambda name: hg_pool.did(c, name)
                if ph == "v":
                    if c:
                        pool.wait_ge(*hg_pe.at(c - 1, "S"))
                    else:
                        pool.wait_ge(*hgp_dve.at(1, f"b1_{TILES - 1}"))
                    pool.tensor_scalar(hK[:, :, 0:n], ckT[:, :, t0:t0 + n], 1.0, 1.0, ALU.mult, ALU.mult).then_inc(*D_("k0"))
                elif ph[0] == "b":
                    l = int(ph[1:])
                    s = 1 << (l - 1)

                    def first(ap):
                        return ap.rearrange("p i (b h r) -> p i b h r", h=2, r=s)[:, :, :, 0, :]

                    pool.wait_ge(*hg_act.at(c, f"E{l}"))
                    pool.wait_ge(*hg_pe.at(c, f"A{l - 1}"))
                    pool.tensor_tensor(first(hK[:, :, 0:n]), first(ckT[:, :, t0:t0 + n]), first(hE[:, :, 0:n]), ALU.mult).then_inc(*D_(f"k{l}"))
                elif ph == "kd":
                    pool.wait_ge(*hg_act.at(c, "ek1"))
                    pool.wait_ge(*hg_pe.at(c, f"A{levels_of(c)}"))
                    pool.tensor_tensor(hK[:, :, 0:n], ckT[:, :, t0:t0 + n], hE[:, :, 0:n], ALU.mult).then_inc(*D_("kd"))
                elif ph == "kdt":
                    pool.wait_ge(*hg_act.at(c, "eq"))
                    pool.tensor_tensor(hE[:, :, 0:n], cqT[:, :, t0:t0 + n], hE[:, :, 0:n], ALU.mult).then_inc(*D_("qe"))

            def mix_out():
                pool.wait_ge(*mo_dve.at(OUT_ORDER[-1], "lo"))
                for p in range(2):
                    pool.wait_ge(*gdn_dve[p].at(TILES - 1, "S"))
                pool.wait_ge(*hg_dve.at(TILES - 1, "on"))
                pool.dma_start(nat[:], mem_prompt[0].rearrange("(c p) d -> p c d", p=P)).then_inc(mem_loaded, 16)
                pool.dma_start(sV[:], cache_mem_v[0, 0].rearrange("(c p) h d -> p c (h d)", p=P)).then_inc(cv_loaded, 16)

            handlers = {"start": start, "post": post, "gdn": gdn, "hg": hg, "mix_out": mix_out}
            for what, *args in SCHED:
                if what in handlers:
                    handlers[what](*args)


_INS = ['x_prompt', 'x_sample', 'cache_mem_k', 'cache_mem_v', 'state_a_conv', 'state_a_S', 'state_b_conv', 'state_b_h',
        'state_c_S', 'state_ffn_conv', 'mem_prompt', 'norm_mix', 'w_in', 'a_conv_w', 'a_A_log', 'a_dt_bias', 'a_norm',
        'b_conv_w', 'b_conv_b', 'b_w_r', 'b_b_r', 'b_w_i', 'b_b_i', 'b_lambda', 'c_lb_logits', 'c_norm', 'w_out',
        'norm_attn', 'norm_mem', 'w_q', 'w_k', 'w_v', 'w_o', 'norm_ffn', 'w_up', 'ffn_conv_w', 'ffn_conv_b', 'w_down',
        'norm_final']
_STATES = [(1, 1, 3, 1536), (1, 1, 4, 128, 128), (1, 1, 3, 256), (1, 1, 256), (1, 1, 4, 64, 64), (1, 1, 2, 5632)]
_OUTS = [(1, 512, 1024), (1, 64, 1024), (1, 1, 256, 4, 256), (1, 1, 256, 4, 256)] + _STATES + _STATES


def kernel(**inputs):
    import numpy as _np
    import concourse.bacc as _bacc
    from concourse import mybir as _mybir
    from concourse.bass_utils import run_bass_kernel_spmd as _run

    nc = _bacc.Bacc("TRN2", target_bir_lowering=False, num_devices=1)
    arrays, args = {}, []
    for name in _INS:
        a = _np.ascontiguousarray(inputs[name])
        arrays[f"in_{name}_dram"] = a
        args.append(nc.dram_tensor(f"in_{name}_dram", a.shape, _mybir.dt.from_np(a.dtype), kind="ExternalInput").ap())
    for i, shape in enumerate(_OUTS):
        args.append(nc.dram_tensor(f"out_{i}_dram", shape, _mybir.dt.float32, kind="ExternalOutput").ap())
    build(nc, *args)
    r = _run(nc, [arrays], core_ids=[0])
    return tuple(r.results[0][f"out_{i}_dram"] for i in range(len(_OUTS)))
```
